# Optimizing a Trainium2 kernel written in Bass

```python
import math
import jax
import jax.numpy as jnp
from jax import lax
import numpy as np

D_MODEL = 1024
BATCH = 1
SEQ = 256
DEPTH = 4

GRID_W = 64
CTX_LEN = 256
N_MIXERS = 3
N_CONV_LAYERS = (DEPTH + 2) // 3
N_SSM_LAYERS = (DEPTH + 1) // 3
N_ATTN_LAYERS = DEPTH // 3

DEEPNORM_ALPHA = (2 * DEPTH) ** 0.25
DEEPNORM_BETA = (8 * DEPTH) ** -0.25
LN_EPS = 1e-5
RMS_EPS = 1e-6

CONV_WIDTH = 31

SSM_D_INNER = 2 * D_MODEL
SSM_HEAD_DIM = 64
SSM_HEADS = SSM_D_INNER // SSM_HEAD_DIM
SSM_GROUPS = 8
SSM_HPG = SSM_HEADS // SSM_GROUPS
SSM_STATE = 128
SSM_CONV_WIDTH = 5
SSM_CHUNK = 128
SSM_BC = SSM_GROUPS * SSM_STATE
SSM_XBC = SSM_D_INNER + 2 * SSM_BC
SSM_IN = SSM_D_INNER + SSM_XBC + 2 * SSM_HEADS

ATTN_HEAD_DIM = 64
ATTN_HEADS = D_MODEL // ATTN_HEAD_DIM
ATTN_KV_HEADS = 4
ATTN_Q_PER_KV = ATTN_HEADS // ATTN_KV_HEADS
ATTN_QKV = (ATTN_HEADS + 2 * ATTN_KV_HEADS) * ATTN_HEAD_DIM
ATTN_BLOCK = 128
ROPE_THETA = 10000.0

FFN_HIDDEN = -(-8 * D_MODEL // (3 * 256)) * 256

F32 = jnp.float32

kernel_name = "hybrid_conv_ssd_gqa_diffusion_trunk"

def layer_norm(x, g, b):
    xf = x.astype(F32)
    mu = jnp.mean(xf, axis=-1, keepdims=True)
    var = jnp.mean(jnp.square(xf - mu), axis=-1, keepdims=True)
    return ((xf - mu) * lax.rsqrt(var + LN_EPS) * g + b).astype(x.dtype)

def rms_norm(x, g):
    xf = x.astype(F32)
    y = xf * lax.rsqrt(jnp.mean(xf * xf, axis=-1, keepdims=True) + RMS_EPS) * g
    return y.astype(x.dtype)

def ada_modulation(cond, w, b):
    m = jax.nn.silu(cond) @ w + b
    if m.ndim == 2:
        m = m[:, None, :]
    return jnp.split(m, 6, axis=-1)

def modulate(h, shift, scale):
    return h * (1.0 + scale) + shift

def post_norm_residual(h, y, gate, g, b):
    return layer_norm(DEEPNORM_ALPHA * h + gate * y, g, b)

def depthwise_conv(x, w, b):
    k = w.shape[0]
    y = lax.conv_general_dilated(
        x, w[:, None, :], window_strides=(1,), padding=[((k - 1) // 2, k // 2)],
        dimension_numbers=("NWC", "WIO", "NWC"), feature_group_count=x.shape[-1])
    return y + b

def swiglu(h, w1, w3, w2):
    return (jax.nn.silu(h @ w1) * (h @ w3)) @ w2

def conformer_conv(u, pw1_w, pw1_b, dw_w, dw_b, n_g, n_b, pw2_w, pw2_b):
    a, g = jnp.split(u @ pw1_w + pw1_b, 2, axis=-1)
    v = a * jax.nn.sigmoid(g)
    v = depthwise_conv(v, dw_w, dw_b)
    v = jax.nn.silu(layer_norm(v, n_g, n_b))
    return v @ pw2_w + pw2_b

def conv_mixer(u_ctx, u_lat, pw1_w, pw1_b, dw_w, dw_b, n_g, n_b, pw2_w, pw2_b, ctx_out):
    y_lat = conformer_conv(u_lat, pw1_w, pw1_b, dw_w, dw_b, n_g, n_b, pw2_w, pw2_b)
    y_ctx = conformer_conv(u_ctx, pw1_w, pw1_b, dw_w, dw_b, n_g, n_b, pw2_w, pw2_b) if ctx_out else None
    return y_ctx, y_lat

def ssd_chunk_scan(x, dt, a_log, bm, cm, h0):
    b, l = x.shape[:2]
    nc = l // SSM_CHUNK

    def chunks(t):
        t = t.astype(F32).reshape((b, nc, SSM_CHUNK) + t.shape[2:])
        return jnp.moveaxis(t, 1, 0)

    a = -jnp.exp(a_log.astype(F32))
    tri = jnp.tril(jnp.ones((SSM_CHUNK, SSM_CHUNK), dtype=bool))[None, :, :, None, None]

    def step(h, inp):
        xc, dtc, bc, cc = inp
        cum = jnp.cumsum(dtc * a, axis=1)
        seg = jnp.exp(jnp.where(tri, cum[:, :, None] - cum[:, None, :], -jnp.inf))
        cb = jnp.einsum("bign,bjgn->bijg", cc, bc)
        y = jnp.einsum("bijgr,bjgrp->bigrp", cb[..., None] * seg, dtc[..., None] * xc)
        y = y + jnp.einsum("bign,bgrpn->bigrp", cc, h) * jnp.exp(cum)[..., None]
        w_end = (jnp.exp(cum[:, -1:] - cum) * dtc)[..., None] * xc
        h = h * jnp.exp(cum[:, -1])[..., None, None] + jnp.einsum("bjgn,bjgrp->bgrpn", bc, w_end)
        return h, y

    h, ys = lax.scan(step, h0.astype(F32), (chunks(x), chunks(dt), chunks(bm), chunks(cm)))
    return jnp.moveaxis(ys, 0, 1).reshape(x.shape), h

def ssm_mixer(u_ctx, u_lat, in_w, conv_w, conv_b, a_log, dt_bias, d_skip, norm_g, out_w, ctx_out):
    a_log = a_log.reshape(2, SSM_GROUPS, SSM_HPG)
    dt_bias = dt_bias.reshape(2, SSM_GROUPS, SSM_HPG)
    d_skip = d_skip.reshape(SSM_GROUPS, SSM_HPG)

    def project(u):
        b, l = u.shape[:2]
        z, xbc, dt = jnp.split(u @ in_w, [SSM_D_INNER, SSM_D_INNER + SSM_XBC], axis=-1)
        xbc = jax.nn.silu(depthwise_conv(xbc, conv_w, conv_b))
        xs, bm, cm = jnp.split(xbc, [SSM_D_INNER, SSM_D_INNER + SSM_BC], axis=-1)
        xs = xs.reshape(b, l, SSM_GROUPS, SSM_HPG, SSM_HEAD_DIM)
        bm = bm.reshape(b, l, SSM_GROUPS, SSM_STATE)
        cm = cm.reshape(b, l, SSM_GROUPS, SSM_STATE)
        dt = jax.nn.softplus(dt.astype(F32).reshape(b, l, 2, SSM_GROUPS, SSM_HPG) + dt_bias)
        return z, xs, bm, cm, dt

    def rev(t):
        return jnp.flip(t, axis=1)

    def bidir(xs, bm, cm, dt, h0_f, h0_b):
        y_f, h_f = ssd_chunk_scan(xs, dt[:, :, 0], a_log[0], bm, cm, h0_f)
        y_b, h_b = ssd_chunk_scan(rev(xs), rev(dt[:, :, 1]), a_log[1], rev(bm), rev(cm), h0_b)
        return y_f + rev(y_b), h_f, h_b

    def finish(y, xs, z):
        y = (y + d_skip[..., None] * xs.astype(F32)).reshape(z.shape)
        g = y * jax.nn.silu(z.astype(F32))
        g = g.reshape(z.shape[:-1] + (SSM_GROUPS, -1))
        g = g * lax.rsqrt(jnp.mean(g * g, axis=-1, keepdims=True) + RMS_EPS)
        g = g.reshape(z.shape) * norm_g
        return g.astype(z.dtype) @ out_w

    zc, xc, bc, cc, dtc = project(u_ctx)
    h0 = jnp.zeros((u_ctx.shape[0], SSM_GROUPS, SSM_HPG, SSM_HEAD_DIM, SSM_STATE), F32)
    yc, hc_f, hc_b = bidir(xc, bc, cc, dtc, h0, h0)
    zl, xl, bl, cl, dtl = project(u_lat)
    yl, _, _ = bidir(xl, bl, cl, dtl, hc_f, hc_b)
    y_lat = finish(yl, xl, zl)
    y_ctx = finish(yc, xc, zc) if ctx_out else None
    return y_ctx, y_lat

def axial_rope(n_tok):
    rows = n_tok // GRID_W
    row = jnp.repeat(jnp.arange(rows, dtype=F32), GRID_W)
    col = jnp.tile(jnp.arange(GRID_W, dtype=F32), rows)
    axis_dim = ATTN_HEAD_DIM // 2
    inv_freq = ROPE_THETA ** (-jnp.arange(0, axis_dim, 2, dtype=F32) / axis_dim)
    ang = jnp.concatenate([row[:, None] * inv_freq, col[:, None] * inv_freq], axis=-1)
    return jnp.cos(ang), jnp.sin(ang)

def apply_rope(x, cos, sin):
    xf = x.astype(F32).reshape(x.shape[:-1] + (-1, 2))
    x1, x2 = xf[..., 0], xf[..., 1]
    c, s = cos[None, :, None, :], sin[None, :, None, :]
    return jnp.stack([x1 * c - x2 * s, x1 * s + x2 * c], axis=-1).reshape(x.shape).astype(x.dtype)

def gqa_attend(q, k, v):
    b, lq = q.shape[:2]
    qg = q.reshape(b, lq, ATTN_KV_HEADS, ATTN_Q_PER_KV, ATTN_HEAD_DIM)
    s = jnp.einsum("bqkrd,bskd->bkrqs", qg, k).astype(F32) * (ATTN_HEAD_DIM ** -0.5)
    p = jax.nn.softmax(s, axis=-1)
    o = jnp.einsum("bkrqs,bskd->bqkrd", p.astype(v.dtype), v)
    return o.reshape(b, lq, ATTN_HEADS * ATTN_HEAD_DIM)

def blocked_attend(q, k, v):
    b, l = q.shape[:2]
    nb = l // ATTN_BLOCK
    qb = jnp.moveaxis(q.reshape(b, nb, ATTN_BLOCK, ATTN_HEADS, ATTN_HEAD_DIM), 1, 0)
    ob = lax.map(lambda qi: gqa_attend(qi, k, v), qb)
    return jnp.moveaxis(ob, 0, 1).reshape(b, l, ATTN_HEADS * ATTN_HEAD_DIM)

def attn_mixer(u_ctx, u_lat, qkv_w, q_g, k_g, out_w, ctx_out):
    def qkv(u):
        b, l = u.shape[:2]
        q, k, v = jnp.split(u @ qkv_w, [ATTN_HEADS * ATTN_HEAD_DIM,
                                        (ATTN_HEADS + ATTN_KV_HEADS) * ATTN_HEAD_DIM], axis=-1)
        q = rms_norm(q.reshape(b, l, ATTN_HEADS, ATTN_HEAD_DIM), q_g)
        k = rms_norm(k.reshape(b, l, ATTN_KV_HEADS, ATTN_HEAD_DIM), k_g)
        return q, k, v.reshape(b, l, ATTN_KV_HEADS, ATTN_HEAD_DIM)

    qc, kc, vc = qkv(u_ctx)
    ql, kl, vl = qkv(u_lat)
    cos, sin = axial_rope(u_lat.shape[1])
    ql, kl = apply_rope(ql, cos, sin), apply_rope(kl, cos, sin)
    k_all = jnp.concatenate([kc, kl], axis=1)
    v_all = jnp.concatenate([vc, vl], axis=1)
    y_lat = blocked_attend(ql, k_all, v_all) @ out_w
    y_ctx = gqa_attend(qc, kc, vc) @ out_w if ctx_out else None
    return y_ctx, y_lat

def setup_inputs(seed: int = 0) -> dict:
    key = jax.random.key(seed)
    keys = iter(jax.random.split(key, 40))

    def nrm(shape, scale):
        return jax.random.normal(next(keys), shape, F32) * scale

    def gain(shape):
        return 1.0 + nrm(shape, 0.02)

    D, L = D_MODEL, DEPTH
    nc, ns, na = N_CONV_LAYERS, N_SSM_LAYERS, N_ATTN_LAYERS
    beta = DEEPNORM_BETA
    dt0 = jnp.exp(jax.random.uniform(next(keys), (ns, 2 * SSM_HEADS), F32,
                                     math.log(1e-3), math.log(1e-1)))
    return {
        "x": nrm((BATCH, SEQ, D), 1.0),
        "c": nrm((BATCH, D), 1.0),
        "ctx": nrm((BATCH, CTX_LEN, D), 1.0),
        "c_ctx": nrm((D,), 1.0),
        "ada_w": nrm((L, D, 6 * D), 0.5 * D ** -0.5),
        "ada_b": nrm((L, 6 * D), 0.02),
        "ln_mix_g": gain((L, D)),
        "ln_mix_b": nrm((L, D), 0.02),
        "ln_ffn_g": gain((L, D)),
        "ln_ffn_b": nrm((L, D), 0.02),
        "ffn_w1": nrm((L, D, FFN_HIDDEN), D ** -0.5),
        "ffn_w3": nrm((L, D, FFN_HIDDEN), D ** -0.5),
        "ffn_w2": nrm((L, FFN_HIDDEN, D), beta * FFN_HIDDEN ** -0.5),
        "conv_pw1_w": nrm((nc, D, 2 * D), D ** -0.5),
        "conv_pw1_b": nrm((nc, 2 * D), 0.02),
        "conv_dw_w": nrm((nc, CONV_WIDTH, D), CONV_WIDTH ** -0.5),
        "conv_dw_b": nrm((nc, D), 0.02),
        "conv_norm_g": gain((nc, D)),
        "conv_norm_b": nrm((nc, D), 0.02),
        "conv_pw2_w": nrm((nc, D, D), beta * D ** -0.5),
        "conv_pw2_b": nrm((nc, D), 0.02),
        "ssm_in_w": nrm((ns, D, SSM_IN), D ** -0.5),
        "ssm_conv_w": nrm((ns, SSM_CONV_WIDTH, SSM_XBC), SSM_CONV_WIDTH ** -0.5),
        "ssm_conv_b": nrm((ns, SSM_XBC), 0.02),
        "ssm_a_log": jnp.log(jax.random.uniform(next(keys), (ns, 2 * SSM_HEADS), F32, 1.0, 16.0)),
        "ssm_dt_bias": dt0 + jnp.log(-jnp.expm1(-dt0)),
        "ssm_d": 1.0 + nrm((ns, SSM_HEADS), 0.1),
        "ssm_norm_g": gain((ns, SSM_D_INNER)),
        "ssm_out_w": nrm((ns, SSM_D_INNER, D), beta * SSM_D_INNER ** -0.5),
        "attn_qkv_w": nrm((na, D, ATTN_QKV), D ** -0.5),
        "attn_q_norm": gain((na, ATTN_HEAD_DIM)),
        "attn_k_norm": gain((na, ATTN_HEAD_DIM)),
        "attn_out_w": nrm((na, D, D), beta * D ** -0.5),
    }

def reference(x, c, ctx, c_ctx, ada_w, ada_b, ln_mix_g, ln_mix_b, ln_ffn_g, ln_ffn_b,
              ffn_w1, ffn_w3, ffn_w2,
              conv_pw1_w, conv_pw1_b, conv_dw_w, conv_dw_b, conv_norm_g, conv_norm_b,
              conv_pw2_w, conv_pw2_b,
              ssm_in_w, ssm_conv_w, ssm_conv_b, ssm_a_log, ssm_dt_bias, ssm_d, ssm_norm_g, ssm_out_w,
              attn_qkv_w, attn_q_norm, attn_k_norm, attn_out_w):
    h_lat, h_ctx = x, ctx
    for i in range(DEPTH):
        last = i == DEPTH - 1
        kind, j = i % N_MIXERS, i // N_MIXERS
        ctx_in = (not last) or kind != 0
        m_lat = ada_modulation(c, ada_w[i], ada_b[i])
        u_lat = modulate(h_lat, m_lat[0], m_lat[1])
        if ctx_in:
            m_ctx = ada_modulation(c_ctx, ada_w[i], ada_b[i])
            u_ctx = modulate(h_ctx, m_ctx[0], m_ctx[1])
        else:
            u_ctx = None
        if kind == 0:
            y_ctx, y_lat = conv_mixer(u_ctx, u_lat, conv_pw1_w[j], conv_pw1_b[j], conv_dw_w[j],
                                      conv_dw_b[j], conv_norm_g[j], conv_norm_b[j],
                                      conv_pw2_w[j], conv_pw2_b[j], not last)
        elif kind == 1:
            y_ctx, y_lat = ssm_mixer(u_ctx, u_lat, ssm_in_w[j], ssm_conv_w[j], ssm_conv_b[j],
                                     ssm_a_log[j], ssm_dt_bias[j], ssm_d[j], ssm_norm_g[j],
                                     ssm_out_w[j], not last)
        else:
            y_ctx, y_lat = attn_mixer(u_ctx, u_lat, attn_qkv_w[j], attn_q_norm[j], attn_k_norm[j],
                                      attn_out_w[j], not last)
        h_lat = post_norm_residual(h_lat, y_lat, m_lat[2], ln_mix_g[i], ln_mix_b[i])
        f_lat = swiglu(modulate(h_lat, m_lat[3], m_lat[4]), ffn_w1[i], ffn_w3[i], ffn_w2[i])
        h_lat = post_norm_residual(h_lat, f_lat, m_lat[5], ln_ffn_g[i], ln_ffn_b[i])
        if not last:
            h_ctx = post_norm_residual(h_ctx, y_ctx, m_ctx[2], ln_mix_g[i], ln_mix_b[i])
            f_ctx = swiglu(modulate(h_ctx, m_ctx[3], m_ctx[4]), ffn_w1[i], ffn_w3[i], ffn_w2[i])
            h_ctx = post_norm_residual(h_ctx, f_ctx, m_ctx[5], ln_ffn_g[i], ln_ffn_b[i])
    return h_lat


_drawn_inputs = setup_inputs


def setup_inputs(seed=0):
    import zlib

    import numpy as np

    out = dict(_drawn_inputs(seed))
    spreads = {}
    factors = {'ctx': 8.0,
     'c_ctx': 4.572,
     'ada_b': 4.936,
     'conv_pw1_b': 8.0,
     'conv_dw_b': 8.0,
     'conv_norm_g': 8.0,
     'conv_norm_b': 8.0,
     'conv_pw2_b': 8.0,
     'ssm_conv_b': 8.0,
     'ssm_a_log': 3.61,
     'ssm_d': 8.0,
     'ssm_norm_g': 8.0,
     'attn_qkv_w': 3.093,
     'attn_q_norm': 8.0,
     'attn_k_norm': 8.0,
     'attn_out_w': 2.98}
    for name, (base, spread) in spreads.items():
        noise = np.random.default_rng([zlib.crc32(name.encode()), seed]).standard_normal(out[name].shape)
        drawn = base * np.exp(spread * noise) if base else spread * noise
        out[name] = jnp.asarray(drawn.astype(out[name].dtype))
    for name, factor in factors.items():
        out[name] = (out[name] * factor).astype(out[name].dtype)
    return out
```

```python
from contextlib import ExitStack

import numpy as np
import concourse.bass as bass
from concourse import mybir

F32 = mybir.dt.float32
F32R = mybir.dt.float32r
ALU = mybir.AluOpType
ACT = mybir.ActivationFunctionType

P = 128
D = 1024
KT = D // P
SEG = 256
N = 2 * SEG
DEPTH = 4
MIX, FFN = 0, 1
ALPHA = (2 * DEPTH) ** 0.25
LN_EPS, RMS_EPS = 1e-5, 1e-6

TAPS = 31
PAD = (TAPS - 1) // 2
VW = SEG + 2 * PAD

FH = -(-8 * D // (3 * 256)) * 256
HT = FH // P
FG = HT // 2

DI = 2 * D
GROUPS = 8
HPG = 4
HD = 64
CW = 5
XW = SEG + CW - 1
CH = 128
NC = N // CH
CONV_LAYERS, SSM_LAYER, ATTN_LAYER = (0, 3), 1, 2

UNIT = 8 * P
CHUNKS = 6 * D // N

MIXER_UNITS = {0: 24, 1: 65, 2: 20, 3: 24}
FFN_UNITS = 4 * FG + 2 * FG


def mix_base(L):
    return sum(MIXER_UNITS[i] + FFN_UNITS for i in range(L))


def ffn_base(L):
    return mix_base(L) + MIXER_UNITS[L]


UNITS = ffn_base(DEPTH - 1) + FFN_UNITS

NORMS = [("conv", 0), (MIX, 0), (FFN, 0), (MIX, 1), (FFN, 1), (MIX, 2), (FFN, 2), ("conv", 3), (MIX, 3), (FFN, 3)]
OPERANDS = [((MIX, 0), 8), (("conv", 0), 8), ((FFN, 0), 8), ((MIX, 1), 8), (("ssm", 1), 16), ((FFN, 1), 8), ((MIX, 2), 8),
            (("attn", 2), 8), ((FFN, 2), 8), ((MIX, 3), 8), (("conv", 3), 8), ((FFN, 3), 8)]
X_BASE = {key: sum(n for _, n in OPERANDS[:i]) for i, (key, _) in enumerate(OPERANDS)}


def params():
    at, out = 0, {}
    for name, width in (
        [(f"ln_{w}_{s}{L}", KT) for L in range(DEPTH) for w in ("mix", "ffn") for s in "gb"]
        + [(f"{name}{j}", width) for j in range(2) for name, width in
           (("pw1_b", 2 * KT), ("dw", KT * (TAPS + 1)), ("cn_g", KT), ("cn_b", KT), ("pw2_b", KT))]
        + [("ada_b", DEPTH * 96), ("sconv", 32 * (CW + 1)), ("snorm", 16), ("sskip", 16), ("dt_b", 1), ("a_log", 1),
           ("qk_g", 10), ("eps_ln", 1), ("eps_rms", 1), ("one", 1)]
    ):
        out[name] = (at, width)
        at += width
    return out, at


PAR, NPAR = params()
CST = {"ident": 0, "mask_f": 128, "mask_b": 256, "rot": 384, "headmean": 512, "cos": 640, "sin": 896, "sel": 1152}
NCST = 1154


def program(nc, xT, condT, par_d, cst_d, adaw, wstream, out_d, layers=DEPTH):
    root = ExitStack()
    with root:
        def sb(name, shape, dt=F32, scope=root):
            return scope.enter_context(nc.sbuf_tensor(name, shape, dt))

        def sem(name):
            return root.enter_context(nc.semaphore(name))

        h = sb("h", [P, KT, N])
        xh = sb("xh", [P, KT, N], F32R)
        xl = sb("xl", [P, KT, N], F32R)
        raw = sb("raw", [P, 4, UNIT])
        wh = sb("wh", [P, 2, UNIT], F32R)
        wl = sb("wl", [P, 2, UNIT], F32R)
        par = sb("par_sb", [P, NPAR])
        cst = sb("cst_sb", [P, NCST])
        condraw = sb("condraw", [P, KT, 2])
        cond = sb("cond", [P, KT, 32])
        mod = sb("mod", [P, 2, 96])
        gbias = sb("gbias", [P, KT, 2])
        meanm = sb("meanm", [P, P])
        tmp = sb("tmp", [P, 2, N])
        act_tmp = sb("act_tmp", [P, 2, N])
        rs = sb("rs", [P, N])
        adarow = rs
        credit = sb("credit", [P, 4])
        bank = [root.enter_context(nc.psum_tensor(f"bank{i}", [P, N], F32)) for i in range(8)]

        with ExitStack() as s:
            ada = sb("ada", [P, 2, 4, N], F32, s)
            hidh = sb("hidh", [P, HT * N], F32R, s)
            hidl = sb("hidl", [P, HT * N], F32R, s)
        with ExitStack() as s:
            vbuf = sb("vbuf", [P, 2, 2, VW], F32, s)
            dwc = sb("dwc", [P, 2, TAPS + 1], F32, s)
            cacc = sb("cacc", [P, 2, N], F32, s)
            cz = sb("cz", [P, KT * N], F32, s)

        with ExitStack() as s:
            yall = sb("yall", [P, 16 * N], F32, s)
            with ExitStack() as s2:
                xc = sb("xc", [P, 2, 4, N], F32, s2)
                zs = sb("zs", [P, 2, N], F32, s2)
                xraw = sb("xraw", [P, 4, 2, XW], F32, s2)
                xdt = sb("xdt", [P, 2, NC, HPG * HD], F32, s2)
                xw = sb("xw", [P, NC, HPG * HD], F32, s2)
                btok = sb("btok", [P, NC, P], F32, s2)
                cbm = sb("cbm", [P, 2, N], F32, s2)
                seg = sb("seg", [P, 3, N], F32, s2)
                hst = sb("hst", [P, 2, 3, HPG * HD], F32, s2)
                cum = sb("cum", [P, N], F32, s2)
                tokq = sb("tokq", [P, 4, NC, 64], F32, s2)
                tg = sb("tg", [P, 4 * NC, 2, HPG], F32, s2)
                pick = sb("pick", [P, 2 * HPG, P], F32, s2)
                sconv = sb("sconv_g", [P, 4, CW + 1], F32, s2)
            with ExitStack() as s2:
                x2h = sb("x2h", [P, KT, N], F32R, s2)
                x2l = sb("x2l", [P, KT, N], F32R, s2)
        with ExitStack() as s:
            qkv = sb("qkv", [P, 12 * N], F32, s)
            vtok = sb("vtok", [P, NC, 4 * HD], F32, s)
            qcur = sb("qcur", [P, N], F32, s)
            pT = sb("pT", [P, 2, N], F32, s)
            rsh = sb("rsh", [P, 2, N], F32, s)
            asm_ = sb("attn_small", [P, 4, 4], F32, s)

        raw_landed = [sem(f"raw_landed{i}") for i in range(4)]
        hi_ready = sem("hi_ready")
        split_ready = sem("split_ready")
        split_free = sem("split_free")
        par_landed = sem("par_landed")
        h_landed = sem("h_landed")
        ada_landed = [sem("ada_landed0"), sem("ada_landed1")]
        ada_used = sem("ada_used")

        ada_row = sem("ada_row")
        ada_col = sem("ada_col")
        mod_ready = sem("mod_ready")
        mod_done = sem("mod_done")
        cleared = sem("cleared")
        cond_ready = sem("cond_ready")
        x_ready = sem("x_ready")
        ah_ready = sem("ah_ready")
        y_done = sem("y_done")
        z_ready = sem("z_ready")
        mean_done = sem("mean_done")
        zc_ready = sem("zc_ready")
        sq_ready = sem("sq_ready")
        sq_used = sem("sq_used")
        rstd_ready = sem("rstd_ready")
        n_ready = sem("n_ready")
        h_ready = sem("h_ready")
        silu_ready = sem("silu_ready")
        pair_free = {L: sem(f"pair_free{L}") for L in range(layers)}
        pair_done = {L: sem(f"pair_done{L}") for L in range(layers)}
        gate_done = {L: sem(f"gate_done{L}") for L in range(layers)}
        hid_ready = {L: sem(f"hid_ready{L}") for L in range(layers)}
        cpair_free = {L: sem(f"cpair_free{L}") for L in CONV_LAYERS}
        cpair_done = {L: sem(f"cpair_done{L}") for L in CONV_LAYERS}
        cgate_done = {L: sem(f"cgate_done{L}") for L in CONV_LAYERS}
        out_landed = sem("out_landed")
        dt_read = sem("dt_read")
        dt_neg = sem("dt_neg")
        dt_log = sem("dt_log")
        a_ready = sem("a_ready")
        cum_ready = sem("cum_ready")
        w_ready = sem("w_ready")
        rows_ready = sem("rows_ready")
        toks_done = sem("toks_done")
        tot_ready = sem("tot_ready")
        proj_read = sem("proj_read")
        conv_done = sem("conv_done")
        xc_ready = sem("xc_ready")
        bt_done = sem("bt_done")
        xt_done = sem("xt_done")
        cb_done = sem("cb_done")
        cb_read = sem("cb_read")
        xw_ready = sem("xw_ready")
        st_done = sem("st_done")
        st_read = sem("st_read")
        pick_ready = sem("pick_ready")
        r_done = sem("r_done")
        seg_ready = sem("seg_ready")
        seg_exp = sem("seg_exp")
        e_ready = sem("e_ready")
        m_ready = sem("m_ready")
        ce_ready = sem("ce_ready")
        yh_done = sem("yh_done")
        yg_ready = sem("yg_ready")
        gsq_ready = sem("gsq_ready")
        gsq_used = sem("gsq_used")
        grs_ready = sem("grs_ready")
        grs_used = sem("grs_used")
        qkv_free = sem("qkv_free")
        qkv_done = sem("qkv_done")
        vt_done = sem("vt_done")
        vt_read = sem("vt_read")
        hsq_ready = sem("hsq_ready")
        hms_done = sem("hms_done")
        hrs_ready = sem("hrs_ready")
        hn_ready = sem("hn_ready")
        rot_done = sem("rot_done")
        rope_done = sem("rope_done")
        q_ready = sem("q_ready")
        sc_done = sem("sc_done")
        mx_ready = sem("mx_ready")
        ex_ready = sem("ex_ready")
        pr_ready = sem("pr_ready")
        ptr_done = sem("ptr_done")
        pt_ready = sem("pt_ready")
        pv_done = sem("pv_done")

        STATES = ((6, 0), (6, 1), (7, 0), (3, 0), (3, 1), (7, 1))

        def unit_done(n):
            return 2 + n + 1

        def segs(L):
            return (1,) if L == DEPTH - 1 else (0, 1)

        def tok(L):
            return slice(SEG if L == DEPTH - 1 else 0, N)

        def first(L):
            return SEG if L == DEPTH - 1 else 0

        def col(name, k, width=1):
            at = PAR[name][0]
            return par[:, at + k:at + k + width]

        def modc(L, m, k, c):
            at = (m * KT + k) * 2 + c
            return mod[:, L % 2, at:at + 1]

        def half(a):
            return a.rearrange("p (s t) -> p s t", s=2)

        def lname(which):
            return ("mix", "ffn")[which]

        used = sum(mix_base(1) if L == 0 else MIXER_UNITS[L] + FFN_UNITS for L in range(layers))
        block = root.enter_context(nc.Block())

        @block.sync
        def _(sp):
            sp.dma_start(par[:, :], par_d).then_inc(par_landed, 16)
            sp.dma_start(condraw[:, :, :], condT).then_inc(par_landed, 16)
            sp.dma_start(cst[:, :], cst_d).then_inc(par_landed, 16)
            sp.dma_start(h[:, :, :], xT).then_inc(h_landed, 16)

            def load(n, slot, split=None):
                if split is not None:
                    sp.wait_ge(split_ready, split)
                sp.dma_start(raw[:, slot, :], wstream[n, :, :]).then_inc(raw_landed[slot], 16)

            for slot in range(4):
                load(slot, slot)
            whole = used - used % 4
            with sp.Fori(1, whole // 4) as i:
                for slot in range(4):
                    load(i * 4 + slot, slot, i * 4 + (slot - 3))
            for n in range(whole, used):
                load(n, n % 4, n - 3)
            for k in range(KT):
                sp.wait_ge(h_ready, KT * (2 * layers - 1) + k + 1)
                if layers == DEPTH:
                    sp.dma_start(out_d[:, k, :], h[:, k, SEG:N]).then_inc(out_landed, 16)
                else:
                    sp.dma_start(out_d[:, k, :], h[:, k, :]).then_inc(out_landed, 16)
            sp.wait_ge(out_landed, 16 * KT)

        @block.gpsimd
        def _(pool):
            pool.memset(credit[:, 0:1], 0.0).then_inc(split_free, 2)

            def low_part(n, slot):
                pool.wait_ge(hi_ready, n + 1)
                pool.tensor_tensor(wl[:, slot % 2, :], raw[:, slot, :], wh[:, slot % 2, :].bitcast(F32),
                                   ALU.subtract).then_inc(split_ready, 1)

            whole = used - used % 4
            with pool.Fori(0, whole // 4) as i:
                for slot in range(4):
                    low_part(i * 4 + slot, slot)
            for n in range(whole, used):
                low_part(n, n % 4)

        @block.scalar
        def _(act):
            def load_ada(c, slot, used_before):
                if used_before is not None:
                    act.wait_ge(ada_used, used_before)
                act.dma_start(ada[:, slot, :, :], adaw[c, :, slot * 4:slot * 4 + 4, :]).then_inc(ada_landed[slot], 16)

            def high_part(base, g=0, stride=4):
                slot, ring = base % 4, base % 2
                n = g * stride + base
                act.wait_ge(raw_landed[slot], g * (4 * stride) + 16 * (base // 4 + 1))
                act.wait_ge(split_free, n + 1)
                act.activation(wh[:, ring, :], raw[:, slot, :], ACT.Copy).then_inc(hi_ready, 1)

            def high_parts(a, b):
                b = min(b, used)
                if b - a >= 8:
                    with act.Fori(0, (b - a) // 4) as i:
                        for c in range(4):
                            high_part(a + c, i)
                    a += (b - a) // 4 * 4
                for n in range(a, b):
                    high_part(n)

            def residual(L, which):
                biased = which == MIX and L in CONV_LAYERS
                for k in range(KT):
                    act.wait_ge(x_ready, X_BASE[which, L] + k + 1)
                    for c in segs(L):
                        t = slice(c * SEG, (c + 1) * SEG)
                        if biased:
                            ins = act.activation(h[:, k, t], h[:, k, t], ACT.Identity, scale=ALPHA,
                                                 bias=gbias[:, k, c:c + 1])
                        else:
                            ins = act.activation(h[:, k, t], h[:, k, t], ACT.Copy, scale=ALPHA)
                    ins.then_inc(ah_ready, 1)

            def norm_scale(kind, L, src):
                li = NORMS.index((kind, L))
                act.preload_act_table_set("natural_log_exp_and_others")
                for m in range(KT):
                    act.wait_ge(zc_ready, KT * li + m + 1)
                    if m >= 2:
                        act.wait_ge(sq_used, KT * li + m - 1)
                    act.activation(act_tmp[:, m % 2, tok(L)], src(m), ACT.Square).then_inc(sq_ready, 1)
                act.wait_ge(sq_used, KT * li + KT)
                act.activation(rs[:, tok(L)], bank[1][:, tok(L)], ACT.Ln, bias=col("eps_ln", 0))
                act.drain()
                act.activation(rs[:, tok(L)], rs[:, tok(L)], ACT.Exp, scale=-0.5).then_inc(rstd_ready, 1)

            def norm_bias(kind, L):
                li = NORMS.index((kind, L))
                for m in range(KT):
                    act.wait_ge(n_ready, KT * li + m + 1)
                    act.activation(h[:, m, tok(L)], h[:, m, tok(L)], ACT.Identity,
                                   bias=col(f"ln_{lname(kind)}_b{L}", m)).then_inc(h_ready, 1)

            def conv_mixer(L):
                j = CONV_LAYERS.index(L)
                act.preload_act_table_set("sigmoid_and_others")
                with act.Fori(0, 4) as g:
                    for c in range(3):
                        high_part(mix_base(L) + 2 + c, g)
                    for p in range(2):
                        if p == 0:
                            act.wait_ge(cpair_done[L], g + 1)
                        else:
                            act.wait_ge(split_free, unit_done(mix_base(L) + g * 4 + 3))
                        act.wait_ge(cpair_free[L], g * 2 + p + 1)
                        act.activation(act_tmp[:, p, tok(L)], bank[2 * p + 1][:, tok(L)], ACT.Sigmoid,
                                       bias=par[:, bass.ds(g * 2 + (PAR[f"pw1_b{j}"][0] + KT + p), 1)]
                                       ).then_inc(cgate_done[L], 1)
                    high_part(mix_base(L) + 5, g)
                norm_scale("conv", L, lambda m: cz[:, m * N + first(L):(m + 1) * N])
                act.preload_act_table_set("silu_and_others")
                for m in range(KT):
                    act.wait_ge(n_ready, KT * NORMS.index(("conv", L)) + m + 1)
                    z = cz[:, m * N + first(L):(m + 1) * N]
                    act.activation(z, z, ACT.Silu, bias=col(f"cn_b{j}", m)).then_inc(silu_ready, 1)
                high_parts(mix_base(L) + 18, mix_base(L) + 26)

            def ffn(L):
                act.preload_act_table_set("silu_and_others")
                if L + 1 < layers:
                    c0 = CHUNKS * (L + 1)
                    act.wait_ge(x_ready, X_BASE[FFN, L] + 1)
                    load_ada(c0, 0, None)
                    load_ada(c0, 1, None)
                with act.Fori(0, FG) as g:
                    for c in range(2):
                        high_part(ffn_base(L) + 2 + c, g)
                    if L + 1 < layers:
                        load_ada(g + (c0 + 1), 0, g * 2 + (2 * c0 + 1))
                        load_ada(g + (c0 + 1), 1, g * 2 + (2 * c0 + 2))
                    high_part(ffn_base(L) + 4, g)
                    for p in range(2):
                        if p == 0:
                            act.wait_ge(pair_done[L], g + 1)
                        else:
                            act.wait_ge(split_free, unit_done(ffn_base(L) + g * 4 + 3))
                        act.wait_ge(pair_free[L], g * 2 + p + 1)
                        act.activation(act_tmp[:, p, tok(L)], bank[2 * p][:, tok(L)], ACT.Silu
                                       ).then_inc(gate_done[L], 1)
                    high_part(ffn_base(L) + 5, g)
                high_parts(ffn_base(L) + 4 * FG + 2, ffn_base(L) + FFN_UNITS + 2)

            def ssm_project(q, role):
                n = mix_base(SSM_LAYER) + q
                act.wait_ge(split_free, unit_done(n))
                if role < 2:
                    act.activation(zs[:, role, :], bank[role][:, :], ACT.Silu).then_inc(proj_read, 1)
                else:
                    r = role - 2
                    act.activation(xraw[:, r, :, 2:2 + SEG], half(bank[r % 2][:, :]), ACT.Copy).then_inc(proj_read, 1)

            def ssm_silu(g, par, r):
                act.wait_ge(conv_done, g * 4 + r + 1)
                act.activation(xc[:, par, r, :], tmp[:, r % 2, :], ACT.Silu).then_inc(xc_ready, 1)

            def ssm_group(it, gg):
                g = it * 2 + gg
                last = isinstance(it, int) and gg == 1
                base = mix_base(SSM_LAYER) + 7 + 6 * gg

                def decay(n):
                    act.wait_ge(seg_ready, g * 8 + n + 1)
                    act.activation(seg[:, n % 3, :], seg[:, n % 3, :], ACT.Exp).then_inc(seg_exp, 1)
                    if n >= 2:
                        act.wait_ge(yh_done, g * 8 + n - 1)
                    act.activation(act_tmp[:, n % 2, :], bank[(2, 4, 5)[n % 3]][:, :], ACT.Exp).then_inc(e_ready, 1)

                def unit(r):
                    ssm_project(it * 12 + (5 + 6 * gg + r), r)
                    high_part(base + r, it, 12)

                decay(0)
                decay(1)
                unit(0)
                unit(1)
                decay(2)
                decay(3)
                if not last:
                    unit(2)
                decay(4)
                decay(5)
                if not last:
                    unit(3)
                    ssm_silu(g + 1, 1 - gg, 0)
                    ssm_silu(g + 1, 1 - gg, 1)
                decay(6)
                decay(7)
                if not last:
                    unit(4)
                    unit(5)
                    ssm_silu(g + 1, 1 - gg, 2)
                    ssm_silu(g + 1, 1 - gg, 3)

            def ssm_mixer():
                b = mix_base(SSM_LAYER)
                t = lambda i: yall[0:64, i * N:(i + 1) * N]
                act.wait_ge(dt_neg, 1)
                act.activation(t(2), t(1), ACT.Exp)
                act.drain()
                act.activation(t(3), t(2), ACT.Ln, bias=col("one", 0)[0:64, :]).then_inc(dt_log, 1)
                act.activation(t(9)[:, 0:1], col("a_log", 0)[0:64, :], ACT.Exp).then_inc(a_ready, 1)
                high_part(b + 2)
                for q in range(1, 5):
                    ssm_project(q, q + 1)
                    high_part(b + q + 2)
                act.wait_ge(cum_ready, 1)
                for c in range(NC):
                    cols = slice(c * CH, (c + 1) * CH)
                    for rows, end in ((slice(0, 32), (c + 1) * CH - 1), (slice(32, 64), c * CH)):
                        ins = act.activation(t(7)[rows, cols], cum[rows, cols], ACT.Exp, scale=-1.0,
                                             bias=cum[rows, end:end + 1])
                ins.then_inc(w_ready, 1)
                act.wait_ge(tot_ready, 1)
                act.activation(tokq[:, 3, :, :], bank[3][:, 256:512].rearrange("p (c h) -> p c h", c=NC), ACT.Exp
                               ).then_inc(tot_ready, 1)
                for r in range(4):
                    ssm_silu(0, 0, r)
                act.preload_act_table_set("natural_log_exp_and_others")
                with act.Fori(0, GROUPS // 2 - 1) as it:
                    ssm_group(it, 0)
                    ssm_group(it, 1)
                ssm_group(GROUPS // 2 - 1, 0)
                ssm_group(GROUPS // 2 - 1, 1)
                act.preload_act_table_set("natural_log_exp_and_others")
                act.wait_ge(yg_ready, 2 * GROUPS)
                for g in range(GROUPS):
                    for e in range(2):
                        if g:
                            act.wait_ge(gsq_used, g)
                        act.activation(act_tmp[:, e, :], yall[:, (2 * g + e) * N:(2 * g + e + 1) * N], ACT.Square
                                       ).then_inc(gsq_ready, 1)
                    act.wait_ge(gsq_used, g + 1)
                    if g:
                        act.wait_ge(grs_used, g)
                    act.activation(rs[:, :], bank[4 + g % 2][:, :], ACT.Ln, scale=4.0, bias=col("eps_rms", 0))
                    act.drain()
                    act.activation(rs[:, :], rs[:, :], ACT.Exp, scale=-0.5).then_inc(grs_ready, 1)
                    if g:
                        high_part(b + 50 + g)
                high_parts(b + 58, b + 67)

            def attn_mixer():
                b = mix_base(ATTN_LAYER)
                act.preload_act_table_set("natural_log_exp_and_others")
                act.activation(credit[:, 3:4], col("one", 0), ACT.Copy).then_inc(qkv_free, 4)
                with act.Fori(0, 3) as g:
                    for c in range(3):
                        high_part(b + 2 + c, g)
                    for t in range(4):
                        if t < 3:
                            act.wait_ge(qkv_done, g * 3 + t + 1)
                        else:
                            act.wait_ge(split_free, unit_done(b + g * 4 + 3))
                        act.activation(qkv[:, bass.ds(g * (4 * N) + t * N, N)], bank[t][:, :], ACT.Copy
                                       ).then_inc(qkv_free, 1)
                    high_part(b + 5, g)
                with act.Fori(0, 5) as it:
                    for e in range(2):
                        act.activation(act_tmp[:, e, :], qkv[:, bass.ds(it * (2 * N) + e * N, N)], ACT.Square
                                       ).then_inc(hsq_ready, 1)
                    for e in range(2):
                        act.wait_ge(hms_done, it * 2 + e + 1)
                        act.activation(rsh[:, e, :], bank[4 + e][:, :], ACT.Ln, bias=col("eps_rms", 0))
                    act.drain()
                    for e in range(2):
                        act.activation(rsh[:, e, :], rsh[:, e, :], ACT.Exp, scale=-0.5).then_inc(hrs_ready, 1)
                    act.wait_ge(hn_ready, it * 2 + 2)
                with act.Fori(0, 8) as j:
                    for s in range(9):
                        if s < 8:
                            keys = SEG if s % 4 < 2 else N
                            act.wait_ge(mx_ready, j * 8 + s + 1)
                            act.activation(act_tmp[:, s % 2, 0:keys], bank[s % 2][:, 0:keys], ACT.Exp, scale=0.125,
                                           bias=asm_[:, s % 4, 1:2], accum_out=asm_[:, s % 4, 2:3]).then_inc(ex_ready, 1)
                        if s >= 1:
                            u = s - 1
                            keys = SEG if u % 4 < 2 else N
                            act.wait_ge(ptr_done, j * 8 + u + 1)
                            act.activation(pT[:, u % 2, 0:keys], bank[2 + u % 2][:, 0:keys], ACT.Copy
                                           ).then_inc(pt_ready, 1)
                high_parts(b + 14, b + 22)

            act.wait_ge(par_landed, 48)
            act.wait_ge(cleared, 1)
            for slot in range(2):
                load_ada(0, slot, None)
            act.activation(cond[:, :, 0:2], condraw[:, :, :], ACT.Silu).then_inc(cond_ready, 1)
            with act.Fori(0, CHUNKS - 1) as c:
                load_ada(c + 1, 0, c * 2 + 1)
                load_ada(c + 1, 1, c * 2 + 2)
            high_parts(0, 2)
            for L in range(layers):
                residual(L, MIX)
                if L in CONV_LAYERS:
                    conv_mixer(L)
                elif L == SSM_LAYER:
                    ssm_mixer()
                else:
                    attn_mixer()
                norm_scale(MIX, L, lambda m: h[:, m, tok(L)])
                norm_bias(MIX, L)
                residual(L, FFN)
                ffn(L)
                norm_scale(FFN, L, lambda m: h[:, m, tok(L)])
                norm_bias(FFN, L)

        @block.tensor
        def _(pe):
            def four_tiles(n, slot, xk, banks, L, start, last=False, tile_done=(), before=None):
                pe.wait_ge(split_ready, n + 1)
                for t in range(4):
                    if before is not None:
                        before(t)
                    for kk in range(2):
                        w = slice((kk * 4 + t) * P, (kk * 4 + t + 1) * P)
                        hi, lo = xk[kk]
                        for i, (a, b) in enumerate(((wh, hi), (wl, hi), (wh, lo))):
                            mm = pe.matmul(banks[t][:, tok(L)], a[:, slot, w], b, start=start and kk == 0 and i == 0,
                                           stop=last and kk == 1 and i == 2)
                    if t == 3:
                        mm.then_inc(split_free, 1)
                    elif last and tile_done and tile_done[t] is not None:
                        mm.then_inc(tile_done[t], 1)

            def x_tiles(L, ku):
                return [(xh[:, 2 * ku + kk, tok(L)], xl[:, 2 * ku + kk, tok(L)]) for kk in range(2)]

            def out_product(n0, L, operand):
                for s in range(2):
                    for ku in range(4):
                        n = n0 + 4 * s + ku
                        pe.wait_ge(x_ready, X_BASE[operand, L] + 2 * ku + 2)
                        four_tiles(n, n % 2, x_tiles(L, ku), bank[4 * s:4 * s + 4], L, ku == 0, ku == 3, [y_done] * 3)

            def norm_sums(kind, L, src):
                li = NORMS.index((kind, L))
                for m in range(KT):
                    pe.wait_ge(z_ready, KT * li + m + 1)
                    mm = pe.matmul(bank[0][:, tok(L)], meanm[:, :], src(m), start=m == 0, stop=m == KT - 1)
                mm.then_inc(mean_done, 1)
                for m in range(KT):
                    pe.wait_ge(sq_ready, KT * li + m + 1)
                    pe.matmul(bank[1][:, tok(L)], meanm[:, :], act_tmp[:, m % 2, tok(L)], start=m == 0,
                              stop=m == KT - 1).then_inc(sq_used, 1)

            def ada_rows(c):
                for s in range(2):
                    pe.wait_ge(ada_landed[s], 16 * (c + 1))
                    for k in range(4):
                        mm = pe.matmul(bank[4][32 * k:32 * k + 32, :], cond[:, 4 * s + k, :], ada[:, s, k, :],
                                       start=s == 0, stop=s == 1)
                    mm.then_inc(ada_used, 1)

            def ada_columns(c):
                pe.wait_ge(ada_row, c + 1)
                for q in range(4):
                    mm = pe.matmul(bank[5][:, 2 * q:2 * q + 2], adarow[:, q * P:(q + 1) * P],
                                   cst[:, CST["sel"]:CST["sel"] + 2], start=True, stop=True)
                mm.then_inc(ada_col, 1)

            def conv_mixer(L):
                def before(t):
                    if t % 2 == 0:
                        pe.wait_ge(cpair_free[L], g * 2 + t // 2 + 1)
                with pe.Fori(0, 4) as g:
                    for ku in range(4):
                        pe.wait_ge(x_ready, X_BASE[MIX, L] + 2 * ku + 2)
                        four_tiles(g * 4 + (mix_base(L) + ku), (mix_base(L) + ku) % 2, x_tiles(L, ku), bank[0:4], L,
                                   ku == 0, ku == 3, [None, cpair_done[L], None], before if ku == 0 else None)
                pe.wait_ge(cpair_free[L], 2 + KT)
                norm_sums("conv", L, lambda m: cz[:, m * N + first(L):(m + 1) * N])
                out_product(mix_base(L) + 16, L, "conv")

            def ffn(L):
                def before(t):
                    if t % 2 == 0:
                        pe.wait_ge(pair_free[L], g * 2 + t // 2 + 1)
                with pe.Fori(0, FG) as g:
                    for ku in range(4):
                        pe.wait_ge(x_ready, X_BASE[FFN, L] + 2 * ku + 2)
                        four_tiles(g * 4 + (ffn_base(L) + ku), (ffn_base(L) + ku) % 2, x_tiles(L, ku), bank[0:4], L,
                                   ku == 0, ku == 3, [None, pair_done[L], None], before if ku == 0 else None)
                        if L + 1 < layers and ku == 1:
                            ada_rows(g + CHUNKS * (L + 1))
                        if L + 1 < layers and ku == 2:
                            ada_columns(g + CHUNKS * (L + 1))
                if L + 1 < layers:
                    ada_rows(CHUNKS * (L + 1) + FG)
                    ada_columns(CHUNKS * (L + 1) + FG)
                n0 = ffn_base(L) + 4 * FG

                def hid(k):
                    at = bass.ds(k * N + first(L), N - first(L))
                    return hidh[:, at], hidl[:, at]

                pe.wait_ge(pair_free[L], 2 + HT)
                for s in range(2):
                    if s == 1 and L + 1 < layers:
                        pe.wait_ge(mod_ready, CHUNKS * (L + 2))
                    banks = bank[4 * s:4 * s + 4]

                    def unit(ku, j, start, last):
                        four_tiles(n0 + FG * s + ku, (n0 + FG * s + j) % 2, [hid(ku * 2), hid(ku * 2 + 1)], banks, L,
                                   start, last, [y_done] * 3)
                    pe.wait_ge(hid_ready[L], HT - 2)
                    unit(0, 0, True, False)
                    with pe.Fori(0, (FG - 3) // 2) as i:
                        unit(i * 2 + 1, 1, False, False)
                        unit(i * 2 + 2, 0, False, False)
                    unit(FG - 2, FG - 2, False, False)
                    pe.wait_ge(hid_ready[L], HT)
                    unit(FG - 1, FG - 1, False, True)

            def one_tile(q, slot, to):
                n = q + mix_base(SSM_LAYER)
                pe.wait_ge(split_ready, n + 1)
                for k in range(KT):
                    w = slice(k * P, (k + 1) * P)
                    for i, (a, b) in enumerate(((wh, xh), (wl, xh), (wh, xl))):
                        mm = pe.matmul(to[:, :], a[:, slot, w], b[:, k, :], start=k == 0 and i == 0,
                                       stop=k == KT - 1 and i == 2)
                mm.then_inc(split_free, 1)

            ORDER = ((0, 1, 2, 3), (1, 0, 3, 2))

            def ssm_group(it, gg):
                g = it * 2 + gg
                last = isinstance(it, int) and gg == 1
                B, C, x0 = xc[:, gg, 0, :], xc[:, gg, 1, :], xc[:, gg, 2:4, :]
                ch = lambda c: slice(c * CH, (c + 1) * CH)
                ident = cst[:, 0:P]

                def unit(r):
                    q = it * 12 + (5 + 6 * gg + r)
                    pe.wait_ge(proj_read, it * 12 + (3 + 6 * gg + r))
                    one_tile(q, (mix_base(SSM_LAYER) + 5 + 6 * gg + r) % 2, bank[r % 2])

                def broadcast(n):
                    if n >= 3:
                        pe.wait_ge(seg_ready, g * 8 + n - 2)
                        pe.wait_ge(e_ready, g * 8 + n - 2)
                    pe.matmul(bank[(2, 4, 5)[n % 3]][:, :], pick[0:64, (n % 2) * HPG + n // 2, :], cum[0:64, :],
                              start=True, stop=True).then_inc(r_done, 1)

                def head(n):
                    r, d = divmod(n, 2)
                    pe.wait_ge(m_ready, g * 8 + n + 1)
                    pe.wait_ge(ce_ready, g * 8 + n + 1)
                    if n == 0:
                        pe.wait_ge(st_read, g * 2 + 2)
                    y = bank[6 + r // 2][64 * (r % 2):64 * (r % 2) + 64, :]
                    f = slice(r * HD, (r + 1) * HD)
                    for c in range(NC):
                        mm = pe.matmul(y[:, ch(c)], xdt[:, d, c, f], seg[:, n % 3, ch(c)], start=d == 0 and c == 0,
                                       stop=d == 1 and c == ORDER[1][0], skip_group_check=True)
                        at = ORDER[d].index(c)
                        if at:
                            mm = pe.matmul(y[:, ch(c)], hst[:, d, at - 1, f], act_tmp[:, n % 2, ch(c)], start=False,
                                           stop=d == 1, skip_group_check=True)
                    mm.then_inc(yh_done, 1)

                pe.wait_ge(xc_ready, g * 4 + 4)
                for c in range(NC):
                    mm = pe.transpose(bank[2][:, ch(c)], B[:, ch(c)], ident)
                mm.then_inc(bt_done, 1)
                for c in range(NC):
                    for t in range(2):
                        at = (c % 2) * 2 * P + t * P
                        mm = pe.transpose(bank[4 + c // 2][:, at:at + P], x0[:, t, ch(c)], ident)
                mm.then_inc(xt_done, 1)
                for c in range(NC):
                    mm = pe.matmul(bank[3][:, ch(c)], B[:, ch(c)], C[:, ch(c)], start=True, stop=True)
                mm.then_inc(cb_done, 1)
                pe.wait_ge(cb_read, g + 1)
                for d in range(2):
                    pe.wait_ge(xw_ready, g * 2 + d + 1)
                    for i in range(3):
                        to, at = STATES[3 * d + i]
                        mm = pe.matmul(bank[to][:, at * 256:at * 256 + 256], btok[:, ORDER[d][i], :],
                                       xw[:, ORDER[d][i], :], start=True, stop=True)
                    mm.then_inc(st_done, 1)
                pe.wait_ge(pick_ready, g + 1)
                broadcast(0)
                broadcast(1)
                broadcast(2)
                unit(0)
                unit(1)
                head(0)
                broadcast(3)
                head(1)
                broadcast(4)
                if not last:
                    unit(2)
                head(2)
                broadcast(5)
                head(3)
                broadcast(6)
                if not last:
                    unit(3)
                head(4)
                broadcast(7)
                head(5)
                if not last:
                    unit(4)
                head(6)
                head(7)
                if not last:
                    unit(5)

            def ssm_mixer():
                t = lambda i: yall[0:64, i * N:(i + 1) * N]
                for k in range(KT):
                    pe.wait_ge(x_ready, X_BASE[MIX, SSM_LAYER] + k + 1)
                for q in range(5):
                    if q == 2:
                        pe.wait_ge(dt_read, 1)
                    if q > 2:
                        pe.wait_ge(proj_read, q - 2)
                    one_tile(q, (mix_base(SSM_LAYER) + q) % 2, bank[(q + 1) % 2])
                pe.wait_ge(rows_ready, 1)
                for q, src in enumerate((cum[0:64, :], t(0), t(7))):
                    for c in range(NC):
                        at = (q % 2) * 256 + c * 64
                        pe.transpose(bank[2 + q // 2][:, at:at + 64], src[:, c * CH:(c + 1) * CH], cst[0:64, 0:64])
                pe.matmul(bank[3][:, 256:512], t(8)[:, 0:P], t(10)[:, 0:256], start=True, stop=True
                          ).then_inc(toks_done, 1)
                pe.wait_ge(tot_ready, 2)
                with pe.Fori(0, GROUPS // 2 - 1) as it:
                    ssm_group(it, 0)
                    ssm_group(it, 1)
                ssm_group(GROUPS // 2 - 1, 0)
                ssm_group(GROUPS // 2 - 1, 1)
                n0 = mix_base(SSM_LAYER) + 49

                def x16(k):
                    a, b = (xh, xl) if k < KT else (x2h, x2l)
                    return a[:, k % KT, :], b[:, k % KT, :]

                def group_square(g):
                    pe.wait_ge(gsq_ready, 2 * g + 2)
                    if g >= 2:
                        pe.wait_ge(grs_ready, g - 1)
                    for e in range(2):
                        mm = pe.matmul(bank[4 + g % 2][:, :], meanm[:, :], act_tmp[:, e, :], start=e == 0, stop=e == 1)
                    mm.then_inc(gsq_used, 1)

                group_square(0)
                for s in range(2):
                    for ku in range(8):
                        if s == 0 and ku + 1 < GROUPS:
                            group_square(ku + 1)
                        pe.wait_ge(x_ready, X_BASE["ssm", SSM_LAYER] + 2 * ku + 2)
                        n = n0 + 8 * s + ku
                        four_tiles(n, n % 2, [x16(2 * ku), x16(2 * ku + 1)], bank[4 * s:4 * s + 4], SSM_LAYER, ku == 0,
                                   ku == 7, [y_done] * 3)

            def attn_mixer():
                L = ATTN_LAYER
                b = mix_base(L)

                def before(t):
                    pe.wait_ge(qkv_free, g * 4 + t + 1)
                with pe.Fori(0, 3) as g:
                    for ku in range(4):
                        pe.wait_ge(x_ready, X_BASE[MIX, L] + 2 * ku + 2)
                        four_tiles(g * 4 + (b + ku), (b + ku) % 2, x_tiles(L, ku), bank[0:4], L, ku == 0, ku == 3,
                                   [qkv_done] * 3, before if ku == 0 else None)
                pe.wait_ge(qkv_free, 16)
                for c in range(NC):
                    for t in range(2):
                        at = (c % 2) * 2 * P + t * P
                        mm = pe.transpose(bank[6 + c // 2][:, at:at + P],
                                          qkv[:, (10 + t) * N + c * CH:(10 + t) * N + (c + 1) * CH], cst[:, 0:P])
                mm.then_inc(vt_done, 1)
                pe.wait_ge(vt_read, 1)
                with pe.Fori(0, 5) as it:
                    for e in range(2):
                        pe.wait_ge(hsq_ready, it * 2 + e + 1)
                        pe.matmul(bank[4 + e][:, :], cst[:, CST["headmean"]:CST["headmean"] + P], act_tmp[:, e, :],
                                  start=True, stop=True).then_inc(hms_done, 1)
                    for e in range(2):
                        pe.wait_ge(hn_ready, it * 2 + e + 1)
                        pe.matmul(bank[6 + e][:, 0:SEG], cst[:, CST["rot"]:CST["rot"] + P],
                                  qkv[:, bass.ds(it * (2 * N) + (e * N + SEG), SEG)], start=True, stop=True
                                  ).then_inc(rot_done, 1)
                pe.wait_ge(rope_done, 10)

                def heads(j, kv):
                    pe.wait_ge(q_ready, j + 1)
                    for s in range(10):
                        if s < 8:
                            e, qt = divmod(s, 4)
                            keys = SEG if qt < 2 else N
                            rows = slice(64 * e, 64 * e + 64)
                            if s >= 2:
                                pe.wait_ge(ex_ready, j * 8 + s - 1)
                            pe.matmul(bank[s % 2][:, 0:keys], qcur[rows, qt * CH:(qt + 1) * CH],
                                      qkv[rows, kv * N:kv * N + keys], start=True, stop=True).then_inc(sc_done, 1)
                        if 1 <= s < 9:
                            u = s - 1
                            pe.wait_ge(pr_ready, j * 8 + u + 1)
                            if u >= 2:
                                pe.wait_ge(pt_ready, j * 8 + u - 1)
                            for c in range(2 if u % 4 < 2 else 4):
                                mm = pe.transpose(bank[2 + u % 2][:, c * CH:(c + 1) * CH],
                                                  act_tmp[:, u % 2, c * CH:(c + 1) * CH], cst[:, 0:P])
                            mm.then_inc(ptr_done, 1)
                        if s >= 2:
                            u = s - 2
                            e, qt = divmod(u, 4)
                            v = slice((2 * kv + e) * HD, (2 * kv + e + 1) * HD)
                            pe.wait_ge(pt_ready, j * 8 + u + 1)
                            nc_ = 2 if qt < 2 else 4
                            for c in range(nc_):
                                mm = pe.matmul(bank[4][64 * e:64 * e + 64, qt * CH:(qt + 1) * CH], vtok[:, c, v],
                                               pT[:, u % 2, c * CH:(c + 1) * CH], start=c == 0, stop=c == nc_ - 1)
                            mm.then_inc(pv_done, 1)
                for kv in range(2):
                    with pe.Fori(0, 4) as r:
                        heads(r + 4 * kv, kv)
                out_product(b + 12, L, "attn")

            pe.wait_ge(cond_ready, 1)
            pe.wait_ge(par_landed, 48)
            with pe.Fori(0, CHUNKS) as c:
                ada_rows(c)
                ada_columns(c)
            for L in range(layers):
                if L in CONV_LAYERS:
                    conv_mixer(L)
                elif L == SSM_LAYER:
                    ssm_mixer()
                else:
                    attn_mixer()
                norm_sums(MIX, L, lambda m: h[:, m, tok(L)])
                ffn(L)
                norm_sums(FFN, L, lambda m: h[:, m, tok(L)])

        @block.vector
        def _(dve):
            def ada_to_sbuf(c):
                dve.wait_ge(ada_used, c * 2 + 2)
                dve.tensor_copy(adarow[:, :], bank[4][:, :]).then_inc(ada_row, 1)

            def ada_to_mod(c, chunk, L):
                dve.wait_ge(ada_col, c + 1)
                dve.tensor_tensor(mod[:, L % 2, bass.ds(chunk * 8, 8)], bank[5][:, 0:8],
                                  par[:, bass.ds(chunk * 8 + (PAR["ada_b"][0] + 96 * L), 8)], ALU.add
                                  ).then_inc(mod_ready, 1)

            def finish_mod(L):
                dve.drain()
                for m in (1, 4):
                    s = mod[:, L % 2, m * 16:m * 16 + 16]
                    last = dve.tensor_scalar(s, s, 1.0, None, ALU.add)
                if L in CONV_LAYERS:
                    gate = mod[:, L % 2, 32:48].rearrange("p (k c) -> p k c", c=2)
                    b = col(f"pw2_b{CONV_LAYERS.index(L)}", 0, KT)
                    for c in range(2):
                        dve.tensor_tensor(gbias[:, :, c], gate[:, :, c], b, ALU.mult)
                dve.drain()

            def modulate(L, which, k):
                if (which, L) == (MIX, 0):
                    dve.wait_ge(h_landed, 16)
                else:
                    dve.wait_ge(h_ready, KT * (2 * L + which - 1) + k + 1)
                for c in segs(L):
                    t = slice(c * SEG, (c + 1) * SEG)
                    sc, sh = modc(L, 3 * which + 1, k, c), modc(L, 3 * which, k, c)
                    dve.tensor_scalar(xh[:, k, t], h[:, k, t], sc, sh, ALU.mult, ALU.add)
                    dve.tensor_scalar(tmp[:, k % 2, t], h[:, k, t], sc, sh, ALU.mult, ALU.add)
                dve.drain()
                dve.tensor_tensor(xl[:, k, tok(L)], tmp[:, k % 2, tok(L)], xh[:, k, tok(L)].bitcast(F32),
                                  ALU.subtract).then_inc(x_ready, 1)

            def residual_sum(L, which, n_sweep):
                dve.wait_ge(ah_ready, KT * (2 * L + which) + KT)
                for m in range(KT):
                    s, t = divmod(m, 4)
                    if t < 3:
                        dve.wait_ge(y_done, 6 * (2 * L + which) + 3 * s + t + 1)
                    else:
                        dve.wait_ge(split_free, unit_done(n_sweep[s]))
                    for c in segs(L):
                        u = slice(c * SEG, (c + 1) * SEG)
                        ins = dve.scalar_tensor_tensor(h[:, m, u], bank[m][:, u], modc(L, 3 * which + 2, m, c),
                                                       h[:, m, u], ALU.mult, ALU.add)
                    ins.then_inc(z_ready, 1)

            def centre(kind, L, src):
                li = NORMS.index((kind, L))
                dve.wait_ge(mean_done, li + 1)
                for m in range(KT):
                    dve.tensor_tensor(src(m), src(m), bank[0][:, tok(L)], ALU.subtract).then_inc(zc_ready, 1)

            def scaled(kind, L, m, z, gain):
                li = NORMS.index((kind, L))
                if m == 0:
                    dve.wait_ge(rstd_ready, li + 1)
                dve.scalar_tensor_tensor(z, z, gain, rs[:, tok(L)], ALU.mult, ALU.mult).then_inc(n_ready, 1)

            def post_norm(L, which, then=None):
                src = lambda m: h[:, m, tok(L)]
                centre(which, L, src)
                for m in range(KT):
                    scaled(which, L, m, src(m), col(f"ln_{lname(which)}_g{L}", m))
                    if then is not None and m >= 2:
                        modulate(*then, m - 2)
                if then is not None:
                    modulate(*then, KT - 2)
                    modulate(*then, KT - 1)

            def conv_mixer(L):
                j = CONV_LAYERS.index(L)
                lo, ns = (1, 1) if L == DEPTH - 1 else (0, 2)
                dve.memset(vbuf[:, :, :, 0:PAD], 0.0)
                dve.memset(vbuf[:, :, :, PAD + SEG:VW], 0.0)
                dve.memset(credit[:, 2:3], 0.0).then_inc(cpair_free[L], 2)
                with dve.Fori(0, 4) as g:
                    for p in range(2):
                        m = g * 2 + p
                        dve.wait_ge(cgate_done[L], m + 1)
                        dve.scalar_tensor_tensor(
                            vbuf[:, p, lo:2, PAD:PAD + SEG], half(bank[2 * p][:, :])[:, lo:2, :],
                            par[:, bass.ds(m + PAR[f"pw1_b{j}"][0], 1)], half(act_tmp[:, p, :])[:, lo:2, :],
                            ALU.add, ALU.mult).then_inc(cpair_free[L], 1)
                        dve.tensor_copy(dwc[:, p, :],
                                        par[:, bass.ds(m * (TAPS + 1) + PAR[f"dw{j}"][0], TAPS + 1)])
                        dve.drain()
                        acc = half(cacc[:, p, :])[:, lo:2, :]
                        for tap in range(TAPS):
                            v = vbuf[:, p, lo:2, tap:tap + SEG]
                            w = dwc[:, p, tap:tap + 1]
                            if tap == 0:
                                dve.tensor_scalar(acc, v, w, dwc[:, p, TAPS:TAPS + 1], ALU.mult, ALU.add)
                            elif tap < TAPS - 1:
                                dve.scalar_tensor_tensor(acc, v, w, acc, ALU.mult, ALU.add)
                            else:
                                dst = cz[:, bass.ds(m * N + first(L), N - first(L))]
                                dve.scalar_tensor_tensor(dst.rearrange("p (s t) -> p s t", s=ns), v, w, acc,
                                                         ALU.mult, ALU.add).then_inc(z_ready, 1)
                            dve.drain()
                z = lambda m: cz[:, m * N + first(L):(m + 1) * N]
                centre("conv", L, z)
                for m in range(KT):
                    scaled("conv", L, m, z(m), col(f"cn_g{j}", m))
                for m in range(KT):
                    dve.wait_ge(silu_ready, KT * j + m + 1)
                    dve.tensor_copy(xh[:, m, tok(L)], z(m))
                    dve.drain()
                    dve.tensor_tensor(xl[:, m, tok(L)], z(m), xh[:, m, tok(L)].bitcast(F32), ALU.subtract
                                      ).then_inc(x_ready, 1)

            def ffn(L):
                dve.memset(credit[:, 2:3], 0.0).then_inc(pair_free[L], 2)
                with dve.Fori(0, FG) as g:
                    if L + 1 < layers:
                        ada_to_sbuf(g + CHUNKS * (L + 1))
                        ada_to_mod(g + CHUNKS * (L + 1), g, L + 1)
                    for p in range(2):
                        m = g * 2 + p
                        at = bass.ds(m * N + first(L), N - first(L))
                        s, y = act_tmp[:, p, tok(L)], bank[2 * p + 1][:, tok(L)]
                        dve.wait_ge(gate_done[L], m + 1)
                        dve.tensor_tensor(tmp[:, p, tok(L)], s, y, ALU.mult)
                        dve.tensor_tensor(hidh[:, at], s, y, ALU.mult).then_inc(pair_free[L], 1)
                        dve.drain()
                        dve.tensor_tensor(hidl[:, at], tmp[:, p, tok(L)], hidh[:, at].bitcast(F32), ALU.subtract
                                          ).then_inc(hid_ready[L], 1)
                if L + 1 < layers:
                    ada_to_sbuf(CHUNKS * (L + 1) + FG)
                    ada_to_mod(CHUNKS * (L + 1) + FG, FG, L + 1)
                    finish_mod(L + 1)

            def ssm_conv(g, r):
                if r == 0:
                    at = PAR["sconv"][0]
                    for role, first_tile, step in ((0, 16, 1), (1, 24, 1), (2, 0, 2), (3, 1, 2)):
                        src = par[:, bass.ds(g * ((CW + 1) * step) + (at + (CW + 1) * first_tile), CW + 1)]
                        dve.tensor_copy(sconv[:, role, :], src)
                    dve.drain()
                if isinstance(g, int) and g == 0:
                    dve.wait_ge(proj_read, r + 1)
                    if r >= 2:
                        dve.wait_ge(xc_ready, r - 1)
                else:
                    dve.wait_ge(proj_read, g * 6 + r + 1)
                    dve.wait_ge(xc_ready, g * 4 + r - 1)
                acc = half(tmp[:, r % 2, :])
                for tap in range(CW):
                    v, w = xraw[:, r, :, tap:tap + SEG], sconv[:, r, tap:tap + 1]
                    if tap == 0:
                        ins = dve.tensor_scalar(acc, v, w, sconv[:, r, CW:CW + 1], ALU.mult, ALU.add)
                    else:
                        dve.drain()
                        ins = dve.scalar_tensor_tensor(acc, v, w, acc, ALU.mult, ALU.add)
                ins.then_inc(conv_done, 1)

            ORDER = ((0, 1, 2, 3), (1, 0, 3, 2))

            def ssm_group(it, gg):
                g = it * 2 + gg
                last = isinstance(it, int) and gg == 1
                heads4 = lambda a: a.rearrange("p c (r f) -> p c r f", r=HPG)

                def wide(a, n):
                    shape = list(a.shape)
                    return a.unsqueeze(len(shape)).broadcast_to(shape + [n])

                for d in range(2):
                    dve.tensor_copy(tg[:, :, d, :], tokq[:, :, :, :].rearrange("p q c h -> p (q c) h")
                                    [:, :, bass.ds(g * HPG + d * 32, HPG)])
                    ins = dve.tensor_copy(pick[0:64, d * HPG:(d + 1) * HPG, :],
                                          wide(cst[0:64, bass.ds(g * HPG + d * 32, HPG)], P))
                ins.then_inc(pick_ready, 1)
                dve.wait_ge(bt_done, g + 1)
                dve.tensor_copy(btok[:, :, :], bank[2][:, :].rearrange("p (c f) -> p c f", c=NC))
                dve.wait_ge(cb_done, g + 1)
                for d, mask in enumerate(("mask_f", "mask_b")):
                    m = cst[:, CST[mask]:CST[mask] + P].unsqueeze(1).broadcast_to([P, NC, P])
                    ins = dve.tensor_tensor(cbm[:, d, :].rearrange("p (c f) -> p c f", c=NC),
                                            bank[3][:, :].rearrange("p (c f) -> p c f", c=NC), m, ALU.mult)
                ins.then_inc(cb_read, 1)
                dve.drain()
                dve.wait_ge(xt_done, g + 1)

                def scaled_x(dst, q, d):
                    for b in range(2):
                        f = tg[:, q * NC + 2 * b:q * NC + 2 * b + 2, d, :]
                        ins = dve.tensor_tensor(heads4(dst[:, 2 * b:2 * b + 2, :]),
                                                heads4(bank[4 + b][:, :].rearrange("p (c f) -> p c f", c=2)),
                                                wide(f, HD), ALU.mult)
                    return ins

                def states(d):
                    dve.wait_ge(st_done, g * 2 + d + 1)
                    for i in range(3):
                        to, at = STATES[3 * d + i]
                        new = bank[to][:, at * 256:at * 256 + 256]
                        if i == 0:
                            ins = dve.tensor_copy(hst[:, d, 0, :], new)
                            continue
                        f = tg[:, 3 * NC + ORDER[d][i], d, :]
                        dve.drain()
                        r4 = lambda a: a.rearrange("p (r f) -> p r f", r=HPG)
                        dve.tensor_tensor(r4(hst[:, d, i, :]), r4(hst[:, d, i - 1, :]), wide(f, HD), ALU.mult)
                        dve.drain()
                        if d == 0 and i == 2:
                            dve.wait_ge(st_done, g * 2 + 2)
                        ins = dve.tensor_tensor(hst[:, d, i, :], hst[:, d, i, :], new, ALU.add)
                    ins.then_inc(st_read, 1)

                scaled_x(xw, 2, 0).then_inc(xw_ready, 1)
                scaled_x(xdt[:, 0, :, :], 1, 0)
                scaled_x(xdt[:, 1, :, :], 1, 1)
                dve.wait_ge(st_done, g * 2 + 1)
                scaled_x(xw, 2, 1).then_inc(xw_ready, 1)
                states(0)
                states(1)

                def exponent(n):
                    r, d = divmod(n, 2)
                    dve.wait_ge(r_done, g * 8 + n + 1)
                    if n >= 3:
                        dve.wait_ge(yh_done, g * 8 + n - 2)
                    for c in range(NC):
                        cols = slice(c * CH, (c + 1) * CH)
                        ins = dve.tensor_scalar(seg[:, n % 3, cols], bank[(2, 4, 5)[n % 3]][:, cols],
                                                tg[:, c, d, r:r + 1], 0.0, ALU.subtract, ALU.min)
                    ins.then_inc(seg_ready, 1)

                def weigh(n):
                    d = n % 2
                    dve.wait_ge(seg_exp, g * 8 + n + 1)
                    dve.tensor_tensor(seg[:, n % 3, :], seg[:, n % 3, :], cbm[:, d, :], ALU.mult).then_inc(m_ready, 1)
                    dve.wait_ge(e_ready, g * 8 + n + 1)
                    dve.tensor_tensor(act_tmp[:, n % 2, :], act_tmp[:, n % 2, :], xc[:, gg, 1, :], ALU.mult
                                      ).then_inc(ce_ready, 1)

                for n in range(9):
                    if n < 8:
                        exponent(n)
                    if n >= 1:
                        weigh(n - 1)
                    if not last and n == 4:
                        ssm_conv(g + 1, 0)
                    if not last and n == 6:
                        ssm_conv(g + 1, 1)
                dve.wait_ge(yh_done, g * 8 + 8)
                dve.wait_ge(proj_read, g * 6 + 6)
                for t in range(2):
                    y = yall[:, bass.ds(g * (2 * N) + t * N, N)]
                    dve.scalar_tensor_tensor(y, xc[:, gg, 2 + t, :], par[:, bass.ds(g * 2 + (PAR["sskip"][0] + t), 1)],
                                             bank[6 + t][:, :], ALU.mult, ALU.add)
                dve.drain()
                for t in range(2):
                    y = yall[:, bass.ds(g * (2 * N) + t * N, N)]
                    dve.tensor_tensor(y, y, zs[:, t, :], ALU.mult).then_inc(yg_ready, 1)
                if not last:
                    ssm_conv(g + 1, 2)
                    ssm_conv(g + 1, 3)

            def ssm_mixer():
                t = lambda i: yall[0:64, i * N:(i + 1) * N]
                x, nx, e, lg, d1, eq, w, ones, a, diag = (t(i) for i in (4, 1, 2, 3, 5, 6, 7, 8, 9, 10))
                dt = t(0)
                dve.memset(xraw[:, :, :, 0:2], 0.0)
                dve.memset(xraw[:, :, :, 2 + SEG:XW], 0.0)
                dve.memset(ones, 1.0)
                dve.wait_ge(split_free, unit_done(mix_base(SSM_LAYER)))
                dve.tensor_scalar(x, bank[1][0:64, :], col("dt_b", 0)[0:64, :], None, ALU.add).then_inc(dt_read, 1)
                dve.drain()
                dve.tensor_scalar(nx, x, -1.0, None, ALU.mult)
                dve.drain()
                dve.tensor_tensor(nx, nx, x, ALU.min).then_inc(dt_neg, 1)
                dve.wait_ge(dt_log, 1)
                dve.tensor_scalar(d1, e, 1.0, -1.0, ALU.add, ALU.add)
                dve.drain()
                dve.tensor_scalar(eq, d1, 0.0, None, ALU.is_equal)
                dve.drain()
                dve.tensor_tensor(d1, d1, eq, ALU.add)
                dve.drain()
                dve.reciprocal(d1, d1)
                dve.tensor_tensor(lg, lg, e, ALU.mult)
                dve.drain()
                dve.tensor_tensor(lg, lg, d1, ALU.mult)
                dve.tensor_tensor(eq, eq, e, ALU.mult)
                dve.drain()
                dve.tensor_tensor(lg, lg, eq, ALU.add)
                dve.drain()
                dve.scalar_tensor_tensor(dt, x, 0.0, lg, ALU.max, ALU.add)
                dve.wait_ge(a_ready, 1)
                dve.drain()
                dve.tensor_scalar(nx, dt, a[:, 0:1], -1.0, ALU.mult, ALU.mult)
                dve.drain()
                for c in range(NC):
                    cols = slice(c * CH, (c + 1) * CH)
                    dve.tensor_tensor_scan(cum[0:32, cols], ones[0:32, 0:CH], nx[0:32, cols], 0.0, ALU.mult, ALU.add)
                    ins = dve.tensor_tensor_scan(cum[32:64, cols][:, ::-1], ones[32:64, 0:CH], nx[32:64, cols][:, ::-1],
                                                 0.0, ALU.mult, ALU.add)
                dve.drain()
                dve.memset(credit[:, 2:3], 0.0).then_inc(cum_ready, 1)
                for c in range(NC):
                    for rows, end in ((slice(0, 32), (c + 1) * CH - 1), (slice(32, 64), c * CH)):
                        dve.tensor_scalar(diag[rows, c * 64:(c + 1) * 64], cst[rows, 0:64], cum[rows, end:end + 1],
                                          None, ALU.mult)
                dve.wait_ge(w_ready, 1)
                dve.tensor_tensor(w, w, dt, ALU.mult)
                dve.drain()
                dve.memset(credit[:, 2:3], 0.0).then_inc(rows_ready, 1)
                dve.wait_ge(toks_done, 1)
                dve.tensor_copy(tokq[:, 0:2, :, :], bank[2][:, :].rearrange("p (q c h) -> p q c h", q=2, c=NC))
                dve.tensor_copy(tokq[:, 2, :, :], bank[3][:, 0:256].rearrange("p (c h) -> p c h", c=NC)
                                ).then_inc(tot_ready, 1)
                dve.wait_ge(tot_ready, 2)
                for r in range(4):
                    ssm_conv(0, r)
                with dve.Fori(0, GROUPS // 2 - 1) as it:
                    ssm_group(it, 0)
                    ssm_group(it, 1)
                ssm_group(GROUPS // 2 - 1, 0)
                ssm_group(GROUPS // 2 - 1, 1)
                for g in range(GROUPS):
                    dve.wait_ge(grs_ready, g + 1)
                    for e in range(2):
                        k = 2 * g + e
                        a, b = (xh, xl) if k < KT else (x2h, x2l)
                        args = (yall[:, k * N:(k + 1) * N], col("snorm", k), rs[:, :], ALU.mult, ALU.mult)
                        dve.scalar_tensor_tensor(tmp[:, e, :], *args)
                        dve.scalar_tensor_tensor(a[:, k % KT, :], *args)
                    dve.drain()
                    for e in range(2):
                        k = 2 * g + e
                        a, b = (xh, xl) if k < KT else (x2h, x2l)
                        dve.tensor_tensor(b[:, k % KT, :], tmp[:, e, :], a[:, k % KT, :].bitcast(F32), ALU.subtract
                                          ).then_inc(x_ready, 1)
                    dve.memset(credit[:, 2:3], 0.0).then_inc(grs_used, 1)

            def attn_mixer():
                dve.wait_ge(vt_done, 1)
                for b in range(2):
                    ins = dve.tensor_copy(vtok[:, 2 * b:2 * b + 2, :], bank[6 + b][:, :].rearrange("p (c f) -> p c f", c=2))
                ins.then_inc(vt_read, 1)
                cos, sin = (cst[:, CST[n]:CST[n] + SEG] for n in ("cos", "sin"))
                with dve.Fori(0, 5) as it:
                    for e in range(2):
                        x = qkv[:, bass.ds(it * (2 * N) + e * N, N)]
                        dve.wait_ge(hrs_ready, it * 2 + e + 1)
                        dve.scalar_tensor_tensor(x, x, par[:, bass.ds(it * 2 + (PAR["qk_g"][0] + e), 1)], rsh[:, e, :],
                                                 ALU.mult, ALU.mult).then_inc(hn_ready, 1)
                    dve.drain()
                    for e in range(2):
                        x = qkv[:, bass.ds(it * (2 * N) + (e * N + SEG), SEG)]
                        dve.wait_ge(rot_done, it * 2 + e + 1)
                        dve.tensor_tensor(tmp[:, e, 0:SEG], x, cos, ALU.mult)
                        dve.tensor_tensor(tmp[:, e, SEG:N], bank[6 + e][:, 0:SEG], sin, ALU.mult)
                    dve.drain()
                    for e in range(2):
                        x = qkv[:, bass.ds(it * (2 * N) + (e * N + SEG), SEG)]
                        dve.tensor_tensor(x, tmp[:, e, 0:SEG], tmp[:, e, SEG:N], ALU.add).then_inc(rope_done, 1)
                dve.drain()

                with dve.Fori(0, 8) as j:
                    dve.tensor_copy(qcur[:, :], qkv[:, bass.ds(j * N + 2 * N, N)]).then_inc(q_ready, 1)
                    for s in range(9):
                        if s < 8:
                            keys = SEG if s % 4 < 2 else N
                            a = asm_[:, s % 4, :]
                            dve.wait_ge(sc_done, j * 8 + s + 1)
                            dve.tensor_reduce(a[:, 0:1], bank[s % 2][:, 0:keys], mybir.AxisListType.X, ALU.max)
                            dve.drain()
                            dve.tensor_scalar(a[:, 1:2], a[:, 0:1], -0.125, None, ALU.mult).then_inc(mx_ready, 1)
                        if s >= 1:
                            u = s - 1
                            keys = SEG if u % 4 < 2 else N
                            a = asm_[:, u % 4, :]
                            dve.wait_ge(ex_ready, j * 8 + u + 1)
                            dve.reciprocal(a[:, 3:4], a[:, 2:3])
                            dve.drain()
                            dve.tensor_scalar(act_tmp[:, u % 2, 0:keys], act_tmp[:, u % 2, 0:keys], a[:, 3:4], None,
                                              ALU.mult).then_inc(pr_ready, 1)
                    dve.wait_ge(pv_done, j * 8 + 8)
                    dve.tensor_copy(tmp[:, 0, :], bank[4][:, :])
                    dve.tensor_copy(xh[:, bass.ds(j, 1), :], bank[4][:, :].unsqueeze(1))
                    dve.drain()
                    dve.tensor_tensor(xl[:, bass.ds(j, 1), :], tmp[:, 0:1, :], xh[:, bass.ds(j, 1), :].bitcast(F32),
                                      ALU.subtract).then_inc(x_ready, 1)

            dve.memset(cond[:, :, :], 0.0).then_inc(cleared, 1)
            dve.memset(meanm[:, :], 1.0 / D)
            dve.drain()
            dve.wait_ge(par_landed, 48)
            with dve.Fori(0, CHUNKS) as c:
                ada_to_sbuf(c)
                ada_to_mod(c, c, 0)
            finish_mod(0)
            for k in range(KT):
                modulate(0, MIX, k)
            for L in range(layers):
                if L in CONV_LAYERS:
                    conv_mixer(L)
                    sweeps = [mix_base(L) + 19, mix_base(L) + 23]
                elif L == SSM_LAYER:
                    ssm_mixer()
                    sweeps = [mix_base(L) + 56, mix_base(L) + 64]
                else:
                    attn_mixer()
                    sweeps = [mix_base(L) + 15, mix_base(L) + 19]
                residual_sum(L, MIX, sweeps)
                post_norm(L, MIX, (L, FFN))
                ffn(L)
                n0 = ffn_base(L) + 4 * FG
                residual_sum(L, FFN, [n0 + FG - 1, n0 + 2 * FG - 1])
                post_norm(L, FFN, (L + 1, MIX) if L + 1 < layers else None)


def tiles(w):
    w = np.asarray(w)
    if w.shape[1] % P:
        w = np.concatenate([w, np.zeros((w.shape[0], P - w.shape[1] % P), w.dtype)], axis=1)
    return w.reshape(w.shape[0] // P, P, w.shape[1] // P, P).transpose(0, 2, 1, 3)


def head_order():
    heads = [8 * (j // 4) + j % 4 + 4 * e for j in range(8) for e in range(2)]
    return np.concatenate([np.arange(HD) + HD * x for x in heads])


def weight_units(i, layers=DEPTH):
    units = []

    def four(t, cols, ks):
        for k in ks:
            units.append([t[c][0][2 * k + kk, m] for kk in range(2) for c, m in enumerate(cols)])

    def groups(a, b, offset, n):
        for g in range(n):
            pick = [(a, 2 * g), (b, offset + 2 * g), (a, 2 * g + 1), (b, offset + 2 * g + 1)]
            for ku in range(4):
                units.append([t[2 * ku + kk, m] for kk in range(2) for t, m in pick])

    def sweeps(t, kn):
        for s in range(2):
            for ku in range(kn):
                units.append([t[2 * ku + kk, 4 * s + m] for kk in range(2) for m in range(4)])

    for L in range(layers):
        if L in CONV_LAYERS:
            j = CONV_LAYERS.index(L)
            t = tiles(i["conv_pw1_w"][j])
            groups(t, t, KT, 4)
            sweeps(tiles(i["conv_pw2_w"][j]), 4)
        if L == SSM_LAYER:
            t = tiles(i["ssm_in_w"][0])
            order = [48]
            for g in range(-1, GROUPS):
                order += [2 * g, 2 * g + 1] if g >= 0 else []
                order += [33 + g, 41 + g, 18 + 2 * g, 19 + 2 * g] if g + 1 < GROUPS else []
            units += [[t[k, m] for k in range(KT)] for m in order]
            sweeps(tiles(i["ssm_out_w"][0]), 8)
        if L == ATTN_LAYER:
            w = np.asarray(i["attn_qkv_w"][0])
            kv = HD * 4
            w = np.concatenate([w[:, D:D + kv], w[:, :D][:, head_order()], w[:, D + kv:]], axis=1)
            t = tiles(w)
            for g in range(3):
                for ku in range(4):
                    units.append([t[2 * ku + kk, 4 * g + m] for kk in range(2) for m in range(4)])
            sweeps(tiles(np.asarray(i["attn_out_w"][0])[head_order()]), 4)
        w1, w3 = tiles(i["ffn_w1"][L]), tiles(i["ffn_w3"][L])
        groups(w1, w3, 0, FG)
        sweeps(tiles(i["ffn_w2"][L]), FG)
    out = np.empty((len(units), P, 8, P), np.float32)
    for n, u in enumerate(units):
        for e, t in enumerate(u):
            out[n, :, e, :] = t
    return out.reshape(len(units), P, UNIT)


def small_parameters(i):
    out = np.zeros((P, NPAR), np.float32)

    def put(name, a):
        at, width = PAR[name]
        a = np.asarray(a)
        out[:a.shape[0], at:at + width] = a

    def columns(v):
        return np.asarray(v).reshape(-1, P).T

    for L in range(DEPTH):
        for w in ("mix", "ffn"):
            for s in "gb":
                put(f"ln_{w}_{s}{L}", columns(i[f"ln_{w}_{s}"][L]))
    for j in range(2):
        put(f"pw1_b{j}", columns(i["conv_pw1_b"][j]))
        dw = np.concatenate([np.asarray(i["conv_dw_w"][j]), np.asarray(i["conv_dw_b"][j])[None]])
        put(f"dw{j}", dw.reshape(TAPS + 1, KT, P).transpose(2, 1, 0).reshape(P, -1))
        put(f"cn_g{j}", columns(i["conv_norm_g"][j]))
        put(f"cn_b{j}", columns(i["conv_norm_b"][j]))
        put(f"pw2_b{j}", columns(i["conv_pw2_b"][j]))
    put("ada_b", np.repeat(np.asarray(i["ada_b"]).reshape(DEPTH * 48, P).T, 2, axis=1))
    conv = np.concatenate([np.asarray(i["ssm_conv_w"][0]), np.asarray(i["ssm_conv_b"])])
    put("sconv", conv.reshape(CW + 1, 32, P).transpose(2, 1, 0).reshape(P, -1))
    put("snorm", columns(i["ssm_norm_g"][0]))
    put("sskip", columns(np.repeat(np.asarray(i["ssm_d"][0]), HD)))
    put("dt_b", np.asarray(i["ssm_dt_bias"][0])[:, None])
    put("a_log", np.asarray(i["ssm_a_log"][0])[:, None])
    qk = [np.tile(np.asarray(i[f"attn_{n}_norm"][0]), 2)[:, None] for n in "kq"]
    put("qk_g", np.concatenate([qk[0]] * 2 + [qk[1]] * 8, axis=1))
    put("eps_ln", np.full((P, 1), LN_EPS, np.float32))
    put("eps_rms", np.full((P, 1), RMS_EPS, np.float32))
    put("one", np.ones((P, 1), np.float32))
    return out


def constants():
    c = np.zeros((P, NCST), np.float32)
    r = np.arange(P)
    c[:, 0:128] = np.eye(P)
    c[:, CST["mask_f"]:][:, :P] = r[None, :] >= r[:, None]
    c[:, CST["mask_b"]:][:, :P] = r[None, :] <= r[:, None]
    rot = np.zeros((P, P), np.float32)
    rot[r[1::2], r[0::2]] = -1.0
    rot[r[0::2], r[1::2]] = 1.0
    c[:, CST["rot"]:][:, :P] = rot
    c[:, CST["headmean"]:][:, :P] = (r[None, :] // HD == r[:, None] // HD) / np.float32(HD)
    inv = np.float32(10000.0) ** (-np.arange(0, 32, 2, dtype=np.float32) / np.float32(32))
    t = np.arange(SEG)
    ang = np.concatenate([(t // 64).astype(np.float32)[:, None] * inv, (t % 64).astype(np.float32)[:, None] * inv], 1)
    c[:, CST["cos"]:][:, :SEG] = np.cos(ang).T[(r % HD) // 2]
    c[:, CST["sin"]:][:, :SEG] = np.sin(ang).T[(r % HD) // 2]
    c[:, CST["sel"]:][:, :2] = r[:, None] % 32 == np.arange(2)[None, :]
    return c


def laid_out(i, layers=DEPTH):
    x = np.concatenate([np.asarray(i["ctx"])[0], np.asarray(i["x"])[0]])
    cond = np.stack([np.asarray(i["c_ctx"]), np.asarray(i["c"])[0]])
    adaw = np.asarray(i["ada_w"])[:layers].reshape(layers, KT, P, CHUNKS, N).transpose(0, 3, 2, 1, 4)
    return {
        "xT": np.ascontiguousarray(x.T.reshape(KT, P, N).transpose(1, 0, 2)),
        "condT": np.ascontiguousarray(cond.T.reshape(KT, P, 2).transpose(1, 0, 2)),
        "par": small_parameters(i),
        "cst": constants(),
        "adaw": np.ascontiguousarray(adaw.reshape(layers * CHUNKS, P, KT, N)),
        "wstream": weight_units(i, layers),
    }


def kernel(**inputs):
    import concourse.bacc as bacc
    from concourse.bass_utils import run_bass_kernel_spmd

    arrays = laid_out(inputs)
    nc = bacc.Bacc("TRN2", target_bir_lowering=False, num_devices=1)
    args = [nc.dram_tensor(k, a.shape, F32, kind="ExternalInput").ap() for k, a in arrays.items()]
    out = nc.dram_tensor("out", (P, KT, SEG), F32, kind="ExternalOutput").ap()
    program(nc, *args, out)
    got = run_bass_kernel_spmd(nc, [arrays], core_ids=[0]).results[0]["out"]
    return np.ascontiguousarray(got.transpose(2, 1, 0).reshape(1, SEG, D))
```

```python
from contextlib import ExitStack

import numpy as np
import concourse.bass as bass
from concourse import mybir

F32 = mybir.dt.float32
F32R = mybir.dt.float32r
ALU = mybir.AluOpType
ACT = mybir.ActivationFunctionType

P = 128
D = 1024
KT = D // P
SEG = 256
N = 2 * SEG
DEPTH = 4
MIX, FFN = 0, 1
ALPHA = (2 * DEPTH) ** 0.25
LN_EPS, RMS_EPS = 1e-5, 1e-6

TAPS = 31
PAD = (TAPS - 1) // 2
VW = SEG + 2 * PAD

FH = -(-8 * D // (3 * 256)) * 256
HT = FH // P
FG = HT // 2

DI = 2 * D
GROUPS = 8
HPG = 4
HD = 64
CW = 5
XW = SEG + CW - 1
CH = 128
NC = N // CH
CONV_LAYERS, SSM_LAYER, ATTN_LAYER = (0, 3), 1, 2

UNIT = 8 * P
CHUNKS = 6 * D // N

MIXER_UNITS = {0: 24, 1: 65, 2: 20, 3: 24}
FFN_UNITS = 4 * FG + 2 * FG


def mix_base(L):
    return sum(MIXER_UNITS[i] + FFN_UNITS for i in range(L))


def ffn_base(L):
    return mix_base(L) + MIXER_UNITS[L]


UNITS = ffn_base(DEPTH - 1) + FFN_UNITS

NORMS = [("conv", 0), (MIX, 0), (FFN, 0), (MIX, 1), (FFN, 1), (MIX, 2), (FFN, 2), ("conv", 3), (MIX, 3), (FFN, 3)]
OPERANDS = [((MIX, 0), 8), (("conv", 0), 8), ((FFN, 0), 8), ((MIX, 1), 8), (("ssm", 1), 16), ((FFN, 1), 8), ((MIX, 2), 8),
            (("attn", 2), 8), ((FFN, 2), 8), ((MIX, 3), 8), (("conv", 3), 8), ((FFN, 3), 8)]
X_BASE = {key: sum(n for _, n in OPERANDS[:i]) for i, (key, _) in enumerate(OPERANDS)}


def params():
    at, out = 0, {}
    for name, width in (
        [(f"ln_{w}_{s}{L}", KT) for L in range(DEPTH) for w in ("mix", "ffn") for s in "gb"]
        + [(f"{name}{j}", width) for j in range(2) for name, width in
           (("pw1_b", 2 * KT), ("dw", KT * (TAPS + 1)), ("cn_g", KT), ("cn_b", KT), ("pw2_b", KT))]
        + [("ada_b", DEPTH * 96), ("sconv", 32 * (CW + 1)), ("snorm", 16), ("sskip", 16), ("dt_b", 1), ("a_log", 1),
           ("qk_g", 10), ("eps_ln", 1), ("eps_rms", 1), ("one", 1)]
    ):
        out[name] = (at, width)
        at += width
    return out, at


PAR, NPAR = params()
CST = {"ident": 0, "mask_f": 128, "mask_b": 256, "rot": 384, "headmean": 512, "cos": 640, "sin": 896, "sel": 1152}
NCST = 1154


def program(nc, xT, condT, par_d, cst_d, adaw, wstream, out_d, layers=DEPTH):
    root = ExitStack()
    with root:
        def sb(name, shape, dt=F32, scope=root):
            return scope.enter_context(nc.sbuf_tensor(name, shape, dt))

        def sem(name):
            return root.enter_context(nc.semaphore(name))

        h = sb("h", [P, KT, N])
        xh = sb("xh", [P, KT, N], F32R)
        xl = sb("xl", [P, KT, N], F32R)
        raw = sb("raw", [P, 4, UNIT])
        wh = sb("wh", [P, 2, UNIT], F32R)
        wl = sb("wl", [P, 2, UNIT], F32R)
        par = sb("par_sb", [P, NPAR])
        cst = sb("cst_sb", [P, NCST])
        condraw = sb("condraw", [P, KT, 2])
        cond = sb("cond", [P, KT, 32])
        mod = sb("mod", [P, 2, 96])
        gbias = sb("gbias", [P, KT, 2])
        meanm = sb("meanm", [P, P])
        tmp = sb("tmp", [P, 2, N])
        act_tmp = sb("act_tmp", [P, 2, N])
        rs = sb("rs", [P, N])
        adarow = rs
        credit = sb("credit", [P, 4])
        bank = [root.enter_context(nc.psum_tensor(f"bank{i}", [P, N], F32)) for i in range(8)]

        with ExitStack() as s:
            ada = sb("ada", [P, 2, 4, N], F32, s)
            hidh = sb("hidh", [P, HT * N], F32R, s)
            hidl = sb("hidl", [P, HT * N], F32R, s)
        with ExitStack() as s:
            vbuf = sb("vbuf", [P, 2, 2, VW], F32, s)
            dwc = sb("dwc", [P, 2, TAPS + 1], F32, s)
            cacc = sb("cacc", [P, 2, N], F32, s)
            cz = sb("cz", [P, KT * N], F32, s)

        with ExitStack() as s:
            yall = sb("yall", [P, 16 * N], F32, s)
            with ExitStack() as s2:
                xc = sb("xc", [P, 2, 4, N], F32, s2)
                zs = sb("zs", [P, 2, N], F32, s2)
                xraw = sb("xraw", [P, 4, 2, XW], F32, s2)
                xdt = sb("xdt", [P, 2, NC, HPG * HD], F32, s2)
                xw = sb("xw", [P, NC, HPG * HD], F32, s2)
                btok = sb("btok", [P, NC, P], F32, s2)
                cbm = sb("cbm", [P, 2, N], F32, s2)
                seg = sb("seg", [P, 3, N], F32, s2)
                hst = sb("hst", [P, 2, 3, HPG * HD], F32, s2)
                cum = sb("cum", [P, N], F32, s2)
                tokq = sb("tokq", [P, 4, NC, 64], F32, s2)
                tg = sb("tg", [P, 4 * NC, 2, HPG], F32, s2)
                pick = sb("pick", [P, 2 * HPG, P], F32, s2)
                sconv = sb("sconv_g", [P, 4, CW + 1], F32, s2)
            with ExitStack() as s2:
                x2h = sb("x2h", [P, KT, N], F32R, s2)
                x2l = sb("x2l", [P, KT, N], F32R, s2)
        with ExitStack() as s:
            kv = sb("kv", [P, 4, N], F32, s)
            q = sb("q", [P, 8 * SEG], F32, s)
            vtok = sb("vtok", [P, NC, 4 * HD], F32, s)
            qcur = sb("qcur", [P, 2, SEG], F32, s)
            rtmp = sb("rtmp", [P, 2, 2, N], F32, s)
            prob = sb("prob", [P, 4, N], F32, s)
            pT = sb("pT", [P, 2, N], F32, s)
            rsh = sb("rsh", [P, 2, N], F32, s)
            asm_ = sb("attn_small", [P, 4, 4], F32, s)

        raw_landed = [sem(f"raw_landed{i}") for i in range(4)]
        hi_ready = sem("hi_ready")
        split_ready = sem("split_ready")
        split_free = sem("split_free")
        par_landed = sem("par_landed")
        h_landed = sem("h_landed")
        ada_landed = [sem("ada_landed0"), sem("ada_landed1")]
        ada_used = sem("ada_used")

        ada_row = sem("ada_row")
        ada_col = sem("ada_col")
        mod_ready = sem("mod_ready")
        mod_done = sem("mod_done")
        cleared = sem("cleared")
        cond_ready = sem("cond_ready")
        x_ready = sem("x_ready")
        ah_ready = sem("ah_ready")
        y_done = sem("y_done")
        z_ready = sem("z_ready")
        mean_done = sem("mean_done")
        zc_ready = sem("zc_ready")
        sq_ready = sem("sq_ready")
        sq_used = sem("sq_used")
        rstd_ready = sem("rstd_ready")
        n_ready = sem("n_ready")
        h_ready = sem("h_ready")
        silu_ready = sem("silu_ready")
        pair_free = {L: sem(f"pair_free{L}") for L in range(layers)}
        pair_done = {L: sem(f"pair_done{L}") for L in range(layers)}
        gate_done = {L: sem(f"gate_done{L}") for L in range(layers)}
        hid_ready = {L: sem(f"hid_ready{L}") for L in range(layers)}
        cpair_free = {L: sem(f"cpair_free{L}") for L in CONV_LAYERS}
        cpair_done = {L: sem(f"cpair_done{L}") for L in CONV_LAYERS}
        cgate_done = {L: sem(f"cgate_done{L}") for L in CONV_LAYERS}
        out_landed = sem("out_landed")
        dt_read = sem("dt_read")
        dt_neg = sem("dt_neg")
        dt_log = sem("dt_log")
        a_ready = sem("a_ready")
        cum_ready = sem("cum_ready")
        w_ready = sem("w_ready")
        rows_ready = sem("rows_ready")
        toks_done = sem("toks_done")
        tot_ready = sem("tot_ready")
        proj_read = sem("proj_read")
        conv_done = sem("conv_done")
        xc_ready = sem("xc_ready")
        bt_done = sem("bt_done")
        xt_done = sem("xt_done")
        cb_done = sem("cb_done")
        cb_read = sem("cb_read")
        xw_ready = sem("xw_ready")
        st_done = sem("st_done")
        st_read = sem("st_read")
        pick_ready = sem("pick_ready")
        r_done = sem("r_done")
        seg_ready = sem("seg_ready")
        seg_exp = sem("seg_exp")
        e_ready = sem("e_ready")
        m_ready = sem("m_ready")
        ce_ready = sem("ce_ready")
        yh_done = sem("yh_done")
        yg_ready = sem("yg_ready")
        gsq_ready = sem("gsq_ready")
        gsq_used = sem("gsq_used")
        grs_ready = sem("grs_ready")
        grs_used = sem("grs_used")
        qkv_free = sem("qkv_free")
        qkv_done = sem("qkv_done")
        vt_done = sem("vt_done")
        vt_read = sem("vt_read")
        hsq_ready = sem("hsq_ready")
        hms_done = sem("hms_done")
        hrs_ready = sem("hrs_ready")
        hn_ready = sem("hn_ready")
        rot_done = sem("rot_done")
        rope_done = sem("rope_done")
        q_ready = sem("q_ready")
        sc_done = sem("sc_done")
        mx_ready = sem("mx_ready")
        ex_ready = sem("ex_ready")
        pr_ready = sem("pr_ready")
        ptr_done = sem("ptr_done")
        pt_ready = sem("pt_ready")
        pv_done = sem("pv_done")

        STATES = ((6, 0), (6, 1), (7, 0), (3, 0), (3, 1), (7, 1))

        def unit_done(n):
            return 2 + n + 1

        def segs(L):
            return (0, 1) if L < ATTN_LAYER else (1,)

        def first(L):
            return segs(L)[0] * SEG

        def tok(L):
            return slice(first(L), N)

        WIDE = ffn_base(ATTN_LAYER)

        def ring(n):
            return 2 if n < WIDE else 4

        def split_slot(n):
            u = (n - WIDE) % 4
            if n < WIDE or u < 2:
                return wh[:, n % 2, :], wl[:, n % 2, :]
            at = HT * SEG + (u - 2) * UNIT
            return hidh[:, at:at + UNIT], hidl[:, at:at + UNIT]

        def col(name, k, width=1):
            at = PAR[name][0]
            return par[:, at + k:at + k + width]

        def modc(L, m, k, c):
            at = (m * KT + k) * 2 + c
            return mod[:, L % 2, at:at + 1]

        def half(a):
            return a.rearrange("p (s t) -> p s t", s=2)

        def lname(which):
            return ("mix", "ffn")[which]

        used = sum(mix_base(1) if L == 0 else MIXER_UNITS[L] + FFN_UNITS for L in range(layers))
        block = root.enter_context(nc.Block())

        @block.sync
        def _(sp):
            sp.dma_start(par[:, :], par_d).then_inc(par_landed, 16)
            sp.dma_start(condraw[:, :, :], condT).then_inc(par_landed, 16)
            sp.dma_start(cst[:, :], cst_d).then_inc(par_landed, 16)
            sp.dma_start(h[:, :, :], xT).then_inc(h_landed, 16)

            def load(n, slot, split=None):
                if split is not None:
                    sp.wait_ge(split_ready, split)
                sp.dma_start(raw[:, slot, :], wstream[n, :, :]).then_inc(raw_landed[slot], 16)

            for slot in range(4):
                load(slot, slot)
            whole = used - used % 4
            with sp.Fori(1, whole // 4) as i:
                for slot in range(4):
                    load(i * 4 + slot, slot, i * 4 + (slot - 3))
            for n in range(whole, used):
                load(n, n % 4, n - 3)
            for k in range(KT):
                sp.wait_ge(h_ready, KT * (2 * layers - 1) + k + 1)
                if layers == DEPTH:
                    sp.dma_start(out_d[:, k, :], h[:, k, SEG:N]).then_inc(out_landed, 16)
                else:
                    sp.dma_start(out_d[:, k, :], h[:, k, :]).then_inc(out_landed, 16)
            sp.wait_ge(out_landed, 16 * KT)

        @block.gpsimd
        def _(pool):
            pool.memset(credit[:, 0:1], 0.0).then_inc(split_free, 2)

            def low_part(base, g=0):
                hi, lo = split_slot(base)
                pool.wait_ge(hi_ready, g * 4 + base + 1)
                pool.tensor_tensor(lo, raw[:, base % 4, :], hi.bitcast(F32), ALU.subtract).then_inc(split_ready, 1)

            for a, b in ((0, min(WIDE, used)), (WIDE, used)):
                if b - a >= 8:
                    with pool.Fori(0, (b - a) // 4) as i:
                        for c in range(4):
                            low_part(a + c, i)
                    a += (b - a) // 4 * 4
                for n in range(a, b):
                    low_part(n)

        @block.scalar
        def _(act):
            def load_ada(c, slot, used_before):
                if used_before is not None:
                    act.wait_ge(ada_used, used_before)
                act.dma_start(ada[:, slot, :, :], adaw[c, :, slot * 4:slot * 4 + 4, :]).then_inc(ada_landed[slot], 16)

            def high_part(base, g=0, stride=4):
                hi, _ = split_slot(base)
                n = g * stride + base
                act.wait_ge(raw_landed[base % 4], g * (4 * stride) + 16 * (base // 4 + 1))
                back = 2 if base < WIDE + 2 else 4
                act.wait_ge(split_free, n + (3 - back))
                act.activation(hi, raw[:, base % 4, :], ACT.Copy).then_inc(hi_ready, 1)

            def high_parts(a, b):
                b = min(b, used)
                for a, b in ((a, min(b, WIDE)), (max(a, WIDE), b)):
                    if b - a >= 8:
                        with act.Fori(0, (b - a) // 4) as i:
                            for c in range(4):
                                high_part(a + c, i)
                        a += (b - a) // 4 * 4
                    for n in range(a, b):
                        high_part(n)

            def residual(L, which):
                biased = which == MIX and L in CONV_LAYERS
                for k in range(KT):
                    act.wait_ge(x_ready, X_BASE[which, L] + k + 1)
                    for c in segs(L):
                        t = slice(c * SEG, (c + 1) * SEG)
                        if biased:
                            ins = act.activation(h[:, k, t], h[:, k, t], ACT.Identity, scale=ALPHA,
                                                 bias=gbias[:, k, c:c + 1])
                        else:
                            ins = act.activation(h[:, k, t], h[:, k, t], ACT.Copy, scale=ALPHA)
                    ins.then_inc(ah_ready, 1)

            def norm_scale(kind, L, src):
                li = NORMS.index((kind, L))
                act.preload_act_table_set("natural_log_exp_and_others")
                for m in range(KT):
                    act.wait_ge(zc_ready, KT * li + m + 1)
                    if m >= 2:
                        act.wait_ge(sq_used, KT * li + m - 1)
                    act.activation(act_tmp[:, m % 2, tok(L)], src(m), ACT.Square).then_inc(sq_ready, 1)
                act.wait_ge(sq_used, KT * li + KT)
                act.activation(rs[:, tok(L)], bank[1][:, tok(L)], ACT.Ln, bias=col("eps_ln", 0))
                act.drain()
                act.activation(rs[:, tok(L)], rs[:, tok(L)], ACT.Exp, scale=-0.5).then_inc(rstd_ready, 1)

            def norm_bias(kind, L):
                li = NORMS.index((kind, L))
                for m in range(KT):
                    act.wait_ge(n_ready, KT * li + m + 1)
                    act.activation(h[:, m, tok(L)], h[:, m, tok(L)], ACT.Identity,
                                   bias=col(f"ln_{lname(kind)}_b{L}", m)).then_inc(h_ready, 1)

            def conv_mixer(L):
                j = CONV_LAYERS.index(L)
                act.preload_act_table_set("sigmoid_and_others")
                with act.Fori(0, 4) as g:
                    for c in range(3):
                        high_part(mix_base(L) + ring(mix_base(L)) + c, g)
                    for p in range(2):
                        if p == 0:
                            act.wait_ge(cpair_done[L], g + 1)
                        else:
                            act.wait_ge(split_free, unit_done(mix_base(L) + g * 4 + 3))
                        act.wait_ge(cpair_free[L], g * 2 + p + 1)
                        act.activation(act_tmp[:, p, tok(L)], bank[2 * p + 1][:, tok(L)], ACT.Sigmoid,
                                       bias=par[:, bass.ds(g * 2 + (PAR[f"pw1_b{j}"][0] + KT + p), 1)]
                                       ).then_inc(cgate_done[L], 1)
                    high_part(mix_base(L) + ring(mix_base(L)) + 3, g)
                norm_scale("conv", L, lambda m: cz[:, m * N + first(L):(m + 1) * N])
                act.preload_act_table_set("silu_and_others")
                for m in range(KT):
                    act.wait_ge(n_ready, KT * NORMS.index(("conv", L)) + m + 1)
                    z = cz[:, m * N + first(L):(m + 1) * N]
                    act.activation(z, z, ACT.Silu, bias=col(f"cn_b{j}", m)).then_inc(silu_ready, 1)
                high_parts(mix_base(L) + 16 + ring(mix_base(L)), ffn_base(L) + ring(ffn_base(L)))

            def ffn(L):
                act.preload_act_table_set("silu_and_others")
                lead = ring(ffn_base(L))
                if L + 1 < layers:
                    c0 = CHUNKS * (L + 1)
                    act.wait_ge(x_ready, X_BASE[FFN, L] + 1)
                    load_ada(c0, 0, None)
                    load_ada(c0, 1, None)
                with act.Fori(0, FG) as g:
                    for c in range(2):
                        high_part(ffn_base(L) + lead + c, g)
                    if L + 1 < layers:
                        load_ada(g + (c0 + 1), 0, g * 2 + (2 * c0 + 1))
                        load_ada(g + (c0 + 1), 1, g * 2 + (2 * c0 + 2))
                    high_part(ffn_base(L) + lead + 2, g)
                    for p in range(2):
                        if p == 0:
                            act.wait_ge(pair_done[L], g + 1)
                        else:
                            act.wait_ge(split_free, unit_done(ffn_base(L) + g * 4 + 3))
                        act.wait_ge(pair_free[L], g * 2 + p + 1)
                        act.activation(act_tmp[:, p, tok(L)], bank[2 * p][:, tok(L)], ACT.Silu
                                       ).then_inc(gate_done[L], 1)
                    high_part(ffn_base(L) + lead + 3, g)
                high_parts(ffn_base(L) + 4 * FG + lead, ffn_base(L) + FFN_UNITS + lead)

            def ssm_project(q, role):
                n = mix_base(SSM_LAYER) + q
                act.wait_ge(split_free, unit_done(n))
                if role < 2:
                    act.activation(zs[:, role, :], bank[role][:, :], ACT.Silu).then_inc(proj_read, 1)
                else:
                    r = role - 2
                    act.activation(xraw[:, r, :, 2:2 + SEG], half(bank[r % 2][:, :]), ACT.Copy).then_inc(proj_read, 1)

            def ssm_silu(g, par, r):
                act.wait_ge(conv_done, g * 4 + r + 1)
                act.activation(xc[:, par, r, :], tmp[:, r % 2, :], ACT.Silu).then_inc(xc_ready, 1)

            def ssm_group(it, gg):
                g = it * 2 + gg
                last = isinstance(it, int) and gg == 1
                base = mix_base(SSM_LAYER) + 7 + 6 * gg

                def decay(n):
                    act.wait_ge(seg_ready, g * 8 + n + 1)
                    act.activation(seg[:, n % 3, :], seg[:, n % 3, :], ACT.Exp).then_inc(seg_exp, 1)
                    if n >= 2:
                        act.wait_ge(yh_done, g * 8 + n - 1)
                    act.activation(act_tmp[:, n % 2, :], bank[(2, 4, 5)[n % 3]][:, :], ACT.Exp).then_inc(e_ready, 1)

                def unit(r):
                    ssm_project(it * 12 + (5 + 6 * gg + r), r)
                    high_part(base + r, it, 12)

                decay(0)
                decay(1)
                unit(0)
                unit(1)
                decay(2)
                decay(3)
                if not last:
                    unit(2)
                decay(4)
                decay(5)
                if not last:
                    unit(3)
                    ssm_silu(g + 1, 1 - gg, 0)
                    ssm_silu(g + 1, 1 - gg, 1)
                decay(6)
                decay(7)
                if not last:
                    unit(4)
                    unit(5)
                    ssm_silu(g + 1, 1 - gg, 2)
                    ssm_silu(g + 1, 1 - gg, 3)

            def ssm_mixer():
                b = mix_base(SSM_LAYER)
                t = lambda i: yall[0:64, i * N:(i + 1) * N]
                act.wait_ge(dt_neg, 1)
                act.activation(t(2), t(1), ACT.Exp)
                act.drain()
                act.activation(t(3), t(2), ACT.Ln, bias=col("one", 0)[0:64, :]).then_inc(dt_log, 1)
                act.activation(t(9)[:, 0:1], col("a_log", 0)[0:64, :], ACT.Exp).then_inc(a_ready, 1)
                high_part(b + 2)
                for q in range(1, 5):
                    ssm_project(q, q + 1)
                    high_part(b + q + 2)
                act.wait_ge(cum_ready, 1)
                for c in range(NC):
                    cols = slice(c * CH, (c + 1) * CH)
                    for rows, end in ((slice(0, 32), (c + 1) * CH - 1), (slice(32, 64), c * CH)):
                        ins = act.activation(t(7)[rows, cols], cum[rows, cols], ACT.Exp, scale=-1.0,
                                             bias=cum[rows, end:end + 1])
                ins.then_inc(w_ready, 1)
                act.wait_ge(tot_ready, 1)
                act.activation(tokq[:, 3, :, :], bank[3][:, 256:512].rearrange("p (c h) -> p c h", c=NC), ACT.Exp
                               ).then_inc(tot_ready, 1)
                for r in range(4):
                    ssm_silu(0, 0, r)
                act.preload_act_table_set("natural_log_exp_and_others")
                with act.Fori(0, GROUPS // 2 - 1) as it:
                    ssm_group(it, 0)
                    ssm_group(it, 1)
                ssm_group(GROUPS // 2 - 1, 0)
                ssm_group(GROUPS // 2 - 1, 1)
                act.preload_act_table_set("natural_log_exp_and_others")
                act.wait_ge(yg_ready, 2 * GROUPS)
                for g in range(GROUPS):
                    for e in range(2):
                        if g:
                            act.wait_ge(gsq_used, g)
                        act.activation(act_tmp[:, e, :], yall[:, (2 * g + e) * N:(2 * g + e + 1) * N], ACT.Square
                                       ).then_inc(gsq_ready, 1)
                    act.wait_ge(gsq_used, g + 1)
                    if g:
                        act.wait_ge(grs_used, g)
                    act.activation(rs[:, :], bank[4 + g % 2][:, :], ACT.Ln, scale=4.0, bias=col("eps_rms", 0))
                    act.drain()
                    act.activation(rs[:, :], rs[:, :], ACT.Exp, scale=-0.5).then_inc(grs_ready, 1)
                    if g:
                        high_part(b + 50 + g)
                high_parts(b + 58, b + 67)

            def attn_mixer():
                b = mix_base(ATTN_LAYER)
                act.preload_act_table_set("natural_log_exp_and_others")
                act.activation(credit[:, 3:4], col("one", 0), ACT.Copy).then_inc(qkv_free, 4)

                def copy_out(g, i, to):
                    for c in range(3):
                        high_part(b + 2 + c, g)
                    for t in range(4):
                        if t < 3:
                            act.wait_ge(qkv_done, g * 3 + t + 1)
                        else:
                            act.wait_ge(split_free, unit_done(b + g * 4 + 3))
                        dst, src = to(i, t)
                        act.activation(dst, src, ACT.Copy).then_inc(qkv_free, 1)
                    high_part(b + 5, g)

                copy_out(0, 0, lambda i, t: (kv[:, t, :], bank[t][:, :]))
                with act.Fori(0, 2) as i:
                    copy_out(i + 1, i, lambda i, t: (q[:, bass.ds(i * (4 * SEG) + t * SEG, SEG)], bank[t][:, SEG:N]))

                def head_scales(c0, src):
                    for e in range(2):
                        act.activation(act_tmp[:, e, :], src(e), ACT.Square).then_inc(hsq_ready, 1)
                    for e in range(2):
                        act.wait_ge(hms_done, c0 + e + 1)
                        act.activation(rsh[:, e, :], bank[4 + e][:, :], ACT.Ln, bias=col("eps_rms", 0))
                    act.drain()
                    for e in range(2):
                        act.activation(rsh[:, e, :], rsh[:, e, :], ACT.Exp, scale=-0.5).then_inc(hrs_ready, 1)
                    act.wait_ge(hn_ready, c0 + 2)

                head_scales(0, lambda e: kv[:, 2 + e, :])
                with act.Fori(0, 2) as i:
                    head_scales(i * 2 + 2, lambda e: q[:, bass.ds(i * (4 * SEG) + e * N, N)])

                def numerators(t, s):
                    act.wait_ge(mx_ready, t + 1)
                    act.activation(prob[:, s % 4, :], bank[s % 4][:, :], ACT.Exp, scale=0.125,
                                   bias=asm_[:, s % 4, 1:2], accum_out=asm_[:, s % 4, 2:3]).then_inc(ex_ready, 1)

                def steps(it, last):
                    for s in range(8):
                        if not (last and s == 7):
                            numerators(it * 8 + s + 1, s + 1)
                        act.wait_ge(ptr_done, it * 8 + s + 1)
                        act.activation(pT[:, s % 2, :], bank[4 + s % 2][:, :], ACT.Copy).then_inc(pt_ready, 1)

                numerators(0, 0)
                with act.Fori(0, 3) as it:
                    steps(it, False)
                steps(3, True)
                high_parts(b + 14, ffn_base(ATTN_LAYER) + ring(ffn_base(ATTN_LAYER)))

            act.wait_ge(par_landed, 48)
            act.wait_ge(cleared, 1)
            for slot in range(2):
                load_ada(0, slot, None)
            act.activation(cond[:, :, 0:2], condraw[:, :, :], ACT.Silu).then_inc(cond_ready, 1)
            with act.Fori(0, CHUNKS - 1) as c:
                load_ada(c + 1, 0, c * 2 + 1)
                load_ada(c + 1, 1, c * 2 + 2)
            high_parts(0, 2)
            for L in range(layers):
                residual(L, MIX)
                if L in CONV_LAYERS:
                    conv_mixer(L)
                elif L == SSM_LAYER:
                    ssm_mixer()
                else:
                    attn_mixer()
                norm_scale(MIX, L, lambda m: h[:, m, tok(L)])
                norm_bias(MIX, L)
                residual(L, FFN)
                ffn(L)
                norm_scale(FFN, L, lambda m: h[:, m, tok(L)])
                norm_bias(FFN, L)

        @block.tensor
        def _(pe):
            def four_tiles(n, like, xk, banks, cols, start, last=False, tile_done=(), before=None):
                whi, wlo = split_slot(like)
                pe.wait_ge(split_ready, n + 1)
                for t in range(4):
                    if before is not None:
                        before(t)
                    for kk in range(2):
                        w = slice((kk * 4 + t) * P, (kk * 4 + t + 1) * P)
                        hi, lo = xk[kk]
                        for i, (a, b) in enumerate(((whi, hi), (wlo, hi), (whi, lo))):
                            mm = pe.matmul(banks[t][:, cols], a[:, w], b, start=start and kk == 0 and i == 0,
                                           stop=last and kk == 1 and i == 2)
                    if t == 3:
                        mm.then_inc(split_free, 1)
                    elif last and tile_done and tile_done[t] is not None:
                        mm.then_inc(tile_done[t], 1)

            def x_tiles(cols, ku):
                return [(xh[:, 2 * ku + kk, cols], xl[:, 2 * ku + kk, cols]) for kk in range(2)]

            def out_product(n0, L, operand):
                for s in range(2):
                    for ku in range(4):
                        n = n0 + 4 * s + ku
                        pe.wait_ge(x_ready, X_BASE[operand, L] + (KT if operand == "attn" else 2 * ku + 2))
                        four_tiles(n, n, x_tiles(tok(L), ku), bank[4 * s:4 * s + 4], tok(L), ku == 0, ku == 3,
                                   [y_done] * 3)

            def norm_sums(kind, L, src):
                li = NORMS.index((kind, L))
                for m in range(KT):
                    pe.wait_ge(z_ready, KT * li + m + 1)
                    mm = pe.matmul(bank[0][:, tok(L)], meanm[:, :], src(m), start=m == 0, stop=m == KT - 1)
                mm.then_inc(mean_done, 1)
                for m in range(KT):
                    pe.wait_ge(sq_ready, KT * li + m + 1)
                    pe.matmul(bank[1][:, tok(L)], meanm[:, :], act_tmp[:, m % 2, tok(L)], start=m == 0,
                              stop=m == KT - 1).then_inc(sq_used, 1)

            def ada_rows(c):
                for s in range(2):
                    pe.wait_ge(ada_landed[s], 16 * (c + 1))
                    for k in range(4):
                        mm = pe.matmul(bank[4][32 * k:32 * k + 32, :], cond[:, 4 * s + k, :], ada[:, s, k, :],
                                       start=s == 0, stop=s == 1)
                    mm.then_inc(ada_used, 1)

            def ada_columns(c):
                pe.wait_ge(ada_row, c + 1)
                for q in range(4):
                    mm = pe.matmul(bank[5][:, 2 * q:2 * q + 2], adarow[:, q * P:(q + 1) * P],
                                   cst[:, CST["sel"]:CST["sel"] + 2], start=True, stop=True)
                mm.then_inc(ada_col, 1)

            def conv_mixer(L):
                def before(t):
                    if t % 2 == 0:
                        pe.wait_ge(cpair_free[L], g * 2 + t // 2 + 1)
                with pe.Fori(0, 4) as g:
                    for ku in range(4):
                        pe.wait_ge(x_ready, X_BASE[MIX, L] + 2 * ku + 2)
                        four_tiles(g * 4 + (mix_base(L) + ku), mix_base(L) + ku, x_tiles(tok(L), ku), bank[0:4], tok(L),
                                   ku == 0, ku == 3, [None, cpair_done[L], None], before if ku == 0 else None)
                pe.wait_ge(cpair_free[L], 2 + KT)
                norm_sums("conv", L, lambda m: cz[:, m * N + first(L):(m + 1) * N])
                out_product(mix_base(L) + 16, L, "conv")

            def ffn(L):
                def before(t):
                    if t % 2 == 0:
                        pe.wait_ge(pair_free[L], g * 2 + t // 2 + 1)
                with pe.Fori(0, FG) as g:
                    for ku in range(4):
                        pe.wait_ge(x_ready, X_BASE[FFN, L] + 2 * ku + 2)
                        four_tiles(g * 4 + (ffn_base(L) + ku), ffn_base(L) + ku, x_tiles(tok(L), ku), bank[0:4], tok(L),
                                   ku == 0, ku == 3, [None, pair_done[L], None], before if ku == 0 else None)
                        if L + 1 < layers and ku == 1:
                            ada_rows(g + CHUNKS * (L + 1))
                        if L + 1 < layers and ku == 2:
                            ada_columns(g + CHUNKS * (L + 1))
                if L + 1 < layers:
                    ada_rows(CHUNKS * (L + 1) + FG)
                    ada_columns(CHUNKS * (L + 1) + FG)
                n0 = ffn_base(L) + 4 * FG

                def hid(k):
                    at = bass.ds(k * (N - first(L)), N - first(L))
                    return hidh[:, at], hidl[:, at]

                pe.wait_ge(pair_free[L], 2 + HT)
                for s in range(2):
                    if s == 1 and L + 1 < layers:
                        pe.wait_ge(mod_ready, CHUNKS * (L + 2))
                    banks = bank[4 * s:4 * s + 4]

                    def unit(ku, j, start, last):
                        four_tiles(n0 + FG * s + ku, n0 + FG * s + j, [hid(ku * 2), hid(ku * 2 + 1)], banks, tok(L),
                                   start, last, [y_done] * 3)
                    pe.wait_ge(hid_ready[L], HT - 2)
                    unit(0, 0, True, False)
                    with pe.Fori(0, (FG - 3) // 4) as i:
                        for j in range(1, 5):
                            unit(i * 4 + j, j, False, False)
                    for j in range(1 + (FG - 3) // 4 * 4, FG - 1):
                        unit(j, j, False, False)
                    pe.wait_ge(hid_ready[L], HT)
                    unit(FG - 1, FG - 1, False, True)

            def one_tile(q, slot, to):
                n = q + mix_base(SSM_LAYER)
                pe.wait_ge(split_ready, n + 1)
                for k in range(KT):
                    w = slice(k * P, (k + 1) * P)
                    for i, (a, b) in enumerate(((wh, xh), (wl, xh), (wh, xl))):
                        mm = pe.matmul(to[:, :], a[:, slot, w], b[:, k, :], start=k == 0 and i == 0,
                                       stop=k == KT - 1 and i == 2)
                mm.then_inc(split_free, 1)

            ORDER = ((0, 1, 2, 3), (1, 0, 3, 2))

            def ssm_group(it, gg):
                g = it * 2 + gg
                last = isinstance(it, int) and gg == 1
                B, C, x0 = xc[:, gg, 0, :], xc[:, gg, 1, :], xc[:, gg, 2:4, :]
                ch = lambda c: slice(c * CH, (c + 1) * CH)
                ident = cst[:, 0:P]

                def unit(r):
                    q = it * 12 + (5 + 6 * gg + r)
                    pe.wait_ge(proj_read, it * 12 + (3 + 6 * gg + r))
                    one_tile(q, (mix_base(SSM_LAYER) + 5 + 6 * gg + r) % 2, bank[r % 2])

                def broadcast(n):
                    if n >= 3:
                        pe.wait_ge(seg_ready, g * 8 + n - 2)
                        pe.wait_ge(e_ready, g * 8 + n - 2)
                    pe.matmul(bank[(2, 4, 5)[n % 3]][:, :], pick[0:64, (n % 2) * HPG + n // 2, :], cum[0:64, :],
                              start=True, stop=True).then_inc(r_done, 1)

                def head(n):
                    r, d = divmod(n, 2)
                    pe.wait_ge(m_ready, g * 8 + n + 1)
                    pe.wait_ge(ce_ready, g * 8 + n + 1)
                    if n == 0:
                        pe.wait_ge(st_read, g * 2 + 2)
                    y = bank[6 + r // 2][64 * (r % 2):64 * (r % 2) + 64, :]
                    f = slice(r * HD, (r + 1) * HD)
                    for c in range(NC):
                        mm = pe.matmul(y[:, ch(c)], xdt[:, d, c, f], seg[:, n % 3, ch(c)], start=d == 0 and c == 0,
                                       stop=d == 1 and c == ORDER[1][0], skip_group_check=True)
                        at = ORDER[d].index(c)
                        if at:
                            mm = pe.matmul(y[:, ch(c)], hst[:, d, at - 1, f], act_tmp[:, n % 2, ch(c)], start=False,
                                           stop=d == 1, skip_group_check=True)
                    mm.then_inc(yh_done, 1)

                pe.wait_ge(xc_ready, g * 4 + 4)
                for c in range(NC):
                    mm = pe.transpose(bank[2][:, ch(c)], B[:, ch(c)], ident)
                mm.then_inc(bt_done, 1)
                for c in range(NC):
                    for t in range(2):
                        at = (c % 2) * 2 * P + t * P
                        mm = pe.transpose(bank[4 + c // 2][:, at:at + P], x0[:, t, ch(c)], ident)
                mm.then_inc(xt_done, 1)
                for c in range(NC):
                    mm = pe.matmul(bank[3][:, ch(c)], B[:, ch(c)], C[:, ch(c)], start=True, stop=True)
                mm.then_inc(cb_done, 1)
                pe.wait_ge(cb_read, g + 1)
                for d in range(2):
                    pe.wait_ge(xw_ready, g * 2 + d + 1)
                    for i in range(3):
                        to, at = STATES[3 * d + i]
                        mm = pe.matmul(bank[to][:, at * 256:at * 256 + 256], btok[:, ORDER[d][i], :],
                                       xw[:, ORDER[d][i], :], start=True, stop=True)
                    mm.then_inc(st_done, 1)
                pe.wait_ge(pick_ready, g + 1)
                broadcast(0)
                broadcast(1)
                broadcast(2)
                unit(0)
                unit(1)
                head(0)
                broadcast(3)
                head(1)
                broadcast(4)
                if not last:
                    unit(2)
                head(2)
                broadcast(5)
                head(3)
                broadcast(6)
                if not last:
                    unit(3)
                head(4)
                broadcast(7)
                head(5)
                if not last:
                    unit(4)
                head(6)
                head(7)
                if not last:
                    unit(5)

            def ssm_mixer():
                t = lambda i: yall[0:64, i * N:(i + 1) * N]
                for k in range(KT):
                    pe.wait_ge(x_ready, X_BASE[MIX, SSM_LAYER] + k + 1)
                for q in range(5):
                    if q == 2:
                        pe.wait_ge(dt_read, 1)
                    if q > 2:
                        pe.wait_ge(proj_read, q - 2)
                    one_tile(q, (mix_base(SSM_LAYER) + q) % 2, bank[(q + 1) % 2])
                pe.wait_ge(rows_ready, 1)
                for q, src in enumerate((cum[0:64, :], t(0), t(7))):
                    for c in range(NC):
                        at = (q % 2) * 256 + c * 64
                        pe.transpose(bank[2 + q // 2][:, at:at + 64], src[:, c * CH:(c + 1) * CH], cst[0:64, 0:64])
                pe.matmul(bank[3][:, 256:512], t(8)[:, 0:P], t(10)[:, 0:256], start=True, stop=True
                          ).then_inc(toks_done, 1)
                pe.wait_ge(tot_ready, 2)
                with pe.Fori(0, GROUPS // 2 - 1) as it:
                    ssm_group(it, 0)
                    ssm_group(it, 1)
                ssm_group(GROUPS // 2 - 1, 0)
                ssm_group(GROUPS // 2 - 1, 1)
                n0 = mix_base(SSM_LAYER) + 49

                def x16(k):
                    a, b = (xh, xl) if k < KT else (x2h, x2l)
                    return a[:, k % KT, :], b[:, k % KT, :]

                def group_square(g):
                    pe.wait_ge(gsq_ready, 2 * g + 2)
                    if g >= 2:
                        pe.wait_ge(grs_ready, g - 1)
                    for e in range(2):
                        mm = pe.matmul(bank[4 + g % 2][:, :], meanm[:, :], act_tmp[:, e, :], start=e == 0, stop=e == 1)
                    mm.then_inc(gsq_used, 1)

                group_square(0)
                for s in range(2):
                    for ku in range(8):
                        if s == 0 and ku + 1 < GROUPS:
                            group_square(ku + 1)
                        pe.wait_ge(x_ready, X_BASE["ssm", SSM_LAYER] + 2 * ku + 2)
                        n = n0 + 8 * s + ku
                        four_tiles(n, n, [x16(2 * ku), x16(2 * ku + 1)], bank[4 * s:4 * s + 4], tok(SSM_LAYER), ku == 0,
                                   ku == 7, [y_done] * 3)

            def attn_mixer():
                L = ATTN_LAYER
                b = mix_base(L)

                def group(g, cols):
                    def before(t):
                        pe.wait_ge(qkv_free, g * 4 + t + 1)
                    for ku in range(4):
                        pe.wait_ge(x_ready, X_BASE[MIX, L] + 2 * ku + 2)
                        four_tiles(g * 4 + (b + ku), b + ku, x_tiles(cols, ku), bank[0:4], cols, ku == 0, ku == 3,
                                   [qkv_done] * 3, before if ku == 0 else None)

                group(0, slice(0, N))
                with pe.Fori(0, 2) as i:
                    group(i + 1, slice(SEG, N))
                pe.wait_ge(qkv_free, 16)
                for c in range(NC):
                    for t in range(2):
                        at = (c % 2) * 2 * P + t * P
                        mm = pe.transpose(bank[6 + c // 2][:, at:at + P], kv[:, t, c * CH:(c + 1) * CH], cst[:, 0:P])
                mm.then_inc(vt_done, 1)
                pe.wait_ge(vt_read, 1)

                def head_products(c0, rotated, cols):
                    for e in range(2):
                        pe.wait_ge(hsq_ready, c0 + e + 1)
                        pe.matmul(bank[4 + e][:, :], cst[:, CST["headmean"]:CST["headmean"] + P], act_tmp[:, e, :],
                                  start=True, stop=True).then_inc(hms_done, 1)
                    for e in range(2):
                        pe.wait_ge(hn_ready, c0 + e + 1)
                        pe.matmul(bank[6 + e][:, cols], cst[:, CST["rot"]:CST["rot"] + P], rotated(e),
                                  start=True, stop=True).then_inc(rot_done, 1)

                head_products(0, lambda e: kv[:, 2 + e, SEG:N], slice(SEG, N))
                with pe.Fori(0, 2) as i:
                    head_products(i * 2 + 2, lambda e: q[:, bass.ds(i * (4 * SEG) + e * N, N)], slice(0, N))
                pe.wait_ge(rope_done, 6)

                def scores(it, s):
                    a, e, qt = s // 4, s // 2 % 2, s % 2
                    rows = slice(64 * e, 64 * e + 64)
                    if s % 4 == 0:
                        pe.wait_ge(q_ready, it * 2 + a + 1)
                    pe.matmul(bank[s % 4][:, :], qcur[rows, a, qt * CH:(qt + 1) * CH], kv[rows, 2 + a, :],
                              start=True, stop=True).then_inc(sc_done, 1)

                def steps(it, last):
                    for s in range(9):
                        t = it * 8 + s
                        if s < 8 and not (last and s >= 5):
                            if s:
                                pe.wait_ge(ex_ready, t)
                            scores(it + (s + 3) // 8, (s + 3) % 8)
                        if s < 8:
                            pe.wait_ge(pr_ready, t + 1)
                            for c in range(NC):
                                mm = pe.transpose(bank[4 + s % 2][:, c * CH:(c + 1) * CH],
                                                  prob[:, s % 4, c * CH:(c + 1) * CH], cst[:, 0:P])
                            mm.then_inc(ptr_done, 1)
                        if s:
                            a, e, qt = (s - 1) // 4, (s - 1) // 2 % 2, (s - 1) % 2
                            v = slice((2 * a + e) * HD, (2 * a + e + 1) * HD)
                            if (s - 1) % 4 == 0:
                                pe.wait_ge(x_ready, it * 2 + (X_BASE["attn", L] + a - 1))
                            pe.wait_ge(pt_ready, t)
                            for c in range(NC):
                                mm = pe.matmul(bank[6 + a][64 * e:64 * e + 64, qt * CH:(qt + 1) * CH], vtok[:, c, v],
                                               pT[:, (s - 1) % 2, c * CH:(c + 1) * CH], start=c == 0, stop=c == NC - 1)
                            mm.then_inc(pv_done, 1)
                for s in range(3):
                    scores(0, s)
                with pe.Fori(0, 3) as it:
                    steps(it, False)
                steps(3, True)
                out_product(b + 12, L, "attn")

            pe.wait_ge(cond_ready, 1)
            pe.wait_ge(par_landed, 48)
            with pe.Fori(0, CHUNKS) as c:
                ada_rows(c)
                ada_columns(c)
            for L in range(layers):
                if L in CONV_LAYERS:
                    conv_mixer(L)
                elif L == SSM_LAYER:
                    ssm_mixer()
                else:
                    attn_mixer()
                norm_sums(MIX, L, lambda m: h[:, m, tok(L)])
                ffn(L)
                norm_sums(FFN, L, lambda m: h[:, m, tok(L)])

        @block.vector
        def _(dve):
            def ada_to_sbuf(c):
                dve.wait_ge(ada_used, c * 2 + 2)
                dve.tensor_copy(adarow[:, :], bank[4][:, :]).then_inc(ada_row, 1)

            def ada_to_mod(c, chunk, L):
                dve.wait_ge(ada_col, c + 1)
                dve.tensor_tensor(mod[:, L % 2, bass.ds(chunk * 8, 8)], bank[5][:, 0:8],
                                  par[:, bass.ds(chunk * 8 + (PAR["ada_b"][0] + 96 * L), 8)], ALU.add
                                  ).then_inc(mod_ready, 1)

            def finish_mod(L):
                dve.drain()
                for m in (1, 4):
                    s = mod[:, L % 2, m * 16:m * 16 + 16]
                    last = dve.tensor_scalar(s, s, 1.0, None, ALU.add)
                if L in CONV_LAYERS:
                    gate = mod[:, L % 2, 32:48].rearrange("p (k c) -> p k c", c=2)
                    b = col(f"pw2_b{CONV_LAYERS.index(L)}", 0, KT)
                    for c in range(2):
                        dve.tensor_tensor(gbias[:, :, c], gate[:, :, c], b, ALU.mult)
                dve.drain()

            def modulate(L, which, k):
                if (which, L) == (MIX, 0):
                    dve.wait_ge(h_landed, 16)
                else:
                    dve.wait_ge(h_ready, KT * (2 * L + which - 1) + k + 1)
                both = (which, L) == (MIX, ATTN_LAYER)
                for c in (0, 1) if both else segs(L):
                    t = slice(c * SEG, (c + 1) * SEG)
                    sc, sh = modc(L, 3 * which + 1, k, c), modc(L, 3 * which, k, c)
                    dve.tensor_scalar(xh[:, k, t], h[:, k, t], sc, sh, ALU.mult, ALU.add)
                    dve.tensor_scalar(tmp[:, k % 2, t], h[:, k, t], sc, sh, ALU.mult, ALU.add)
                dve.drain()
                t = slice(0, N) if both else tok(L)
                dve.tensor_tensor(xl[:, k, t], tmp[:, k % 2, t], xh[:, k, t].bitcast(F32), ALU.subtract
                                  ).then_inc(x_ready, 1)

            def residual_sum(L, which, n_sweep):
                dve.wait_ge(ah_ready, KT * (2 * L + which) + KT)
                for m in range(KT):
                    s, t = divmod(m, 4)
                    if t < 3:
                        dve.wait_ge(y_done, 6 * (2 * L + which) + 3 * s + t + 1)
                    else:
                        dve.wait_ge(split_free, unit_done(n_sweep[s]))
                    for c in segs(L):
                        u = slice(c * SEG, (c + 1) * SEG)
                        ins = dve.scalar_tensor_tensor(h[:, m, u], bank[m][:, u], modc(L, 3 * which + 2, m, c),
                                                       h[:, m, u], ALU.mult, ALU.add)
                    ins.then_inc(z_ready, 1)

            def centre(kind, L, src):
                li = NORMS.index((kind, L))
                dve.wait_ge(mean_done, li + 1)
                for m in range(KT):
                    dve.tensor_tensor(src(m), src(m), bank[0][:, tok(L)], ALU.subtract).then_inc(zc_ready, 1)

            def scaled(kind, L, m, z, gain):
                li = NORMS.index((kind, L))
                if m == 0:
                    dve.wait_ge(rstd_ready, li + 1)
                dve.scalar_tensor_tensor(z, z, gain, rs[:, tok(L)], ALU.mult, ALU.mult).then_inc(n_ready, 1)

            def post_norm(L, which, then=None):
                src = lambda m: h[:, m, tok(L)]
                centre(which, L, src)
                for m in range(KT):
                    scaled(which, L, m, src(m), col(f"ln_{lname(which)}_g{L}", m))
                    if then is not None and m >= 2:
                        modulate(*then, m - 2)
                if then is not None:
                    modulate(*then, KT - 2)
                    modulate(*then, KT - 1)

            def conv_mixer(L):
                j = CONV_LAYERS.index(L)
                lo, ns = (1, 1) if L == DEPTH - 1 else (0, 2)
                dve.memset(vbuf[:, :, :, 0:PAD], 0.0)
                dve.memset(vbuf[:, :, :, PAD + SEG:VW], 0.0)
                dve.memset(credit[:, 2:3], 0.0).then_inc(cpair_free[L], 2)
                with dve.Fori(0, 4) as g:
                    for p in range(2):
                        m = g * 2 + p
                        dve.wait_ge(cgate_done[L], m + 1)
                        dve.scalar_tensor_tensor(
                            vbuf[:, p, lo:2, PAD:PAD + SEG], half(bank[2 * p][:, :])[:, lo:2, :],
                            par[:, bass.ds(m + PAR[f"pw1_b{j}"][0], 1)], half(act_tmp[:, p, :])[:, lo:2, :],
                            ALU.add, ALU.mult).then_inc(cpair_free[L], 1)
                        dve.tensor_copy(dwc[:, p, :],
                                        par[:, bass.ds(m * (TAPS + 1) + PAR[f"dw{j}"][0], TAPS + 1)])
                        dve.drain()
                        acc = half(cacc[:, p, :])[:, lo:2, :]
                        for tap in range(TAPS):
                            v = vbuf[:, p, lo:2, tap:tap + SEG]
                            w = dwc[:, p, tap:tap + 1]
                            if tap == 0:
                                dve.tensor_scalar(acc, v, w, dwc[:, p, TAPS:TAPS + 1], ALU.mult, ALU.add)
                            elif tap < TAPS - 1:
                                dve.scalar_tensor_tensor(acc, v, w, acc, ALU.mult, ALU.add)
                            else:
                                dst = cz[:, bass.ds(m * N + first(L), N - first(L))]
                                dve.scalar_tensor_tensor(dst.rearrange("p (s t) -> p s t", s=ns), v, w, acc,
                                                         ALU.mult, ALU.add).then_inc(z_ready, 1)
                            dve.drain()
                z = lambda m: cz[:, m * N + first(L):(m + 1) * N]
                centre("conv", L, z)
                for m in range(KT):
                    scaled("conv", L, m, z(m), col(f"cn_g{j}", m))
                for m in range(KT):
                    dve.wait_ge(silu_ready, KT * j + m + 1)
                    dve.tensor_copy(xh[:, m, tok(L)], z(m))
                    dve.drain()
                    dve.tensor_tensor(xl[:, m, tok(L)], z(m), xh[:, m, tok(L)].bitcast(F32), ALU.subtract
                                      ).then_inc(x_ready, 1)

            def ffn(L):
                dve.memset(credit[:, 2:3], 0.0).then_inc(pair_free[L], 2)
                with dve.Fori(0, FG) as g:
                    if L + 1 < layers:
                        ada_to_sbuf(g + CHUNKS * (L + 1))
                        ada_to_mod(g + CHUNKS * (L + 1), g, L + 1)
                    for p in range(2):
                        m = g * 2 + p
                        at = bass.ds(m * (N - first(L)), N - first(L))
                        s, y = act_tmp[:, p, tok(L)], bank[2 * p + 1][:, tok(L)]
                        dve.wait_ge(gate_done[L], m + 1)
                        dve.tensor_tensor(tmp[:, p, tok(L)], s, y, ALU.mult)
                        dve.tensor_tensor(hidh[:, at], s, y, ALU.mult).then_inc(pair_free[L], 1)
                        dve.drain()
                        dve.tensor_tensor(hidl[:, at], tmp[:, p, tok(L)], hidh[:, at].bitcast(F32), ALU.subtract
                                          ).then_inc(hid_ready[L], 1)
                if L + 1 < layers:
                    ada_to_sbuf(CHUNKS * (L + 1) + FG)
                    ada_to_mod(CHUNKS * (L + 1) + FG, FG, L + 1)
                    finish_mod(L + 1)

            def ssm_conv(g, r):
                if r == 0:
                    at = PAR["sconv"][0]
                    for role, first_tile, step in ((0, 16, 1), (1, 24, 1), (2, 0, 2), (3, 1, 2)):
                        src = par[:, bass.ds(g * ((CW + 1) * step) + (at + (CW + 1) * first_tile), CW + 1)]
                        dve.tensor_copy(sconv[:, role, :], src)
                    dve.drain()
                if isinstance(g, int) and g == 0:
                    dve.wait_ge(proj_read, r + 1)
                    if r >= 2:
                        dve.wait_ge(xc_ready, r - 1)
                else:
                    dve.wait_ge(proj_read, g * 6 + r + 1)
                    dve.wait_ge(xc_ready, g * 4 + r - 1)
                acc = half(tmp[:, r % 2, :])
                for tap in range(CW):
                    v, w = xraw[:, r, :, tap:tap + SEG], sconv[:, r, tap:tap + 1]
                    if tap == 0:
                        ins = dve.tensor_scalar(acc, v, w, sconv[:, r, CW:CW + 1], ALU.mult, ALU.add)
                    else:
                        dve.drain()
                        ins = dve.scalar_tensor_tensor(acc, v, w, acc, ALU.mult, ALU.add)
                ins.then_inc(conv_done, 1)

            ORDER = ((0, 1, 2, 3), (1, 0, 3, 2))

            def ssm_group(it, gg):
                g = it * 2 + gg
                last = isinstance(it, int) and gg == 1
                heads4 = lambda a: a.rearrange("p c (r f) -> p c r f", r=HPG)

                def wide(a, n):
                    shape = list(a.shape)
                    return a.unsqueeze(len(shape)).broadcast_to(shape + [n])

                for d in range(2):
                    dve.tensor_copy(tg[:, :, d, :], tokq[:, :, :, :].rearrange("p q c h -> p (q c) h")
                                    [:, :, bass.ds(g * HPG + d * 32, HPG)])
                    ins = dve.tensor_copy(pick[0:64, d * HPG:(d + 1) * HPG, :],
                                          wide(cst[0:64, bass.ds(g * HPG + d * 32, HPG)], P))
                ins.then_inc(pick_ready, 1)
                dve.wait_ge(bt_done, g + 1)
                dve.tensor_copy(btok[:, :, :], bank[2][:, :].rearrange("p (c f) -> p c f", c=NC))
                dve.wait_ge(cb_done, g + 1)
                for d, mask in enumerate(("mask_f", "mask_b")):
                    m = cst[:, CST[mask]:CST[mask] + P].unsqueeze(1).broadcast_to([P, NC, P])
                    ins = dve.tensor_tensor(cbm[:, d, :].rearrange("p (c f) -> p c f", c=NC),
                                            bank[3][:, :].rearrange("p (c f) -> p c f", c=NC), m, ALU.mult)
                ins.then_inc(cb_read, 1)
                dve.drain()
                dve.wait_ge(xt_done, g + 1)

                def scaled_x(dst, q, d):
                    for b in range(2):
                        f = tg[:, q * NC + 2 * b:q * NC + 2 * b + 2, d, :]
                        ins = dve.tensor_tensor(heads4(dst[:, 2 * b:2 * b + 2, :]),
                                                heads4(bank[4 + b][:, :].rearrange("p (c f) -> p c f", c=2)),
                                                wide(f, HD), ALU.mult)
                    return ins

                def states(d):
                    dve.wait_ge(st_done, g * 2 + d + 1)
                    for i in range(3):
                        to, at = STATES[3 * d + i]
                        new = bank[to][:, at * 256:at * 256 + 256]
                        if i == 0:
                            ins = dve.tensor_copy(hst[:, d, 0, :], new)
                            continue
                        f = tg[:, 3 * NC + ORDER[d][i], d, :]
                        dve.drain()
                        r4 = lambda a: a.rearrange("p (r f) -> p r f", r=HPG)
                        dve.tensor_tensor(r4(hst[:, d, i, :]), r4(hst[:, d, i - 1, :]), wide(f, HD), ALU.mult)
                        dve.drain()
                        if d == 0 and i == 2:
                            dve.wait_ge(st_done, g * 2 + 2)
                        ins = dve.tensor_tensor(hst[:, d, i, :], hst[:, d, i, :], new, ALU.add)
                    ins.then_inc(st_read, 1)

                scaled_x(xw, 2, 0).then_inc(xw_ready, 1)
                scaled_x(xdt[:, 0, :, :], 1, 0)
                scaled_x(xdt[:, 1, :, :], 1, 1)
                dve.wait_ge(st_done, g * 2 + 1)
                scaled_x(xw, 2, 1).then_inc(xw_ready, 1)
                states(0)
                states(1)

                def exponent(n):
                    r, d = divmod(n, 2)
                    dve.wait_ge(r_done, g * 8 + n + 1)
                    if n >= 3:
                        dve.wait_ge(yh_done, g * 8 + n - 2)
                    for c in range(NC):
                        cols = slice(c * CH, (c + 1) * CH)
                        ins = dve.tensor_scalar(seg[:, n % 3, cols], bank[(2, 4, 5)[n % 3]][:, cols],
                                                tg[:, c, d, r:r + 1], 0.0, ALU.subtract, ALU.min)
                    ins.then_inc(seg_ready, 1)

                def weigh(n):
                    d = n % 2
                    dve.wait_ge(seg_exp, g * 8 + n + 1)
                    dve.tensor_tensor(seg[:, n % 3, :], seg[:, n % 3, :], cbm[:, d, :], ALU.mult).then_inc(m_ready, 1)
                    dve.wait_ge(e_ready, g * 8 + n + 1)
                    dve.tensor_tensor(act_tmp[:, n % 2, :], act_tmp[:, n % 2, :], xc[:, gg, 1, :], ALU.mult
                                      ).then_inc(ce_ready, 1)

                for n in range(9):
                    if n < 8:
                        exponent(n)
                    if n >= 1:
                        weigh(n - 1)
                    if not last and n == 4:
                        ssm_conv(g + 1, 0)
                    if not last and n == 6:
                        ssm_conv(g + 1, 1)
                dve.wait_ge(yh_done, g * 8 + 8)
                dve.wait_ge(proj_read, g * 6 + 6)
                for t in range(2):
                    y = yall[:, bass.ds(g * (2 * N) + t * N, N)]
                    dve.scalar_tensor_tensor(y, xc[:, gg, 2 + t, :], par[:, bass.ds(g * 2 + (PAR["sskip"][0] + t), 1)],
                                             bank[6 + t][:, :], ALU.mult, ALU.add)
                dve.drain()
                for t in range(2):
                    y = yall[:, bass.ds(g * (2 * N) + t * N, N)]
                    dve.tensor_tensor(y, y, zs[:, t, :], ALU.mult).then_inc(yg_ready, 1)
                if not last:
                    ssm_conv(g + 1, 2)
                    ssm_conv(g + 1, 3)

            def ssm_mixer():
                t = lambda i: yall[0:64, i * N:(i + 1) * N]
                x, nx, e, lg, d1, eq, w, ones, a, diag = (t(i) for i in (4, 1, 2, 3, 5, 6, 7, 8, 9, 10))
                dt = t(0)
                dve.memset(xraw[:, :, :, 0:2], 0.0)
                dve.memset(xraw[:, :, :, 2 + SEG:XW], 0.0)
                dve.memset(ones, 1.0)
                dve.wait_ge(split_free, unit_done(mix_base(SSM_LAYER)))
                dve.tensor_scalar(x, bank[1][0:64, :], col("dt_b", 0)[0:64, :], None, ALU.add).then_inc(dt_read, 1)
                dve.drain()
                dve.tensor_scalar(nx, x, -1.0, None, ALU.mult)
                dve.drain()
                dve.tensor_tensor(nx, nx, x, ALU.min).then_inc(dt_neg, 1)
                dve.wait_ge(dt_log, 1)
                dve.tensor_scalar(d1, e, 1.0, -1.0, ALU.add, ALU.add)
                dve.drain()
                dve.tensor_scalar(eq, d1, 0.0, None, ALU.is_equal)
                dve.drain()
                dve.tensor_tensor(d1, d1, eq, ALU.add)
                dve.drain()
                dve.reciprocal(d1, d1)
                dve.tensor_tensor(lg, lg, e, ALU.mult)
                dve.drain()
                dve.tensor_tensor(lg, lg, d1, ALU.mult)
                dve.tensor_tensor(eq, eq, e, ALU.mult)
                dve.drain()
                dve.tensor_tensor(lg, lg, eq, ALU.add)
                dve.drain()
                dve.scalar_tensor_tensor(dt, x, 0.0, lg, ALU.max, ALU.add)
                dve.wait_ge(a_ready, 1)
                dve.drain()
                dve.tensor_scalar(nx, dt, a[:, 0:1], -1.0, ALU.mult, ALU.mult)
                dve.drain()
                for c in range(NC):
                    cols = slice(c * CH, (c + 1) * CH)
                    dve.tensor_tensor_scan(cum[0:32, cols], ones[0:32, 0:CH], nx[0:32, cols], 0.0, ALU.mult, ALU.add)
                    ins = dve.tensor_tensor_scan(cum[32:64, cols][:, ::-1], ones[32:64, 0:CH], nx[32:64, cols][:, ::-1],
                                                 0.0, ALU.mult, ALU.add)
                dve.drain()
                dve.memset(credit[:, 2:3], 0.0).then_inc(cum_ready, 1)
                for c in range(NC):
                    for rows, end in ((slice(0, 32), (c + 1) * CH - 1), (slice(32, 64), c * CH)):
                        dve.tensor_scalar(diag[rows, c * 64:(c + 1) * 64], cst[rows, 0:64], cum[rows, end:end + 1],
                                          None, ALU.mult)
                dve.wait_ge(w_ready, 1)
                dve.tensor_tensor(w, w, dt, ALU.mult)
                dve.drain()
                dve.memset(credit[:, 2:3], 0.0).then_inc(rows_ready, 1)
                dve.wait_ge(toks_done, 1)
                dve.tensor_copy(tokq[:, 0:2, :, :], bank[2][:, :].rearrange("p (q c h) -> p q c h", q=2, c=NC))
                dve.tensor_copy(tokq[:, 2, :, :], bank[3][:, 0:256].rearrange("p (c h) -> p c h", c=NC)
                                ).then_inc(tot_ready, 1)
                dve.wait_ge(tot_ready, 2)
                for r in range(4):
                    ssm_conv(0, r)
                with dve.Fori(0, GROUPS // 2 - 1) as it:
                    ssm_group(it, 0)
                    ssm_group(it, 1)
                ssm_group(GROUPS // 2 - 1, 0)
                ssm_group(GROUPS // 2 - 1, 1)
                for g in range(GROUPS):
                    dve.wait_ge(grs_ready, g + 1)
                    for e in range(2):
                        k = 2 * g + e
                        a, b = (xh, xl) if k < KT else (x2h, x2l)
                        args = (yall[:, k * N:(k + 1) * N], col("snorm", k), rs[:, :], ALU.mult, ALU.mult)
                        dve.scalar_tensor_tensor(tmp[:, e, :], *args)
                        dve.scalar_tensor_tensor(a[:, k % KT, :], *args)
                    dve.drain()
                    for e in range(2):
                        k = 2 * g + e
                        a, b = (xh, xl) if k < KT else (x2h, x2l)
                        dve.tensor_tensor(b[:, k % KT, :], tmp[:, e, :], a[:, k % KT, :].bitcast(F32), ALU.subtract
                                          ).then_inc(x_ready, 1)
                    dve.memset(credit[:, 2:3], 0.0).then_inc(grs_used, 1)

            def attn_mixer():
                dve.wait_ge(vt_done, 1)
                for b in range(2):
                    ins = dve.tensor_copy(vtok[:, 2 * b:2 * b + 2, :], bank[6 + b][:, :].rearrange("p (c f) -> p c f", c=2))
                ins.then_inc(vt_read, 1)
                cos, sin = (cst[:, CST[n]:CST[n] + SEG].unsqueeze(1) for n in ("cos", "sin"))

                def rotary(c0, gain, src, blocks):
                    t = slice(N - blocks * SEG, N)
                    wide = lambda a: a.rearrange("p (b t) -> p b t", b=blocks)
                    c, s_ = (a.broadcast_to([P, blocks, SEG]) for a in (cos, sin))
                    for e in range(2):
                        dve.wait_ge(hrs_ready, c0 + e + 1)
                        x = src(e, 0)
                        dve.scalar_tensor_tensor(x, x, gain, rsh[:, e, :], ALU.mult, ALU.mult).then_inc(hn_ready, 1)
                    dve.drain()
                    for e in range(2):
                        dve.wait_ge(rot_done, c0 + e + 1)
                        dve.tensor_tensor(wide(rtmp[:, e, 0, t]), wide(src(e, t.start)), c, ALU.mult)
                        dve.tensor_tensor(wide(rtmp[:, e, 1, t]), wide(bank[6 + e][:, t]), s_, ALU.mult)
                    dve.drain()
                    for e in range(2):
                        dve.tensor_tensor(src(e, t.start), rtmp[:, e, 0, t], rtmp[:, e, 1, t], ALU.add
                                          ).then_inc(rope_done, 1)

                rotary(0, col("qk_g", 0), lambda e, at: kv[:, 2 + e, at:N], 1)
                with dve.Fori(0, 2) as i:
                    rotary(i * 2 + 2, col("qk_g", 2), lambda e, at: q[:, bass.ds(i * (4 * SEG) + (e * N + at), N - at)], 2)
                dve.drain()

                def next_q(it, a):
                    dve.tensor_copy(qcur[:, a, :], q[:, bass.ds(it * SEG + 4 * a * SEG, SEG)]).then_inc(q_ready, 1)

                def maximum(t, s):
                    m = asm_[:, s % 4, :]
                    dve.wait_ge(sc_done, t + 1)
                    dve.tensor_reduce(m[:, 0:1], bank[s % 4][:, :], mybir.AxisListType.X, ALU.max)
                    dve.drain()
                    dve.tensor_scalar(m[:, 1:2], m[:, 0:1], -0.125, None, ALU.mult).then_inc(mx_ready, 1)

                def probabilities(t, s):
                    m = asm_[:, s % 4, :]
                    dve.wait_ge(ex_ready, t + 1)
                    dve.reciprocal(m[:, 3:4], m[:, 2:3])
                    dve.drain()
                    dve.tensor_scalar(prob[:, s % 4, :], prob[:, s % 4, :], m[:, 3:4], None, ALU.mult
                                      ).then_inc(pr_ready, 1)

                def output(it, a):
                    dve.wait_ge(pv_done, it * 8 + 4 * a + 4)
                    k = bass.ds(it + 4 * a, 1)
                    dve.tensor_copy(tmp[:, a, SEG:N], bank[6 + a][:, 0:SEG])
                    dve.tensor_copy(xh[:, k, SEG:N], bank[6 + a][:, 0:SEG].unsqueeze(1))
                    dve.drain()
                    dve.tensor_tensor(xl[:, k, SEG:N], tmp[:, a:a + 1, SEG:N], xh[:, k, SEG:N].bitcast(F32),
                                      ALU.subtract).then_inc(x_ready, 1)

                def steps(it, last):
                    for s in range(8):
                        if s in (3, 7) and not last:
                            next_q(it + 1, s // 4)
                        if not (last and s >= 6):
                            maximum(it * 8 + s + 2, s + 2)
                        if not (last and s == 7):
                            probabilities(it * 8 + s + 1, s + 1)
                        if s == 5:
                            output(it, 0)
                    output(it, 1)

                next_q(0, 0)
                next_q(0, 1)
                maximum(0, 0)
                maximum(1, 1)
                probabilities(0, 0)
                with dve.Fori(0, 3) as it:
                    steps(it, False)
                steps(3, True)

            dve.memset(cond[:, :, :], 0.0).then_inc(cleared, 1)
            dve.memset(meanm[:, :], 1.0 / D)
            dve.drain()
            dve.wait_ge(par_landed, 48)
            with dve.Fori(0, CHUNKS) as c:
                ada_to_sbuf(c)
                ada_to_mod(c, c, 0)
            finish_mod(0)
            for k in range(KT):
                modulate(0, MIX, k)
            for L in range(layers):
                if L in CONV_LAYERS:
                    conv_mixer(L)
                    sweeps = [mix_base(L) + 19, mix_base(L) + 23]
                elif L == SSM_LAYER:
                    ssm_mixer()
                    sweeps = [mix_base(L) + 56, mix_base(L) + 64]
                else:
                    attn_mixer()
                    sweeps = [mix_base(L) + 15, mix_base(L) + 19]
                residual_sum(L, MIX, sweeps)
                post_norm(L, MIX, (L, FFN))
                ffn(L)
                n0 = ffn_base(L) + 4 * FG
                residual_sum(L, FFN, [n0 + FG - 1, n0 + 2 * FG - 1])
                post_norm(L, FFN, (L + 1, MIX) if L + 1 < layers else None)


def tiles(w):
    w = np.asarray(w)
    if w.shape[1] % P:
        w = np.concatenate([w, np.zeros((w.shape[0], P - w.shape[1] % P), w.dtype)], axis=1)
    return w.reshape(w.shape[0] // P, P, w.shape[1] // P, P).transpose(0, 2, 1, 3)


def head_order():
    heads = [8 * (j // 4) + j % 4 + 4 * e for j in range(8) for e in range(2)]
    return np.concatenate([np.arange(HD) + HD * x for x in heads])


def weight_units(i, layers=DEPTH):
    units = []

    def four(t, cols, ks):
        for k in ks:
            units.append([t[c][0][2 * k + kk, m] for kk in range(2) for c, m in enumerate(cols)])

    def groups(a, b, offset, n):
        for g in range(n):
            pick = [(a, 2 * g), (b, offset + 2 * g), (a, 2 * g + 1), (b, offset + 2 * g + 1)]
            for ku in range(4):
                units.append([t[2 * ku + kk, m] for kk in range(2) for t, m in pick])

    def sweeps(t, kn):
        for s in range(2):
            for ku in range(kn):
                units.append([t[2 * ku + kk, 4 * s + m] for kk in range(2) for m in range(4)])

    for L in range(layers):
        if L in CONV_LAYERS:
            j = CONV_LAYERS.index(L)
            t = tiles(i["conv_pw1_w"][j])
            groups(t, t, KT, 4)
            sweeps(tiles(i["conv_pw2_w"][j]), 4)
        if L == SSM_LAYER:
            t = tiles(i["ssm_in_w"][0])
            order = [48]
            for g in range(-1, GROUPS):
                order += [2 * g, 2 * g + 1] if g >= 0 else []
                order += [33 + g, 41 + g, 18 + 2 * g, 19 + 2 * g] if g + 1 < GROUPS else []
            units += [[t[k, m] for k in range(KT)] for m in order]
            sweeps(tiles(i["ssm_out_w"][0]), 8)
        if L == ATTN_LAYER:
            w = np.asarray(i["attn_qkv_w"][0])
            kv = HD * 4
            w = np.concatenate([w[:, D + kv:], w[:, D:D + kv], w[:, :D][:, head_order()]], axis=1)
            t = tiles(w)
            for g in range(3):
                for ku in range(4):
                    units.append([t[2 * ku + kk, 4 * g + m] for kk in range(2) for m in range(4)])
            sweeps(tiles(np.asarray(i["attn_out_w"][0])[head_order()]), 4)
        w1, w3 = tiles(i["ffn_w1"][L]), tiles(i["ffn_w3"][L])
        groups(w1, w3, 0, FG)
        sweeps(tiles(i["ffn_w2"][L]), FG)
    out = np.empty((len(units), P, 8, P), np.float32)
    for n, u in enumerate(units):
        for e, t in enumerate(u):
            out[n, :, e, :] = t
    return out.reshape(len(units), P, UNIT)


def small_parameters(i):
    out = np.zeros((P, NPAR), np.float32)

    def put(name, a):
        at, width = PAR[name]
        a = np.asarray(a)
        out[:a.shape[0], at:at + width] = a

    def columns(v):
        return np.asarray(v).reshape(-1, P).T

    for L in range(DEPTH):
        for w in ("mix", "ffn"):
            for s in "gb":
                put(f"ln_{w}_{s}{L}", columns(i[f"ln_{w}_{s}"][L]))
    for j in range(2):
        put(f"pw1_b{j}", columns(i["conv_pw1_b"][j]))
        dw = np.concatenate([np.asarray(i["conv_dw_w"][j]), np.asarray(i["conv_dw_b"][j])[None]])
        put(f"dw{j}", dw.reshape(TAPS + 1, KT, P).transpose(2, 1, 0).reshape(P, -1))
        put(f"cn_g{j}", columns(i["conv_norm_g"][j]))
        put(f"cn_b{j}", columns(i["conv_norm_b"][j]))
        put(f"pw2_b{j}", columns(i["conv_pw2_b"][j]))
    put("ada_b", np.repeat(np.asarray(i["ada_b"]).reshape(DEPTH * 48, P).T, 2, axis=1))
    conv = np.concatenate([np.asarray(i["ssm_conv_w"][0]), np.asarray(i["ssm_conv_b"])])
    put("sconv", conv.reshape(CW + 1, 32, P).transpose(2, 1, 0).reshape(P, -1))
    put("snorm", columns(i["ssm_norm_g"][0]))
    put("sskip", columns(np.repeat(np.asarray(i["ssm_d"][0]), HD)))
    put("dt_b", np.asarray(i["ssm_dt_bias"][0])[:, None])
    put("a_log", np.asarray(i["ssm_a_log"][0])[:, None])
    qk = [np.tile(np.asarray(i[f"attn_{n}_norm"][0]), 2)[:, None] for n in "kq"]
    put("qk_g", np.concatenate([qk[0]] * 2 + [qk[1]] * 8, axis=1))
    put("eps_ln", np.full((P, 1), LN_EPS, np.float32))
    put("eps_rms", np.full((P, 1), RMS_EPS, np.float32))
    put("one", np.ones((P, 1), np.float32))
    return out


def constants():
    c = np.zeros((P, NCST), np.float32)
    r = np.arange(P)
    c[:, 0:128] = np.eye(P)
    c[:, CST["mask_f"]:][:, :P] = r[None, :] >= r[:, None]
    c[:, CST["mask_b"]:][:, :P] = r[None, :] <= r[:, None]
    rot = np.zeros((P, P), np.float32)
    rot[r[1::2], r[0::2]] = -1.0
    rot[r[0::2], r[1::2]] = 1.0
    c[:, CST["rot"]:][:, :P] = rot
    c[:, CST["headmean"]:][:, :P] = (r[None, :] // HD == r[:, None] // HD) / np.float32(HD)
    inv = np.float32(10000.0) ** (-np.arange(0, 32, 2, dtype=np.float32) / np.float32(32))
    t = np.arange(SEG)
    ang = np.concatenate([(t // 64).astype(np.float32)[:, None] * inv, (t % 64).astype(np.float32)[:, None] * inv], 1)
    c[:, CST["cos"]:][:, :SEG] = np.cos(ang).T[(r % HD) // 2]
    c[:, CST["sin"]:][:, :SEG] = np.sin(ang).T[(r % HD) // 2]
    c[:, CST["sel"]:][:, :2] = r[:, None] % 32 == np.arange(2)[None, :]
    return c


def laid_out(i, layers=DEPTH):
    x = np.concatenate([np.asarray(i["ctx"])[0], np.asarray(i["x"])[0]])
    cond = np.stack([np.asarray(i["c_ctx"]), np.asarray(i["c"])[0]])
    adaw = np.asarray(i["ada_w"])[:layers].reshape(layers, KT, P, CHUNKS, N).transpose(0, 3, 2, 1, 4)
    return {
        "xT": np.ascontiguousarray(x.T.reshape(KT, P, N).transpose(1, 0, 2)),
        "condT": np.ascontiguousarray(cond.T.reshape(KT, P, 2).transpose(1, 0, 2)),
        "par": small_parameters(i),
        "cst": constants(),
        "adaw": np.ascontiguousarray(adaw.reshape(layers * CHUNKS, P, KT, N)),
        "wstream": weight_units(i, layers),
    }


def kernel(**inputs):
    import concourse.bacc as bacc
    from concourse.bass_utils import run_bass_kernel_spmd

    arrays = laid_out(inputs)
    nc = bacc.Bacc("TRN2", target_bir_lowering=False, num_devices=1)
    args = [nc.dram_tensor(k, a.shape, F32, kind="ExternalInput").ap() for k, a in arrays.items()]
    out = nc.dram_tensor("out", (P, KT, SEG), F32, kind="ExternalOutput").ap()
    program(nc, *args, out)
    got = run_bass_kernel_spmd(nc, [arrays], core_ids=[0]).results[0]["out"]
    return np.ascontiguousarray(got.transpose(2, 1, 0).reshape(1, SEG, D))
```

```python
from contextlib import ExitStack

import numpy as np
import concourse.bass as bass
from concourse import mybir

F32 = mybir.dt.float32
F32R = mybir.dt.float32r
ALU = mybir.AluOpType
ACT = mybir.ActivationFunctionType

P = 128
D = 1024
KT = D // P
SEG = 256
N = 2 * SEG
DEPTH = 4
MIX, FFN = 0, 1
ALPHA = (2 * DEPTH) ** 0.25
LN_EPS, RMS_EPS = 1e-5, 1e-6

TAPS = 31
PAD = (TAPS - 1) // 2
VW = SEG + 2 * PAD

FH = -(-8 * D // (3 * 256)) * 256
HT = FH // P
FG = HT // 2

GROUPS = 8
HPG = 4
HD = 64
CW = 5
XW = SEG + CW - 1
CH = 128
NC = N // CH
PE_TAPS = {0: (6, 10), 3: (11, 13)}
CONV_LAYERS, SSM_LAYER, ATTN_LAYER = (0, 3), 1, 2

UNIT = 8 * P
CHUNKS = 6 * D // N
EARLY = 2 * D // N

MIXER_UNITS = {0: 24, 1: 65, 2: 20, 3: 24}
FFN_UNITS = 4 * FG + 2 * FG


def mix_base(L):
    return sum(MIXER_UNITS[i] + FFN_UNITS for i in range(L))


def ffn_base(L):
    return mix_base(L) + MIXER_UNITS[L]



NORMS = [("conv", 0), (MIX, 0), (FFN, 0), (MIX, 1), (FFN, 1), (MIX, 2), (FFN, 2), ("conv", 3), (MIX, 3), (FFN, 3)]
OPERANDS = [((MIX, 0), 8), (("conv", 0), 8), ((FFN, 0), 8), ((MIX, 1), 8), (("ssm", 1), 16), ((FFN, 1), 8), ((MIX, 2), 8),
            (("attn", 2), 8), ((FFN, 2), 8), ((MIX, 3), 8), (("conv", 3), 8), ((FFN, 3), 8)]
X_BASE = {key: sum(n for _, n in OPERANDS[:i]) for i, (key, _) in enumerate(OPERANDS)}


def params():
    at, out = 0, {}
    for name, width in (
        [(f"ln_{w}_{s}{L}", KT) for L in range(DEPTH) for w in ("mix", "ffn") for s in "gb"]
        + [(f"{name}{j}", width) for j in range(2) for name, width in
           (("pw1_b", 2 * KT), ("dw", KT * (TAPS + 1)), ("cn_g", KT), ("cn_b", KT), ("pw2_b", KT))]
        + [("ada_b", DEPTH * 96), ("sconv", 32 * (CW + 1)), ("snorm", 16), ("sskip", 16), ("dt_b", 1), ("a_log", 1),
           ("qk_g", 10), ("eps_ln", 1), ("eps_rms", 1), ("one", 1)]
    ):
        out[name] = (at, width)
        at += width
    return out, at


PAR, NPAR = params()
CST = {"ident": 0, "mask_f": 128, "mask_b": 256, "sel": 384}
NCST = 386
ATT = {"rot": NCST, "headmean": NCST + 128, "cos": NCST + 256, "sin": NCST + 512}
NATT = 768


def program(nc, xT, condT, par_d, cst_d, adaw, wstream, out_d, layers=DEPTH):
    root = ExitStack()
    with root:
        def sb(name, shape, dt=F32, scope=root):
            return scope.enter_context(nc.sbuf_tensor(name, shape, dt))

        def sem(name):
            return root.enter_context(nc.semaphore(name))

        h = sb("h", [P, KT, N])
        xh = sb("xh", [P, KT, N], F32R)
        xl = sb("xl", [P, KT, N], F32R)
        raw = sb("raw", [P, 4, UNIT])
        wh = sb("wh", [P, 2, UNIT], F32R)
        wl = sb("wl", [P, 2, UNIT], F32R)
        par = sb("par_sb", [P, NPAR])
        cst = sb("cst_sb", [P, NCST])
        condraw = sb("condraw", [P, KT, 2])
        cond = sb("cond", [P, KT, 32])
        mod = sb("mod", [P, 2, 96])
        gbias = sb("gbias", [P, KT, 2])
        meanm = sb("meanm", [P, 2, P])
        affine = sb("affine", [P, 56])
        tmp = sb("tmp", [P, 2, N])
        act_tmp = sb("act_tmp", [P, 2, N])
        rs = sb("rs", [P, N])
        sqpart = sb("sqpart", [P, N])
        part = (tmp[:, 0, :], tmp[:, 1, :], rs[:, :], sqpart[:, :])
        adarow = rs
        credit = sb("credit", [P, 4])
        bank = [root.enter_context(nc.psum_tensor(f"bank{i}", [P, N], F32)) for i in range(8)]

        with ExitStack() as s:
            hidh = sb("hidh", [P, HT * N], F32R, s)
            hidl = sb("hidl", [P, HT * N], F32R, s)
            ada = sb("ada", [P, 2, 4, N], F32, s)
        with ExitStack() as s:
            ada_early = sb("ada_early", [P, EARLY, KT, N], F32, s)
        with ExitStack() as s:
            sb("conv_offset", [P, HT * SEG + 2 * UNIT], F32, s)
            diag = sb("diag", [P, 2, max(max(n) for n in PE_TAPS.values()), P], F32, s)
            vbuf = sb("vbuf", [P, 2, 2, VW], F32, s)
            dwc = sb("dwc", [P, 2, TAPS + 1], F32, s)
            cacc = sb("cacc", [P, 2, N], F32, s)
            cz = sb("cz", [P, KT * N], F32, s)

        with ExitStack() as s:
            yall = sb("yall", [P, 16 * N], F32, s)
            with ExitStack() as s2:
                xc = sb("xc", [P, 2, 4, N], F32, s2)
                zs = sb("zs", [P, 2, N], F32, s2)
                xraw = sb("xraw", [P, 4, 2, XW], F32, s2)
                xdt = sb("xdt", [P, 2, NC, HPG * HD], F32, s2)
                xw = sb("xw", [P, NC, HPG * HD], F32, s2)
                btok = sb("btok", [P, NC, P], F32, s2)
                cbm = sb("cbm", [P, 2, N], F32, s2)
                seg = sb("seg", [P, 3, N], F32, s2)
                hst = sb("hst", [P, 2, 3, HPG * HD], F32, s2)
                cum = sb("cum", [P, N], F32, s2)
                tokq = sb("tokq", [P, 4, NC, 64], F32, s2)
                tg = sb("tg", [P, 4 * NC, 2, HPG], F32, s2)
                pick = sb("pick", [P, 2 * HPG, P], F32, s2)
                sconv = sb("sconv_g", [P, 4, CW + 1], F32, s2)
            with ExitStack() as s2:
                x2h = sb("x2h", [P, KT, N], F32R, s2)
                x2l = sb("x2l", [P, KT, N], F32R, s2)
                gsq = sb("gsq", [P, 2, 2, N], F32, s2)
                grs = sb("grs", [P, 2, N], F32, s2)
        with ExitStack() as s:
            att = sb("att", [P, NATT], F32, s)
            kv = sb("kv", [P, 4, N], F32, s)
            q = sb("q", [P, 8 * SEG], F32, s)
            vtok = sb("vtok", [P, NC, 4 * HD], F32, s)
            qcur = sb("qcur", [P, 2, SEG], F32, s)
            rtmp = sb("rtmp", [P, 2, 2, N], F32, s)
            prob = sb("prob", [P, 4, N], F32, s)
            pT = sb("pT", [P, 2, N], F32, s)
            rsh = sb("rsh", [P, 2, N], F32, s)
            asm_ = sb("attn_small", [P, 4, 4], F32, s)

        raw_landed = [sem(f"raw_landed{i}") for i in range(4)]
        hi_ready = sem("hi_ready")
        split_ready = sem("split_ready")
        split_free = sem("split_free")
        par_landed = sem("par_landed")
        cond_landed = sem("cond_landed")
        h_landed = sem("h_landed")
        early_landed = [sem(f"early_landed{c}") for c in range(EARLY)]
        ada_landed = [sem("ada_landed0"), sem("ada_landed1")]
        ada_used = sem("ada_used")

        ada_row = sem("ada_row")
        ada_col = sem("ada_col")
        mod_ready = sem("mod_ready")
        mod_done = sem("mod_done")
        cleared = sem("cleared")
        cond_ready = sem("cond_ready")
        x_ready = sem("x_ready")
        ah_ready = sem("ah_ready")
        y_done = sem("y_done")
        z_ready = sem("z_ready")
        zsum_ready = sem("zsum_ready")
        dsum_ready = sem("dsum_ready")
        sqsum_ready = sem("sqsum_ready")
        sqsum_used = sem("sqsum_used")
        shift_done = sem("shift_done")
        d_ready = sem("d_ready")
        sq_ready = sem("sq_ready")
        sq_used = sem("sq_used")
        delta_done = sem("delta_done")
        var_ready = sem("var_ready")
        rstd_ready = sem("rstd_ready")
        u_ready = sem("u_ready")
        xf_ready = sem("xf_ready")
        h_ready = sem("h_ready")
        silu_ready = sem("silu_ready")
        pair_free = {L: sem(f"pair_free{L}") for L in range(layers)}
        pair_done = {L: sem(f"pair_done{L}") for L in range(layers)}
        gate_done = {L: sem(f"gate_done{L}") for L in range(layers)}
        hid_ready = {L: sem(f"hid_ready{L}") for L in range(layers)}
        cpair_free = {L: sem(f"cpair_free{L}") for L in CONV_LAYERS}
        diag_ready = {L: sem(f"diag_ready{L}") for L in CONV_LAYERS}
        taps_done = {L: sem(f"taps_done{L}") for L in CONV_LAYERS}
        cpair_done = {L: sem(f"cpair_done{L}") for L in CONV_LAYERS}
        cgate_done = {L: sem(f"cgate_done{L}") for L in CONV_LAYERS}
        out_landed = sem("out_landed")
        dt_read = sem("dt_read")
        dt_neg = sem("dt_neg")
        dt_log = sem("dt_log")
        a_ready = sem("a_ready")
        cum_ready = sem("cum_ready")
        w_ready = sem("w_ready")
        rows_ready = sem("rows_ready")
        toks_done = sem("toks_done")
        tot_ready = sem("tot_ready")
        proj_read = sem("proj_read")
        conv_done = sem("conv_done")
        xc_ready = sem("xc_ready")
        bt_done = sem("bt_done")
        xt_done = sem("xt_done")
        cb_done = sem("cb_done")
        cb_read = sem("cb_read")
        xw_ready = sem("xw_ready")
        st_done = sem("st_done")
        st_read = sem("st_read")
        pick_ready = sem("pick_ready")
        r_done = sem("r_done")
        seg_ready = sem("seg_ready")
        seg_exp = sem("seg_exp")
        e_ready = sem("e_ready")
        m_ready = sem("m_ready")
        ce_ready = sem("ce_ready")
        yh_done = sem("yh_done")
        yg_ready = sem("yg_ready")
        gsq_ready = sem("gsq_ready")
        gsq_used = sem("gsq_used")
        grs_ready = sem("grs_ready")
        grs_used = sem("grs_used")
        att_landed = sem("att_landed")
        qkv_free = sem("qkv_free")
        qkv_done = sem("qkv_done")
        vt_done = sem("vt_done")
        vt_read = sem("vt_read")
        hsq_ready = sem("hsq_ready")
        hms_done = sem("hms_done")
        hrs_ready = sem("hrs_ready")
        hn_ready = sem("hn_ready")
        rot_done = sem("rot_done")
        rope_done = sem("rope_done")
        q_ready = sem("q_ready")
        sc_done = sem("sc_done")
        mx_ready = sem("mx_ready")
        ex_ready = sem("ex_ready")
        pr_ready = sem("pr_ready")
        ptr_done = sem("ptr_done")
        pt_ready = sem("pt_ready")
        pv_done = sem("pv_done")

        STATES = ((6, 0), (6, 1), (7, 0), (3, 0), (3, 1), (7, 1))

        def unit_done(n):
            return 2 + n + 1

        def segs(L):
            return (0, 1) if L < ATTN_LAYER else (1,)

        def first(L):
            return segs(L)[0] * SEG

        def tok(L):
            return slice(first(L), N)

        WIDE = ffn_base(ATTN_LAYER)

        def ring(n):
            return 2 if n < WIDE else 4

        def split_slot(n):
            u = (n - WIDE) % 4
            if n < WIDE or u < 2:
                return wh[:, n % 2, :], wl[:, n % 2, :]
            at = HT * SEG + (u - 2) * UNIT
            return hidh[:, at:at + UNIT], hidl[:, at:at + UNIT]

        def col(name, k, width=1):
            at = PAR[name][0]
            return par[:, at + k:at + k + width]

        def modc(L, m, k, c):
            at = (m * KT + k) * 2 + c
            return mod[:, L % 2, at:at + 1]

        def half(a):
            return a.rearrange("p (s t) -> p s t", s=2)

        def lname(which):
            return ("mix", "ffn")[which]

        LEAD_IN = {(which, L): 0 if which == FFN and L + 1 == SSM_LAYER else 2 for which in (MIX, FFN) for L in range(DEPTH)}
        used = sum(mix_base(1) if L == 0 else MIXER_UNITS[L] + FFN_UNITS for L in range(layers))
        block = root.enter_context(nc.Block())

        @block.sync
        def _(sp):
            sp.dma_start(condraw[:, :, :], condT).then_inc(cond_landed, 16)
            for c in range(EARLY):
                sp.dma_start(ada_early[:, c, :, :], adaw[c, :, :, :]).then_inc(early_landed[c], 16)
                if c == 0:
                    sp.dma_start(cst[:, :], cst_d[:, 0:NCST]).then_inc(par_landed, 16)
                    sp.dma_start(par[:, :], par_d).then_inc(par_landed, 16)
            sp.dma_start(h[:, :, :], xT).then_inc(h_landed, 16)

            def load(n, slot, split=None):
                if split is not None:
                    sp.wait_ge(split_ready, split)
                sp.dma_start(raw[:, slot, :], wstream[n, :, :]).then_inc(raw_landed[slot], 16)

            for slot in range(4):
                load(slot, slot)
            whole = used - used % 4
            with sp.Fori(1, whole // 4) as i:
                for slot in range(4):
                    load(i * 4 + slot, slot, i * 4 + (slot - 3))
            for n in range(whole, used):
                load(n, n % 4, n - 3)
            for k in range(KT):
                sp.wait_ge(h_ready, k + 1)
                if layers == DEPTH:
                    sp.dma_start(out_d[:, k, :], h[:, k, SEG:N]).then_inc(out_landed, 16)
                else:
                    sp.dma_start(out_d[:, k, :], h[:, k, :]).then_inc(out_landed, 16)
            sp.wait_ge(out_landed, 16 * KT)

        @block.gpsimd
        def _(pool):
            pool.memset(credit[:, 0:1], 0.0).then_inc(split_free, 2)

            def low_part(base, g=0):
                hi, lo = split_slot(base)
                pool.wait_ge(hi_ready, g * 4 + base + 1)
                pool.tensor_tensor(lo, raw[:, base % 4, :], hi.bitcast(F32), ALU.subtract).then_inc(split_ready, 1)

            for a, b in ((0, min(WIDE, used)), (WIDE, used)):
                if b - a >= 8:
                    with pool.Fori(0, (b - a) // 4) as i:
                        for c in range(4):
                            low_part(a + c, i)
                    a += (b - a) // 4 * 4
                for n in range(a, b):
                    low_part(n)

        @block.scalar
        def _(act):
            def load_ada(c, slot, used_before):
                if used_before is not None:
                    act.wait_ge(ada_used, used_before)
                act.dma_start(ada[:, slot, :, :], adaw[c, :, slot * 4:slot * 4 + 4, :]).then_inc(ada_landed[slot], 16)

            def ada_row_out(c, b):
                act.wait_ge(ada_used, c * 2 + 2)
                act.activation(adarow[:, :], bank[b][:, :], ACT.Copy).then_inc(ada_row, 1)

            def high_part(base, g=0, stride=4):
                hi, _ = split_slot(base)
                n = g * stride + base
                act.wait_ge(raw_landed[base % 4], g * (4 * stride) + 16 * (base // 4 + 1))
                back = 2 if base < WIDE + 2 else 4
                act.wait_ge(split_free, n + (3 - back))
                act.activation(hi, raw[:, base % 4, :], ACT.Copy).then_inc(hi_ready, 1)

            def high_parts(a, b):
                b = min(b, used)
                for a, b in ((a, min(b, WIDE)), (max(a, WIDE), b)):
                    if b - a >= 8:
                        with act.Fori(0, (b - a) // 4) as i:
                            for c in range(4):
                                high_part(a + c, i)
                        a += (b - a) // 4 * 4
                    for n in range(a, b):
                        high_part(n)

            def first_residual():
                for k in range(KT):
                    act.wait_ge(x_ready, k + 1)
                    for c in range(2):
                        t = slice(c * SEG, (c + 1) * SEG)
                        ins = act.activation(h[:, k, t], h[:, k, t], ACT.Identity, scale=ALPHA, bias=gbias[:, k, c:c + 1])
                    ins.then_inc(ah_ready, 1)

            def squares(kind, L, src, tiles):
                li = NORMS.index((kind, L))
                for m in tiles:
                    act.wait_ge(d_ready, KT * li + m + 1)
                    if m >= 2 and kind == "conv":
                        act.wait_ge(sq_used, KT * CONV_LAYERS.index(L) + m - 1)
                    elif m >= 2:
                        act.wait_ge(sqsum_ready, 4 * (2 * L + kind) + m // 2)
                    act.activation(act_tmp[:, m % 2, tok(L)], src(m), ACT.Square).then_inc(sq_ready, 1)

            def inverse_deviation(kind, L):
                act.wait_ge(var_ready, NORMS.index((kind, L)) + 1)
                act.activation(rs[:, tok(L)], tmp[:, 1, tok(L)], ACT.Ln, bias=col("eps_ln", 0))
                act.drain()
                act.activation(rs[:, tok(L)], rs[:, tok(L)], ACT.Exp, scale=-0.5).then_inc(rstd_ready, 1)

            def post_norm(L, which, a, end):
                li = NORMS.index((which, L))
                src = lambda m: h[:, m, tok(L)]
                act.preload_act_table_set("natural_log_exp_and_others")
                if which == MIX and 0 < L < layers - 1:
                    load_ada(CHUNKS * (L + 1), 0, 2 * CHUNKS * (L + 1))
                    load_ada(CHUNKS * (L + 1), 1, None)
                early = end if end <= WIDE else end + 2
                high_parts(a, early)
                squares(which, L, src, range(4))
                high_parts(early, early + 1)
                squares(which, L, src, range(4, KT))
                inverse_deviation(which, L)
                final = which == FFN and L == layers - 1

                def next_residual(k):
                    act.wait_ge(x_ready, x0 + k + 1)
                    act.activation(h[:, k, tok(L)], h[:, k, tok(L)], ACT.Identity, scale=affine[:, 32 + k:33 + k],
                                   bias=affine[:, 40 + k:41 + k]).then_inc(ah_ready, 1)

                if final:
                    for k in range(KT):
                        act.wait_ge(u_ready, KT * li + k + 1)
                        act.activation(src(k), src(k), ACT.Identity, scale=col(f"ln_ffn_g{L}", k),
                                       bias=col(f"ln_ffn_b{L}", k)).then_inc(h_ready, 1)
                    return
                x0 = X_BASE[(FFN, L) if which == MIX else (MIX, L + 1)]
                for k in range(KT):
                    act.wait_ge(u_ready, KT * li + k + 1)
                    for c in segs(L):
                        t = slice(c * SEG, (c + 1) * SEG)
                        ins = act.activation(act_tmp[:, k % 2, t], h[:, k, t], ACT.Identity,
                                             scale=affine[:, 2 * k + c:2 * k + c + 1],
                                             bias=affine[:, 16 + 2 * k + c:17 + 2 * k + c])
                    ins.then_inc(xf_ready, 1)
                    if k >= 1:
                        next_residual(k - 1)
                    if k == 2:
                        high_parts(early + 1, end + ring(end))
                    if k in (5, 7) and LEAD_IN[which, L]:
                        high_part(end + ring(end) + (k == 7))
                next_residual(KT - 1)

            def conv_mixer(L):
                j = CONV_LAYERS.index(L)
                act.preload_act_table_set("sigmoid_and_others")

                def pair(g, skip=0, taps=PE_TAPS[L][0]):
                    for c in range(skip, 3):
                        high_part(mix_base(L) + ring(mix_base(L)) + c, g)
                    for p in range(2):
                        if p == 0:
                            act.wait_ge(cpair_done[L], g + 1)
                        else:
                            act.wait_ge(split_free, unit_done(mix_base(L) + g * 4 + 3))
                        act.wait_ge(cpair_free[L], g * 2 + p + 1)
                        act.activation(act_tmp[:, p, tok(L)], bank[2 * p + 1][:, tok(L)], ACT.Sigmoid,
                                       bias=par[:, bass.ds(g * 2 + (PAR[f"pw1_b{j}"][0] + KT + p), 1)]
                                       ).then_inc(cgate_done[L], 1)
                    high_part(mix_base(L) + ring(mix_base(L)) + 3, g)
                    for p in range(2):
                        act.wait_ge(cpair_free[L], g * 2 + p + 3)
                        for i in range(taps):
                            w = par[:, bass.ds(g * (2 * (TAPS + 1)) + (p * (TAPS + 1) + PAR[f"dw{j}"][0] + i), 1)]
                            ins = act.activation(diag[:, p, i, :], cst[:, 0:P], ACT.Copy, scale=w)
                        ins.then_inc(diag_ready[L], 1)
                    if L == 0:
                        for i in range(2):
                            ada_row_out(g * 2 + (EARLY + i), 6)
                            load_ada(g * 2 + (EARLY + i + 1), 0, g * 4 + (2 * (EARLY + i) + 1))
                            load_ada(g * 2 + (EARLY + i + 1), 1, g * 4 + (2 * (EARLY + i) + 2))

                pair(0, LEAD_IN[FFN, L - 1] if L else 0)
                with act.Fori(1, 3) as g:
                    pair(g)
                pair(3, taps=PE_TAPS[L][1])
                n = N - first(L)
                li = NORMS.index(("conv", L))
                act.preload_act_table_set("natural_log_exp_and_others")
                squares("conv", L, lambda m: cz[:, m * n:(m + 1) * n], range(KT))
                inverse_deviation("conv", L)
                act.preload_act_table_set("silu_and_others")
                for m in range(KT):
                    act.wait_ge(u_ready, KT * li + m + 1)
                    z = cz[:, m * n:(m + 1) * n]
                    act.activation(z, z, ACT.Silu, scale=col(f"cn_g{j}", m), bias=col(f"cn_b{j}", m)
                                   ).then_inc(silu_ready, 1)
                lead = mix_base(L) + 16 + ring(mix_base(L))
                if L == 0:
                    high_parts(lead, lead + 2)
                    act.wait_ge(mod_done, 1)
                    first_residual()
                    lead += 2
                post_norm(L, MIX, lead, ffn_base(L))

            def ffn(L):
                act.preload_act_table_set("silu_and_others")
                lead = ring(ffn_base(L))
                if L + 1 < layers:
                    c0 = CHUNKS * (L + 1)

                def group(g, skip=0):
                    for c in range(skip, 2):
                        high_part(ffn_base(L) + lead + c, g)
                    if L + 1 < layers:
                        load_ada(g + (c0 + 1), 0, g * 2 + (2 * c0 + 1))
                        load_ada(g + (c0 + 1), 1, g * 2 + (2 * c0 + 2))
                    high_part(ffn_base(L) + lead + 2, g)
                    for p in range(2):
                        if p == 0:
                            act.wait_ge(pair_done[L], g + 1)
                        else:
                            act.wait_ge(split_free, unit_done(ffn_base(L) + g * 4 + 3))
                        act.wait_ge(pair_free[L], g * 2 + p + 1)
                        act.activation(act_tmp[:, p, tok(L)], bank[2 * p][:, tok(L)], ACT.Silu
                                       ).then_inc(gate_done[L], 1)
                    high_part(ffn_base(L) + lead + 3, g)
                group(0, LEAD_IN[MIX, L])
                with act.Fori(1, FG) as g:
                    group(g)
                post_norm(L, FFN, ffn_base(L) + 4 * FG + lead, ffn_base(L) + FFN_UNITS)

            def ssm_project(q, role):
                n = mix_base(SSM_LAYER) + q
                act.wait_ge(split_free, unit_done(n))
                if role < 2:
                    act.activation(zs[:, role, :], bank[role][:, :], ACT.Silu).then_inc(proj_read, 1)
                else:
                    r = role - 2
                    act.activation(xraw[:, r, :, 2:2 + SEG], half(bank[r % 2][:, :]), ACT.Copy).then_inc(proj_read, 1)

            def ssm_silu(g, par, r):
                act.wait_ge(conv_done, g * 4 + r + 1)
                act.activation(xc[:, par, r, :], tmp[:, r % 2, :], ACT.Silu).then_inc(xc_ready, 1)

            def ssm_group(it, gg):
                g = it * 2 + gg
                last = isinstance(it, int) and gg == 1
                base = mix_base(SSM_LAYER) + 7 + 6 * gg

                def decay(n):
                    act.wait_ge(seg_ready, g * 8 + n + 1)
                    act.activation(seg[:, n % 3, :], seg[:, n % 3, :], ACT.Exp).then_inc(seg_exp, 1)
                    if n >= 2:
                        act.wait_ge(yh_done, g * 8 + n - 1)
                    act.activation(act_tmp[:, n % 2, :], bank[(2, 4, 5)[n % 3]][:, :], ACT.Exp).then_inc(e_ready, 1)

                def unit(role):
                    if last and role > 1:
                        return
                    r = role if last else (role - 2) % 6
                    ssm_project(it * 12 + (5 + 6 * gg + r), role)
                    high_part(base + r, it, 12)

                def silu(r):
                    if not last:
                        ssm_silu(g + 1, 1 - gg, r)

                unit(2)
                unit(3)
                decay(0)
                decay(1)
                unit(4)
                decay(2)
                silu(0)
                silu(1)
                decay(3)
                unit(5)
                decay(4)
                silu(2)
                decay(5)
                unit(0)
                silu(3)
                decay(6)
                decay(7)
                unit(1)

            def ssm_mixer():
                b = mix_base(SSM_LAYER)
                t = lambda i: yall[0:64, i * N:(i + 1) * N]
                high_part(b + 2)
                act.wait_ge(dt_neg, 1)
                act.activation(t(2), t(1), ACT.Exp)
                act.drain()
                act.activation(t(3), t(2), ACT.Ln, bias=col("one", 0)[0:64, :]).then_inc(dt_log, 1)
                act.activation(t(9)[:, 0:1], col("a_log", 0)[0:64, :], ACT.Exp).then_inc(a_ready, 1)
                def project(q):
                    ssm_project(q, q + 1)
                    high_part(b + q + 2)

                project(1)
                project(2)
                act.wait_ge(cum_ready, 1)
                for c in range(NC):
                    cols = slice(c * CH, (c + 1) * CH)
                    for rows, end in ((slice(0, 32), (c + 1) * CH - 1), (slice(32, 64), c * CH)):
                        ins = act.activation(t(7)[rows, cols], cum[rows, cols], ACT.Exp, scale=-1.0,
                                             bias=cum[rows, end:end + 1])
                ins.then_inc(w_ready, 1)
                project(3)
                ssm_silu(0, 0, 0)
                project(4)
                ssm_silu(0, 0, 1)
                ssm_silu(0, 0, 2)
                ssm_silu(0, 0, 3)
                act.preload_act_table_set("natural_log_exp_and_others")
                act.wait_ge(tot_ready, 1)
                act.activation(tokq[:, 3, :, :], bank[3][:, 256:512].rearrange("p (c h) -> p c h", c=NC), ACT.Exp
                               ).then_inc(tot_ready, 1)
                with act.Fori(0, GROUPS // 2 - 1) as it:
                    ssm_group(it, 0)
                    ssm_group(it, 1)
                ssm_group(GROUPS // 2 - 1, 0)
                ssm_group(GROUPS // 2 - 1, 1)
                act.preload_act_table_set("natural_log_exp_and_others")
                act.wait_ge(yg_ready, 2 * GROUPS)
                def squares_of(g):
                    if g >= 2:
                        act.wait_ge(gsq_used, g - 1)
                    for e in range(2):
                        act.activation(gsq[:, g % 2, e, :], yall[:, (2 * g + e) * N:(2 * g + e + 1) * N], ACT.Square
                                       ).then_inc(gsq_ready, 1)

                squares_of(0)
                for g in range(GROUPS):
                    if g + 1 < GROUPS:
                        squares_of(g + 1)
                    act.wait_ge(gsq_used, g + 1)
                    if g >= 2:
                        act.wait_ge(grs_used, g - 1)
                    act.activation(grs[:, g % 2, :], bank[4 + g % 2][:, :], ACT.Ln, scale=4.0, bias=col("eps_rms", 0))
                    act.drain()
                    act.activation(grs[:, g % 2, :], grs[:, g % 2, :], ACT.Exp, scale=-0.5).then_inc(grs_ready, 1)
                    if g:
                        high_part(b + 50 + g)
                post_norm(SSM_LAYER, MIX, b + 58, b + 65)

            def attn_mixer():
                b = mix_base(ATTN_LAYER)
                act.preload_act_table_set("natural_log_exp_and_others")
                act.dma_start(att[:, :], cst_d[:, NCST:NCST + NATT]).then_inc(att_landed, 16)

                def copy_out(g, to):
                    for t in range(4):
                        if t < 3:
                            act.wait_ge(qkv_done, g * 3 + t + 1)
                        else:
                            act.wait_ge(split_free, unit_done(b + g * 4 + 3))
                        dst, src = to(t)
                        act.activation(dst, src, ACT.Copy).then_inc(qkv_free, 1)

                def head_squares(src):
                    act.drain()
                    for e in range(2):
                        act.activation(act_tmp[:, e, :], src(e), ACT.Square).then_inc(hsq_ready, 1)

                def head_scales(c0):
                    if c0:
                        act.wait_ge(hn_ready, c0)
                    for e in range(2):
                        act.wait_ge(hms_done, c0 + e + 1)
                        act.activation(rsh[:, e, :], bank[4 + e][:, :], ACT.Ln, bias=col("eps_rms", 0))
                    act.drain()
                    for e in range(2):
                        act.activation(rsh[:, e, :], rsh[:, e, :], ACT.Exp, scale=-0.5).then_inc(hrs_ready, 1)

                high_parts(b + 2 + LEAD_IN[FFN, ATTN_LAYER - 1], b + 5)
                copy_out(0, lambda t: (kv[:, t, :], bank[t][:, :]))
                high_parts(b + 5, b + 7)
                head_squares(lambda e: kv[:, 2 + e, :])
                high_parts(b + 7, b + 8)
                head_scales(0)
                for g in (1, 2):
                    high_parts(b + 4 + 4 * g, b + 5 + 4 * g)
                    copy_out(g, lambda t: (q[:, (4 * g - 4 + t) * SEG:(4 * g - 3 + t) * SEG], bank[t][:, SEG:N]))
                    high_parts(b + 5 + 4 * g, b + 6 + 4 * g)
                    if g == 1:
                        high_parts(b + 10, b + 11)
                    head_squares(lambda e: q[:, (2 * g - 2 + e) * N:(2 * g - 1 + e) * N])
                    if g == 1:
                        high_parts(b + 11, b + 12)
                    head_scales(2 * g)

                def numerators(t, s):
                    act.wait_ge(mx_ready, t + 1)
                    act.activation(prob[:, s % 4, :], bank[s % 4][:, :], ACT.Exp, scale=0.125,
                                   bias=asm_[:, s % 4, 1:2], accum_out=asm_[:, s % 4, 2:3]).then_inc(ex_ready, 1)

                def steps(it, last):
                    for s in range(8):
                        if not (last and s == 7):
                            numerators(it * 8 + s + 1, s + 1)
                        act.wait_ge(ptr_done, it * 8 + s + 1)
                        act.activation(pT[:, s % 2, :], bank[4 + s % 2][:, :], ACT.Copy).then_inc(pt_ready, 1)

                numerators(0, 0)
                with act.Fori(0, 3) as it:
                    steps(it, False)
                steps(3, True)
                post_norm(ATTN_LAYER, MIX, b + 14, WIDE)

            act.wait_ge(cond_landed, 16)
            act.wait_ge(cleared, 1)
            act.activation(cond[:, :, 0:2], condraw[:, :, :], ACT.Silu).then_inc(cond_ready, 1)
            act.wait_ge(par_landed, 32)
            load_ada(EARLY, 0, 2 * EARLY)
            load_ada(EARLY, 1, None)
            high_parts(0, 2)
            for L in range(layers):
                if L in CONV_LAYERS:
                    conv_mixer(L)
                elif L == SSM_LAYER:
                    ssm_mixer()
                else:
                    attn_mixer()
                ffn(L)

        @block.tensor
        def _(pe):
            def four_tiles(n, like, xk, banks, cols, start, last=False, tile_done=(), before=None,
                           x_before=None):
                whi, wlo = split_slot(like)
                pe.wait_ge(split_ready, n + 1)
                step = 1 if last else 2 if before is not None else 4
                order = [(t, kk) for t0 in range(0, 4, step) for kk in range(2) for t in range(t0, t0 + step)]
                for t, kk in order:
                    if x_before is not None and t == 0 and (kk == 0 or not last):
                        pe.wait_ge(x_ready, x_before + (2 if last else kk + 1))
                    if before is not None and kk == 0:
                        before(t)
                    w = slice((kk * 4 + t) * P, (kk * 4 + t + 1) * P)
                    hi, lo = xk[kk]
                    for i, (a, b) in enumerate(((whi, hi), (wlo, hi), (whi, lo))):
                        mm = pe.matmul(banks[t][:, cols], a[:, w], b, start=start and kk == 0 and i == 0,
                                       stop=last and kk == 1 and i == 2)
                    if kk == 1 and t == 3:
                        mm.then_inc(split_free, 1)
                    elif kk == 1 and last and tile_done and tile_done[t] is not None:
                        mm.then_inc(tile_done[t], 1)

            def x_tiles(cols, ku):
                return [(xh[:, 2 * ku + kk, cols], xl[:, 2 * ku + kk, cols]) for kk in range(2)]

            def out_product(n0, L, operand):
                for s in range(2):
                    for ku in range(4):
                        n = n0 + 4 * s + ku
                        if s == 1 and ku == 3:
                            moments(L, MIX, False)
                        if operand == "attn":
                            pe.wait_ge(x_ready, X_BASE[operand, L] + KT)
                        four_tiles(n, n, x_tiles(tok(L), ku), bank[4 * s:4 * s + 4], tok(L), ku == 0, ku == 3,
                                   [y_done] * 3, x_before=X_BASE[operand, L] + 2 * ku)
                        if s == 1 and ku == 0:
                            shift(L, MIX)
                moments(L, MIX, True)

            def shift(L, which):
                pe.wait_ge(zsum_ready, 2 * L + which + 1)
                pe.matmul(bank[0][:, tok(L)], meanm[:, 1, :], part[0][:, tok(L)], start=True, stop=True
                          ).then_inc(shift_done, 1)

            def moments(L, which, late):
                i = 2 * L + which
                for j in (2, 3) if late else (0, 1):
                    if j:
                        pe.wait_ge(dsum_ready, 3 * i + j)
                        mm = pe.matmul(bank[1][:, tok(L)], meanm[:, 0, :], part[(1, 0, 1)[j - 1]][:, tok(L)],
                                       start=j == 1, stop=j == 3)
                        if j == 3:
                            mm.then_inc(delta_done, 1)
                    pe.wait_ge(sqsum_ready, 4 * i + j + 1)
                    pe.matmul(bank[2][:, tok(L)], meanm[:, 0, :], part[2 + j % 2][:, tok(L)], start=j == 0, stop=j == 3
                              ).then_inc(sqsum_used, 1)

            def conv_shift(L, src):
                for m in range(4):
                    pe.wait_ge(z_ready, 4 * CONV_LAYERS.index(L) + m + 1)
                    mm = pe.matmul(bank[0][:, tok(L)], meanm[:, 1, :], src(m), start=m == 0, stop=m == 3)
                mm.then_inc(shift_done, 1)

            def conv_moments(L, src):
                li = NORMS.index(("conv", L))
                for m in range(KT):
                    pe.wait_ge(d_ready, KT * li + m + 1)
                    mm = pe.matmul(bank[1][:, tok(L)], meanm[:, 0, :], src(m), start=m == 0, stop=m == KT - 1)
                    if m == KT - 1:
                        mm.then_inc(delta_done, 1)
                    pe.wait_ge(sq_ready, KT * li + m + 1)
                    pe.matmul(bank[2][:, tok(L)], meanm[:, 0, :], act_tmp[:, m % 2, tok(L)], start=m == 0,
                              stop=m == KT - 1).then_inc(sq_used, 1)

            def ada_rows(c, b=4, early=False):
                for s in range(2):
                    if early:
                        pe.wait_ge(early_landed[c], 16)
                    else:
                        pe.wait_ge(ada_landed[s], c * 16 + (16 - 16 * EARLY))
                    for k in range(4):
                        w = ada_early[:, c, 4 * s + k, :] if early else ada[:, s, k, :]
                        mm = pe.matmul(bank[b][32 * k:32 * k + 32, :], cond[:, 4 * s + k, :], w,
                                       start=s == 0, stop=s == 1)
                    mm.then_inc(ada_used, 1)

            def ada_columns(c, b=5, at=0):
                pe.wait_ge(ada_row, c + 1)
                for q in range(4):
                    mm = pe.matmul(bank[b][:, bass.ds(at + 2 * q, 2)], adarow[:, q * P:(q + 1) * P],
                                   cst[:, CST["sel"]:CST["sel"] + 2], start=True, stop=True)
                mm.then_inc(ada_col, 1)

            def conv_mixer(L):
                def project(g, before_unit=lambda ku: None):
                    def before(t):
                        if t % 2 == 0:
                            pe.wait_ge(cpair_free[L], g * 2 + t // 2 + 1)
                    for ku in range(4):
                        before_unit(ku)
                        four_tiles(g * 4 + (mix_base(L) + ku), mix_base(L) + ku, x_tiles(tok(L), ku), bank[0:4], tok(L),
                                   ku == 0, ku == 3, [None, cpair_done[L], None], before if ku == 0 else None,
                                   X_BASE[MIX, L] + 2 * ku)

                def taps(g, count):
                    for p in range(2):
                        pe.wait_ge(diag_ready[L], g * 2 + p + 1)
                        for i in range(count):
                            mm = pe.matmul(half(bank[4 + p][:, :])[:, segs(L)[0]:2, :], diag[:, p, i, :],
                                           vbuf[:, p, segs(L)[0]:2, i:i + SEG], start=i == 0, stop=i == count - 1)
                        mm.then_inc(taps_done[L], 1)

                def late_modulation(g, ku):
                    c = g * 2 + EARLY
                    if L == 0 and ku == 0:
                        ada_rows(c, 6)
                    if L == 0 and ku == 1:
                        ada_columns(c, 7, g * 16)
                        ada_rows(c + 1, 6)
                    if L == 0 and ku == 2:
                        ada_columns(c + 1, 7, g * 16 + 8)

                project(0)
                with pe.Fori(0, 3) as g:
                    project(g + 1, lambda ku: late_modulation(g, ku))
                    taps(g, PE_TAPS[L][0])
                for ku in range(3):
                    late_modulation(3, ku)
                pe.wait_ge(cpair_free[L], 2 + KT)
                n = N - first(L)
                z = lambda m: cz[:, m * n:(m + 1) * n]
                conv_shift(L, z)
                taps(3, PE_TAPS[L][1])
                conv_moments(L, z)
                out_product(mix_base(L) + 16, L, "conv")

            def ffn(L):
                def before(t):
                    if t % 2 == 0:
                        pe.wait_ge(pair_free[L], g * 2 + t // 2 + 1)
                if L + 1 < layers:
                    ada_rows(CHUNKS * (L + 1))
                with pe.Fori(0, FG) as g:
                    for ku in range(4):
                        four_tiles(g * 4 + (ffn_base(L) + ku), ffn_base(L) + ku, x_tiles(tok(L), ku), bank[0:4], tok(L),
                                   ku == 0, ku == 3, [None, pair_done[L], None], before if ku == 0 else None,
                                   X_BASE[FFN, L] + 2 * ku)
                    if L + 1 < layers:
                        ada_columns(g + CHUNKS * (L + 1))
                        ada_rows(g + (CHUNKS * (L + 1) + 1))
                if L + 1 < layers:
                    ada_columns(CHUNKS * (L + 1) + FG)
                n0 = ffn_base(L) + 4 * FG

                def hid(k):
                    at = bass.ds(k * (N - first(L)), N - first(L))
                    return hidh[:, at], hidl[:, at]

                pe.wait_ge(pair_free[L], 2 + HT)
                for s in range(2):
                    if s == 1 and L + 1 < layers:
                        pe.wait_ge(mod_ready, CHUNKS * (L + 2))
                    banks = bank[4 * s:4 * s + 4]

                    def unit(ku, j, start, last):
                        four_tiles(n0 + FG * s + ku, n0 + FG * s + j, [hid(ku * 2), hid(ku * 2 + 1)], banks, tok(L),
                                   start, last, [y_done] * 3)
                    pe.wait_ge(hid_ready[L], HT - 2)
                    unit(0, 0, True, False)
                    if s == 1:
                        shift(L, FFN)
                    with pe.Fori(0, (FG - 3) // 4) as i:
                        for j in range(1, 5):
                            unit(i * 4 + j, j, False, False)
                    for j in range(1 + (FG - 3) // 4 * 4, FG - 1):
                        unit(j, j, False, False)
                    if s == 1:
                        moments(L, FFN, False)
                    pe.wait_ge(hid_ready[L], HT)
                    unit(FG - 1, FG - 1, False, True)
                moments(L, FFN, True)

            def one_tile(q, slot, to, first=False):
                n = q + mix_base(SSM_LAYER)
                pe.wait_ge(split_ready, n + 1)
                for k in range(KT):
                    w = slice(k * P, (k + 1) * P)
                    if first:
                        pe.wait_ge(x_ready, X_BASE[MIX, SSM_LAYER] + k + 1)
                    for i, (a, b) in enumerate(((wh, xh), (wl, xh), (wh, xl))):
                        mm = pe.matmul(to[:, :], a[:, slot, w], b[:, k, :], start=k == 0 and i == 0,
                                       stop=k == KT - 1 and i == 2)
                mm.then_inc(split_free, 1)

            ORDER = ((0, 1, 2, 3), (1, 0, 3, 2))

            def ssm_group(it, gg):
                g = it * 2 + gg
                last = isinstance(it, int) and gg == 1
                B, C, x0 = xc[:, gg, 0, :], xc[:, gg, 1, :], xc[:, gg, 2:4, :]
                ch = lambda c: slice(c * CH, (c + 1) * CH)
                ident = cst[:, 0:P]

                def unit(role):
                    if last and role > 1:
                        return
                    r = role if last else (role - 2) % 6
                    q = it * 12 + (5 + 6 * gg + r)
                    pe.wait_ge(proj_read, it * 12 + (3 + 6 * gg + r))
                    one_tile(q, (mix_base(SSM_LAYER) + 5 + 6 * gg + r) % 2, bank[r % 2])

                def broadcast(n):
                    if n >= 3:
                        pe.wait_ge(seg_ready, g * 8 + n - 2)
                        pe.wait_ge(e_ready, g * 8 + n - 2)
                    pe.matmul(bank[(2, 4, 5)[n % 3]][:, :], pick[0:64, (n % 2) * HPG + n // 2, :], cum[0:64, :],
                              start=True, stop=True).then_inc(r_done, 1)

                def head(n):
                    r, d = divmod(n, 2)
                    pe.wait_ge(m_ready, g * 8 + n + 1)
                    pe.wait_ge(ce_ready, g * 8 + n + 1)
                    if n == 0:
                        pe.wait_ge(st_read, g * 2 + 2)
                    y = bank[6 + r // 2][64 * (r % 2):64 * (r % 2) + 64, :]
                    f = slice(r * HD, (r + 1) * HD)
                    for c in range(NC):
                        mm = pe.matmul(y[:, ch(c)], xdt[:, d, c, f], seg[:, n % 3, ch(c)], start=d == 0 and c == 0,
                                       stop=d == 1 and c == ORDER[1][0], skip_group_check=True)
                        at = ORDER[d].index(c)
                        if at:
                            mm = pe.matmul(y[:, ch(c)], hst[:, d, at - 1, f], act_tmp[:, n % 2, ch(c)], start=False,
                                           stop=d == 1, skip_group_check=True)
                    mm.then_inc(yh_done, 1)

                pe.wait_ge(xc_ready, g * 4 + 4)
                for c in range(NC):
                    mm = pe.transpose(bank[2][:, ch(c)], B[:, ch(c)], ident)
                mm.then_inc(bt_done, 1)
                for c in range(NC):
                    for t in range(2):
                        at = (c % 2) * 2 * P + t * P
                        mm = pe.transpose(bank[4 + c // 2][:, at:at + P], x0[:, t, ch(c)], ident)
                mm.then_inc(xt_done, 1)
                for c in range(NC):
                    mm = pe.matmul(bank[3][:, ch(c)], B[:, ch(c)], C[:, ch(c)], start=True, stop=True)
                mm.then_inc(cb_done, 1)
                unit(2)
                pe.wait_ge(cb_read, g + 1)
                for d in range(2):
                    if d == 1:
                        unit(3)
                    pe.wait_ge(xw_ready, g * 2 + d + 1)
                    for i in range(3):
                        to, at = STATES[3 * d + i]
                        mm = pe.matmul(bank[to][:, at * 256:at * 256 + 256], btok[:, ORDER[d][i], :],
                                       xw[:, ORDER[d][i], :], start=True, stop=True)
                    mm.then_inc(st_done, 1)
                pe.wait_ge(pick_ready, g + 1)
                broadcast(0)
                broadcast(1)
                broadcast(2)
                unit(4)
                head(0)
                broadcast(3)
                head(1)
                broadcast(4)
                unit(5)
                head(2)
                broadcast(5)
                head(3)
                broadcast(6)
                unit(0)
                head(4)
                broadcast(7)
                head(5)
                unit(1)
                head(6)
                head(7)

            def ssm_mixer():
                t = lambda i: yall[0:64, i * N:(i + 1) * N]
                for q in range(5):
                    if q == 2:
                        pe.wait_ge(dt_read, 1)
                    if q > 2:
                        pe.wait_ge(proj_read, q - 2)
                    one_tile(q, (mix_base(SSM_LAYER) + q) % 2, bank[(q + 1) % 2], q == 0)
                pe.wait_ge(rows_ready, 1)
                for q, src in enumerate((cum[0:64, :], t(0), t(7))):
                    for c in range(NC):
                        at = (q % 2) * 256 + c * 64
                        pe.transpose(bank[2 + q // 2][:, at:at + 64], src[:, c * CH:(c + 1) * CH], cst[0:64, 0:64])
                pe.matmul(bank[3][:, 256:512], t(8)[:, 0:P], t(10)[:, 0:256], start=True, stop=True
                          ).then_inc(toks_done, 1)
                pe.wait_ge(tot_ready, 2)
                with pe.Fori(0, GROUPS // 2 - 1) as it:
                    ssm_group(it, 0)
                    ssm_group(it, 1)
                ssm_group(GROUPS // 2 - 1, 0)
                ssm_group(GROUPS // 2 - 1, 1)
                n0 = mix_base(SSM_LAYER) + 49

                def x16(k):
                    a, b = (xh, xl) if k < KT else (x2h, x2l)
                    return a[:, k % KT, :], b[:, k % KT, :]

                def group_square(g):
                    pe.wait_ge(gsq_ready, 2 * g + 2)
                    if g >= 2:
                        pe.wait_ge(grs_ready, g - 1)
                    for e in range(2):
                        mm = pe.matmul(bank[4 + g % 2][:, :], meanm[:, 0, :], gsq[:, g % 2, e, :], start=e == 0, stop=e == 1)
                    mm.then_inc(gsq_used, 1)

                group_square(0)
                for s in range(2):
                    for ku in range(8):
                        if s == 0 and ku + 1 < GROUPS:
                            group_square(ku + 1)
                        if s == 1 and ku == 7:
                            moments(SSM_LAYER, MIX, False)
                        pe.wait_ge(x_ready, X_BASE["ssm", SSM_LAYER] + 2 * ku + 2)
                        n = n0 + 8 * s + ku
                        four_tiles(n, n, [x16(2 * ku), x16(2 * ku + 1)], bank[4 * s:4 * s + 4], tok(SSM_LAYER), ku == 0,
                                   ku == 7, [y_done] * 3)
                        if s == 1 and ku == 0:
                            shift(SSM_LAYER, MIX)
                moments(SSM_LAYER, MIX, True)

            def attn_mixer():
                L = ATTN_LAYER
                b = mix_base(L)

                def group(g, cols, kus=range(4)):
                    def before(t):
                        pe.wait_ge(qkv_free, g * 4 + t + 1)
                    for ku in kus:
                        four_tiles(g * 4 + (b + ku), b + ku, x_tiles(cols, ku), bank[0:4], cols, ku == 0, ku == 3,
                                   [qkv_done] * 3, before if ku == 0 else None, X_BASE[MIX, L] + 2 * ku)

                def head_means(c0):
                    for e in range(2):
                        pe.wait_ge(hsq_ready, c0 + e + 1)
                        pe.matmul(bank[4 + e][:, :], att[:, ATT["headmean"] - NCST:ATT["headmean"] - NCST + P],
                                  act_tmp[:, e, :], start=True, stop=True).then_inc(hms_done, 1)

                def rotate(c0, src, cols):
                    for e in range(2):
                        pe.wait_ge(hn_ready, c0 + e + 1)
                        pe.matmul(bank[6 + e][:, cols], att[:, ATT["rot"] - NCST:ATT["rot"] - NCST + P], src(e),
                                  start=True, stop=True).then_inc(rot_done, 1)

                group(0, slice(0, N))
                group(1, slice(SEG, N), (0, 1))
                pe.wait_ge(qkv_free, 8)
                for c in range(NC):
                    for t in range(2):
                        at = (c % 2) * 2 * P + t * P
                        mm = pe.transpose(bank[6 + c // 2][:, at:at + P], kv[:, t, c * CH:(c + 1) * CH], cst[:, 0:P])
                mm.then_inc(vt_done, 1)
                pe.wait_ge(att_landed, 16)
                head_means(0)
                group(1, slice(SEG, N), (2, 3))
                pe.wait_ge(vt_read, 1)
                rotate(0, lambda e: kv[:, 2 + e, SEG:N], slice(SEG, N))
                group(2, slice(SEG, N), (0, 1))
                head_means(2)
                group(2, slice(SEG, N), (2, 3))
                rotate(2, lambda e: q[:, e * N:(e + 1) * N], slice(0, N))
                head_means(4)
                rotate(4, lambda e: q[:, (2 + e) * N:(3 + e) * N], slice(0, N))
                pe.wait_ge(rope_done, 6)

                def scores(it, s):
                    a, e, qt = s // 4, s // 2 % 2, s % 2
                    rows = slice(64 * e, 64 * e + 64)
                    if s % 4 == 0:
                        pe.wait_ge(q_ready, it * 2 + a + 1)
                    pe.matmul(bank[s % 4][:, :], qcur[rows, a, qt * CH:(qt + 1) * CH], kv[rows, 2 + a, :],
                              start=True, stop=True).then_inc(sc_done, 1)

                def steps(it, last):
                    for s in range(9):
                        t = it * 8 + s
                        if s < 8 and not (last and s >= 5):
                            if s:
                                pe.wait_ge(ex_ready, t)
                            scores(it + (s + 3) // 8, (s + 3) % 8)
                        if s < 8:
                            pe.wait_ge(pr_ready, t + 1)
                            for c in range(NC):
                                mm = pe.transpose(bank[4 + s % 2][:, c * CH:(c + 1) * CH],
                                                  prob[:, s % 4, c * CH:(c + 1) * CH], cst[:, 0:P])
                            mm.then_inc(ptr_done, 1)
                        if s:
                            a, e, qt = (s - 1) // 4, (s - 1) // 2 % 2, (s - 1) % 2
                            v = slice((2 * a + e) * HD, (2 * a + e + 1) * HD)
                            if (s - 1) % 4 == 0:
                                pe.wait_ge(x_ready, it * 2 + (X_BASE["attn", L] + a - 1))
                            pe.wait_ge(pt_ready, t)
                            for c in range(NC):
                                mm = pe.matmul(bank[6 + a][64 * e:64 * e + 64, qt * CH:(qt + 1) * CH], vtok[:, c, v],
                                               pT[:, (s - 1) % 2, c * CH:(c + 1) * CH], start=c == 0, stop=c == NC - 1)
                            mm.then_inc(pv_done, 1)
                for s in range(3):
                    scores(0, s)
                with pe.Fori(0, 3) as it:
                    steps(it, False)
                steps(3, True)
                out_product(b + 12, L, "attn")

            pe.wait_ge(cond_ready, 1)
            pe.wait_ge(par_landed, 32)
            for c in range(EARLY):
                ada_rows(c, 4, early=True)
                ada_columns(c)
            for L in range(layers):
                if L in CONV_LAYERS:
                    conv_mixer(L)
                elif L == SSM_LAYER:
                    ssm_mixer()
                else:
                    attn_mixer()
                ffn(L)

        @block.vector
        def _(dve):
            def ada_to_sbuf(c):
                dve.wait_ge(ada_used, c * 2 + 2)
                dve.tensor_copy(adarow[:, :], bank[4][:, :]).then_inc(ada_row, 1)

            def ada_to_mod(c, chunk, L):
                dve.wait_ge(ada_col, c + 1)
                dve.tensor_tensor(mod[:, L % 2, bass.ds(chunk * 8, 8)], bank[5][:, 0:8],
                                  par[:, bass.ds(chunk * 8 + (PAR["ada_b"][0] + 96 * L), 8)], ALU.add
                                  ).then_inc(mod_ready, 1)

            def finish_mod(L, scales=(1, 4)):
                dve.drain()
                for m in scales:
                    s = mod[:, L % 2, m * 16:m * 16 + 16]
                    dve.tensor_scalar(s, s, 1.0, None, ALU.add)
                if L in CONV_LAYERS and 4 in scales:
                    gate = mod[:, L % 2, 32:48].rearrange("p (k c) -> p k c", c=2)
                    b = col(f"pw2_b{CONV_LAYERS.index(L)}", 0, KT)
                    for c in range(2):
                        dve.tensor_tensor(gbias[:, :, c], gate[:, :, c], b, ALU.mult)
                dve.drain()

            def first_operand(k):
                for c in range(2):
                    t = slice(c * SEG, (c + 1) * SEG)
                    sc, sh = modc(0, 1, k, c), modc(0, 0, k, c)
                    dve.tensor_scalar(xh[:, k, t], h[:, k, t], sc, sh, ALU.mult, ALU.add)
                    dve.tensor_scalar(tmp[:, k % 2, t], h[:, k, t], sc, sh, ALU.mult, ALU.add)
                dve.drain()
                dve.tensor_tensor(xl[:, k, :], tmp[:, k % 2, :], xh[:, k, :].bitcast(F32), ALU.subtract
                                  ).then_inc(x_ready, 1)

            def fold_affine(L, which):
                nl, m = (L, 3) if which == MIX else (L + 1, 0)
                g, b = (col(f"ln_{lname(which)}_{x}{L}", 0, KT) for x in "gb")
                two = lambda a: a.rearrange("p (k c) -> p k c", c=2)
                wide = lambda a: a.unsqueeze(2).broadcast_to([P, KT, 2])
                sc, sh = (two(mod[:, nl % 2, i * 16:i * 16 + 16]) for i in (m + 1, m))
                dve.tensor_tensor(two(affine[:, 0:16]), sc, wide(g), ALU.mult)
                dve.tensor_tensor(two(affine[:, 16:32]), sc, wide(b), ALU.mult)
                dve.tensor_scalar(affine[:, 32:40], g, ALPHA, None, ALU.mult)
                dve.tensor_scalar(affine[:, 40:48], b, ALPHA, None, ALU.mult)
                dve.drain()
                dve.tensor_tensor(two(affine[:, 16:32]), two(affine[:, 16:32]), sh, ALU.add)
                if which == FFN and nl in CONV_LAYERS:
                    dve.tensor_tensor(affine[:, 40:48], affine[:, 40:48], gbias[:, :, 1], ALU.add)

            def deviations(kind, L, src):
                li = NORMS.index((kind, L))
                t = tok(L)
                dve.wait_ge(delta_done, li + 1)
                dve.tensor_copy(tmp[:, 0, t], bank[1][:, t])
                dve.drain()
                dve.tensor_tensor(tmp[:, 1, t], tmp[:, 0, t], tmp[:, 0, t], ALU.mult)
                dve.drain()
                if kind == "conv":
                    dve.wait_ge(sq_used, KT * CONV_LAYERS.index(L) + KT)
                else:
                    dve.wait_ge(sqsum_used, 4 * (2 * L + kind) + 4)
                dve.tensor_tensor(tmp[:, 1, t], bank[2][:, t], tmp[:, 1, t], ALU.subtract).then_inc(var_ready, 1)
                for m in range(2):
                    centre(src(m), L)
                dve.drain()

            def centre(z, L):
                dve.tensor_tensor(z, z, tmp[:, 0, tok(L)], ALU.subtract)

            def normalise(kind, L, m, src):
                li = NORMS.index((kind, L))
                if m == 0:
                    dve.wait_ge(rstd_ready, li + 1)
                dve.tensor_tensor(src(m), src(m), rs[:, tok(L)], ALU.mult).then_inc(u_ready, 1)

            def post_norm(L, which, n_sweep):
                li = NORMS.index((which, L))
                src = lambda m: h[:, m, tok(L)]
                final = which == FFN and L == layers - 1
                dve.wait_ge(ah_ready, KT * (2 * L + which) + KT)

                def residual_sum(m, done=None):
                    s, t = divmod(m, 4)
                    if t < 3:
                        dve.wait_ge(y_done, 6 * (2 * L + which) + 3 * s + t + 1)
                    else:
                        dve.wait_ge(split_free, unit_done(n_sweep[s]))
                    for c in segs(L):
                        u = slice(c * SEG, (c + 1) * SEG)
                        ins = dve.scalar_tensor_tensor(h[:, m, u], bank[m][:, u], modc(L, 3 * which + 2, m, c),
                                                       h[:, m, u], ALU.mult, ALU.add)
                    if done is not None:
                        ins.then_inc(done, 1)

                p = lambda j: part[j][:, tok(L)]
                square = lambda m: act_tmp[:, m % 2, tok(L)]
                i2 = 2 * L + which

                def square_sum(j):
                    dve.wait_ge(sq_ready, KT * li + 2 * j + 2)
                    if j >= 2:
                        dve.wait_ge(sqsum_used, 4 * i2 + j - 1)
                    dve.tensor_tensor(p(2 + j % 2), square(2 * j), square(2 * j + 1), ALU.add).then_inc(sqsum_ready, 1)

                for m in range(4):
                    residual_sum(m)
                dve.drain()
                dve.tensor_tensor(p(0), src(0), src(1), ALU.add)
                dve.tensor_tensor(p(1), src(2), src(3), ALU.add)
                dve.drain()
                dve.tensor_tensor(p(0), p(0), p(1), ALU.add).then_inc(zsum_ready, 1)
                if not final:
                    fold_affine(L, which)
                dve.wait_ge(shift_done, li + 1)
                for m in range(4):
                    dve.tensor_tensor(src(m), src(m), bank[0][:, tok(L)], ALU.subtract).then_inc(d_ready, 1)
                dve.scalar_tensor_tensor(p(1), bank[0][:, tok(L)], -4.0, p(0), ALU.mult, ALU.add).then_inc(dsum_ready, 1)
                square_sum(0)
                for m in range(4, KT):
                    dve.tensor_tensor(src(m), src(m), bank[0][:, tok(L)], ALU.subtract)
                square_sum(1)
                dve.drain()
                residual_sum(4, d_ready)
                residual_sum(5, d_ready)
                dve.drain()
                dve.tensor_tensor(p(0), src(4), src(5), ALU.add).then_inc(dsum_ready, 1)
                residual_sum(6, d_ready)
                square_sum(2)
                residual_sum(7, d_ready)
                dve.drain()
                dve.tensor_tensor(p(1), src(6), src(7), ALU.add).then_inc(dsum_ready, 1)
                square_sum(3)
                deviations(which, L, src)
                if not final:
                    nxt = L + (which == FFN)
                    if which == MIX:
                        dve.memset(credit[:, 2:3], 0.0).then_inc(pair_free[nxt], 2)
                    elif nxt in CONV_LAYERS:
                        dve.memset(credit[:, 2:3], 0.0).then_inc(cpair_free[nxt], 2)
                    elif nxt == ATTN_LAYER:
                        dve.memset(credit[:, 2:3], 0.0).then_inc(qkv_free, 4)

                def low(k):
                    dve.wait_ge(xf_ready, xf_before + k + 1)
                    dve.tensor_tensor(xl[:, k, tok(L)], act_tmp[:, k % 2, tok(L)], xh[:, k, tok(L)].bitcast(F32),
                                      ALU.subtract).then_inc(x_ready, 1)

                xf_before = KT * (2 * L + which)
                for k in range(KT):
                    normalise(which, L, k, src)
                    if not final:
                        dve.drain()
                        for c in segs(L):
                            t = slice(c * SEG, (c + 1) * SEG)
                            dve.tensor_scalar(xh[:, k, t], h[:, k, t], affine[:, 2 * k + c:2 * k + c + 1],
                                              affine[:, 16 + 2 * k + c:17 + 2 * k + c], ALU.mult, ALU.add)
                    if k + 2 < KT:
                        centre(src(k + 2), L)
                    dve.drain()
                    if not final:
                        low(k)

            def conv_mixer(L):
                j = CONV_LAYERS.index(L)
                li = NORMS.index(("conv", L))
                lo = segs(L)[0]
                dve.memset(vbuf[:, :, :, 0:PAD], 0.0)
                dve.memset(vbuf[:, :, :, PAD + SEG:VW], 0.0)
                dve.memset(credit[:, 3:4], 0.0).then_inc(taps_done[L], 2)
                n = N - first(L)
                z = lambda m: cz[:, m * n:(m + 1) * n]

                def pair(g, last, counted):
                    first_tap = PE_TAPS[L][last]
                    for p in range(2):
                        m = g * 2 + p
                        dve.wait_ge(cgate_done[L], m + 1)
                        dve.wait_ge(taps_done[L], m + 1)
                        dve.scalar_tensor_tensor(
                            vbuf[:, p, lo:2, PAD:PAD + SEG], half(bank[2 * p][:, :])[:, lo:2, :],
                            par[:, bass.ds(m + PAR[f"pw1_b{j}"][0], 1)], half(act_tmp[:, p, :])[:, lo:2, :],
                            ALU.add, ALU.mult).then_inc(cpair_free[L], 1)
                        dve.tensor_copy(dwc[:, p, :],
                                        par[:, bass.ds(m * (TAPS + 1) + PAR[f"dw{j}"][0], TAPS + 1)])
                    dve.drain()
                    for tap in range(first_tap, TAPS):
                        for p in range(2):
                            acc = half(cacc[:, p, :])[:, lo:2, :]
                            v = vbuf[:, p, lo:2, tap:tap + SEG]
                            w = dwc[:, p, tap:tap + 1]
                            if tap == first_tap:
                                dve.tensor_scalar(acc, v, w, dwc[:, p, TAPS:TAPS + 1], ALU.mult, ALU.add)
                            else:
                                dve.scalar_tensor_tensor(acc, v, w, acc, ALU.mult, ALU.add)
                        dve.drain()
                        if last and tap == first_tap + 4:
                            dve.wait_ge(shift_done, li + 1)
                            for m in range(KT - 2):
                                dve.tensor_tensor(z(m), z(m), bank[0][:, tok(L)], ALU.subtract).then_inc(d_ready, 1)
                    if last:
                        for p in range(2):
                            acc = cacc[:, p, tok(L)]
                            dve.tensor_tensor(acc, acc, bank[0][:, tok(L)], ALU.subtract)
                        dve.drain()
                    for p in range(2):
                        m = g * 2 + p
                        dve.wait_ge(taps_done[L], m + 3)
                        ins = dve.tensor_tensor(cz[:, bass.ds(m * n, n)], cacc[:, p, tok(L)], bank[4 + p][:, tok(L)],
                                                ALU.add)
                        if last:
                            ins.then_inc(d_ready, 1)
                        elif counted:
                            ins.then_inc(z_ready, 1)

                with dve.Fori(0, 2) as g:
                    pair(g, False, True)
                pair(2, False, False)
                pair(3, True, False)
                deviations("conv", L, z)
                if L == 0:
                    dve.wait_ge(ada_col, CHUNKS)
                    dve.tensor_tensor(mod[:, 0, 8 * EARLY:96], bank[7][:, 0:96 - 8 * EARLY],
                                      col("ada_b", 8 * EARLY, 96 - 8 * EARLY), ALU.add).then_inc(mod_ready, CHUNKS - EARLY)
                    finish_mod(0, (4,))
                    dve.memset(credit[:, 2:3], 0.0).then_inc(mod_done, 1)
                for m in range(KT + 1):
                    if m < KT:
                        normalise("conv", L, m, z)
                    if m + 2 < KT:
                        centre(z(m + 2), L)
                    if m:
                        dve.wait_ge(silu_ready, KT * j + m)
                        dve.tensor_copy(xh[:, m - 1, tok(L)], z(m - 1))
                    dve.drain()
                    if m:
                        dve.tensor_tensor(xl[:, m - 1, tok(L)], z(m - 1), xh[:, m - 1, tok(L)].bitcast(F32), ALU.subtract
                                          ).then_inc(x_ready, 1)

            def ffn(L):
                with dve.Fori(0, FG) as g:
                    if L + 1 < layers:
                        ada_to_sbuf(g + CHUNKS * (L + 1))
                    for p in range(2):
                        m = g * 2 + p
                        at = bass.ds(m * (N - first(L)), N - first(L))
                        s, y = act_tmp[:, p, tok(L)], bank[2 * p + 1][:, tok(L)]
                        dve.wait_ge(gate_done[L], m + 1)
                        dve.tensor_tensor(tmp[:, p, tok(L)], s, y, ALU.mult)
                        dve.tensor_tensor(hidh[:, at], s, y, ALU.mult).then_inc(pair_free[L], 1)
                        dve.drain()
                        dve.tensor_tensor(hidl[:, at], tmp[:, p, tok(L)], hidh[:, at].bitcast(F32), ALU.subtract
                                          ).then_inc(hid_ready[L], 1)
                    if L + 1 < layers:
                        ada_to_mod(g + CHUNKS * (L + 1), g, L + 1)
                if L + 1 < layers:
                    ada_to_sbuf(CHUNKS * (L + 1) + FG)
                    ada_to_mod(CHUNKS * (L + 1) + FG, FG, L + 1)
                    finish_mod(L + 1)

            def ssm_conv(g, r):
                if r == 0:
                    at = PAR["sconv"][0]
                    for role, first_tile, step in ((0, 16, 1), (1, 24, 1), (2, 0, 2), (3, 1, 2)):
                        src = par[:, bass.ds(g * ((CW + 1) * step) + (at + (CW + 1) * first_tile), CW + 1)]
                        dve.tensor_copy(sconv[:, role, :], src)
                    dve.drain()
                if isinstance(g, int) and g == 0:
                    dve.wait_ge(proj_read, r + 1)
                    if r >= 2:
                        dve.wait_ge(xc_ready, r - 1)
                else:
                    dve.wait_ge(proj_read, g * 6 + (r - 1))
                    dve.wait_ge(xc_ready, g * 4 + r - 1)
                acc = half(tmp[:, r % 2, :])
                for tap in range(CW):
                    v, w = xraw[:, r, :, tap:tap + SEG], sconv[:, r, tap:tap + 1]
                    if tap == 0:
                        ins = dve.tensor_scalar(acc, v, w, sconv[:, r, CW:CW + 1], ALU.mult, ALU.add)
                    else:
                        dve.drain()
                        ins = dve.scalar_tensor_tensor(acc, v, w, acc, ALU.mult, ALU.add)
                ins.then_inc(conv_done, 1)

            ORDER = ((0, 1, 2, 3), (1, 0, 3, 2))

            def ssm_group(it, gg):
                g = it * 2 + gg
                last = isinstance(it, int) and gg == 1
                heads4 = lambda a: a.rearrange("p c (r f) -> p c r f", r=HPG)

                def wide(a, n):
                    shape = list(a.shape)
                    return a.unsqueeze(len(shape)).broadcast_to(shape + [n])

                for d in range(2):
                    dve.tensor_copy(tg[:, :, d, :], tokq[:, :, :, :].rearrange("p q c h -> p (q c) h")
                                    [:, :, bass.ds(g * HPG + d * 32, HPG)])
                    ins = dve.tensor_copy(pick[0:64, d * HPG:(d + 1) * HPG, :],
                                          wide(cst[0:64, bass.ds(g * HPG + d * 32, HPG)], P))
                ins.then_inc(pick_ready, 1)
                dve.wait_ge(bt_done, g + 1)
                dve.tensor_copy(btok[:, :, :], bank[2][:, :].rearrange("p (c f) -> p c f", c=NC))
                dve.wait_ge(cb_done, g + 1)
                for d, mask in enumerate(("mask_f", "mask_b")):
                    m = cst[:, CST[mask]:CST[mask] + P].unsqueeze(1).broadcast_to([P, NC, P])
                    ins = dve.tensor_tensor(cbm[:, d, :].rearrange("p (c f) -> p c f", c=NC),
                                            bank[3][:, :].rearrange("p (c f) -> p c f", c=NC), m, ALU.mult)
                ins.then_inc(cb_read, 1)
                dve.drain()
                dve.wait_ge(xt_done, g + 1)

                def scaled_x(dst, q, d):
                    for b in range(2):
                        f = tg[:, q * NC + 2 * b:q * NC + 2 * b + 2, d, :]
                        ins = dve.tensor_tensor(heads4(dst[:, 2 * b:2 * b + 2, :]),
                                                heads4(bank[4 + b][:, :].rearrange("p (c f) -> p c f", c=2)),
                                                wide(f, HD), ALU.mult)
                    return ins

                def states(d):
                    dve.wait_ge(st_done, g * 2 + d + 1)
                    for i in range(3):
                        to, at = STATES[3 * d + i]
                        new = bank[to][:, at * 256:at * 256 + 256]
                        if i == 0:
                            ins = dve.tensor_copy(hst[:, d, 0, :], new)
                            continue
                        f = tg[:, 3 * NC + ORDER[d][i], d, :]
                        dve.drain()
                        r4 = lambda a: a.rearrange("p (r f) -> p r f", r=HPG)
                        dve.tensor_tensor(r4(hst[:, d, i, :]), r4(hst[:, d, i - 1, :]), wide(f, HD), ALU.mult)
                        dve.drain()
                        if d == 0 and i == 2:
                            dve.wait_ge(st_done, g * 2 + 2)
                        ins = dve.tensor_tensor(hst[:, d, i, :], hst[:, d, i, :], new, ALU.add)
                    ins.then_inc(st_read, 1)

                scaled_x(xw, 2, 0).then_inc(xw_ready, 1)
                scaled_x(xdt[:, 0, :, :], 1, 0)
                scaled_x(xdt[:, 1, :, :], 1, 1)
                dve.wait_ge(st_done, g * 2 + 1)
                scaled_x(xw, 2, 1).then_inc(xw_ready, 1)
                states(0)
                states(1)

                def exponent(n):
                    r, d = divmod(n, 2)
                    dve.wait_ge(r_done, g * 8 + n + 1)
                    if n >= 3:
                        dve.wait_ge(yh_done, g * 8 + n - 2)
                    for c in range(NC):
                        cols = slice(c * CH, (c + 1) * CH)
                        ins = dve.tensor_scalar(seg[:, n % 3, cols], bank[(2, 4, 5)[n % 3]][:, cols],
                                                tg[:, c, d, r:r + 1], 0.0, ALU.subtract, ALU.min)
                    ins.then_inc(seg_ready, 1)

                def weigh(n):
                    d = n % 2
                    dve.wait_ge(seg_exp, g * 8 + n + 1)
                    dve.tensor_tensor(seg[:, n % 3, :], seg[:, n % 3, :], cbm[:, d, :], ALU.mult).then_inc(m_ready, 1)
                    dve.wait_ge(e_ready, g * 8 + n + 1)
                    dve.tensor_tensor(act_tmp[:, n % 2, :], act_tmp[:, n % 2, :], xc[:, gg, 1, :], ALU.mult
                                      ).then_inc(ce_ready, 1)

                for n in range(9):
                    if n < 8:
                        exponent(n)
                    if n >= 1:
                        weigh(n - 1)
                    if not last and n in (2, 4, 6):
                        for r in {2: (0, 1), 4: (2,), 6: (3,)}[n]:
                            ssm_conv(g + 1, r)
                dve.wait_ge(yh_done, g * 8 + 8)
                dve.wait_ge(proj_read, g * 6 + (6 if last else 10))
                for t in range(2):
                    y = yall[:, bass.ds(g * (2 * N) + t * N, N)]
                    dve.scalar_tensor_tensor(y, xc[:, gg, 2 + t, :], par[:, bass.ds(g * 2 + (PAR["sskip"][0] + t), 1)],
                                             bank[6 + t][:, :], ALU.mult, ALU.add)
                dve.drain()
                for t in range(2):
                    y = yall[:, bass.ds(g * (2 * N) + t * N, N)]
                    dve.tensor_tensor(y, y, zs[:, t, :], ALU.mult).then_inc(yg_ready, 1)

            def ssm_mixer():
                t = lambda i: yall[0:64, i * N:(i + 1) * N]
                x, nx, e, lg, d1, eq, w, ones, a, diag = (t(i) for i in (4, 1, 2, 3, 5, 6, 7, 8, 9, 10))
                dt = t(0)
                dve.memset(xraw[:, :, :, 0:2], 0.0)
                dve.memset(xraw[:, :, :, 2 + SEG:XW], 0.0)
                dve.memset(ones, 1.0)
                dve.wait_ge(split_free, unit_done(mix_base(SSM_LAYER)))
                dve.tensor_scalar(x, bank[1][0:64, :], col("dt_b", 0)[0:64, :], None, ALU.add).then_inc(dt_read, 1)
                dve.drain()
                dve.tensor_scalar(nx, x, -1.0, None, ALU.mult)
                dve.drain()
                dve.tensor_tensor(nx, nx, x, ALU.min).then_inc(dt_neg, 1)
                dve.wait_ge(dt_log, 1)
                dve.tensor_scalar(d1, e, 1.0, -1.0, ALU.add, ALU.add)
                dve.drain()
                dve.tensor_scalar(eq, d1, 0.0, None, ALU.is_equal)
                dve.drain()
                dve.tensor_tensor(d1, d1, eq, ALU.add)
                dve.drain()
                dve.reciprocal(d1, d1)
                dve.tensor_tensor(lg, lg, e, ALU.mult)
                dve.drain()
                dve.tensor_tensor(lg, lg, d1, ALU.mult)
                dve.tensor_tensor(eq, eq, e, ALU.mult)
                dve.drain()
                dve.tensor_tensor(lg, lg, eq, ALU.add)
                dve.drain()
                dve.scalar_tensor_tensor(dt, x, 0.0, lg, ALU.max, ALU.add)
                dve.wait_ge(a_ready, 1)
                dve.drain()
                dve.tensor_scalar(nx, dt, a[:, 0:1], -1.0, ALU.mult, ALU.mult)
                dve.drain()
                for c in range(NC):
                    cols = slice(c * CH, (c + 1) * CH)
                    dve.tensor_tensor_scan(cum[0:32, cols], ones[0:32, 0:CH], nx[0:32, cols], 0.0, ALU.mult, ALU.add)
                    ins = dve.tensor_tensor_scan(cum[32:64, cols][:, ::-1], ones[32:64, 0:CH], nx[32:64, cols][:, ::-1],
                                                 0.0, ALU.mult, ALU.add)
                dve.drain()
                dve.memset(credit[:, 2:3], 0.0).then_inc(cum_ready, 1)
                for c in range(NC):
                    for rows, end in ((slice(0, 32), (c + 1) * CH - 1), (slice(32, 64), c * CH)):
                        dve.tensor_scalar(diag[rows, c * 64:(c + 1) * 64], cst[rows, 0:64], cum[rows, end:end + 1],
                                          None, ALU.mult)
                ssm_conv(0, 0)
                dve.wait_ge(w_ready, 1)
                dve.tensor_tensor(w, w, dt, ALU.mult)
                dve.drain()
                dve.memset(credit[:, 2:3], 0.0).then_inc(rows_ready, 1)
                ssm_conv(0, 1)
                ssm_conv(0, 2)
                dve.wait_ge(toks_done, 1)
                dve.tensor_copy(tokq[:, 0:2, :, :], bank[2][:, :].rearrange("p (q c h) -> p q c h", q=2, c=NC))
                dve.tensor_copy(tokq[:, 2, :, :], bank[3][:, 0:256].rearrange("p (c h) -> p c h", c=NC)
                                ).then_inc(tot_ready, 1)
                ssm_conv(0, 3)
                dve.wait_ge(tot_ready, 2)
                with dve.Fori(0, GROUPS // 2 - 1) as it:
                    ssm_group(it, 0)
                    ssm_group(it, 1)
                ssm_group(GROUPS // 2 - 1, 0)
                ssm_group(GROUPS // 2 - 1, 1)
                for g in range(GROUPS):
                    dve.wait_ge(grs_ready, g + 1)
                    f32 = (tmp, act_tmp)[g % 2]
                    for e in range(2):
                        k = 2 * g + e
                        a, b = (xh, xl) if k < KT else (x2h, x2l)
                        args = (yall[:, k * N:(k + 1) * N], col("snorm", k), grs[:, g % 2, :], ALU.mult, ALU.mult)
                        dve.scalar_tensor_tensor(f32[:, e, :], *args)
                        dve.scalar_tensor_tensor(a[:, k % KT, :], *args)
                    dve.drain()
                    for e in range(2):
                        k = 2 * g + e
                        a, b = (xh, xl) if k < KT else (x2h, x2l)
                        dve.tensor_tensor(b[:, k % KT, :], f32[:, e, :], a[:, k % KT, :].bitcast(F32), ALU.subtract
                                          ).then_inc(x_ready, 1)
                    dve.memset(credit[:, 2:3], 0.0).then_inc(grs_used, 1)

            def attn_mixer():
                dve.wait_ge(att_landed, 16)
                dve.wait_ge(vt_done, 1)
                for b in range(2):
                    ins = dve.tensor_copy(vtok[:, 2 * b:2 * b + 2, :], bank[6 + b][:, :].rearrange("p (c f) -> p c f", c=2))
                ins.then_inc(vt_read, 1)
                cos, sin = (att[:, ATT[n] - NCST:ATT[n] - NCST + SEG].unsqueeze(1) for n in ("cos", "sin"))

                def rotary(c0, gain, src, blocks):
                    t = slice(N - blocks * SEG, N)
                    wide = lambda a: a.rearrange("p (b t) -> p b t", b=blocks)
                    c, s_ = (a.broadcast_to([P, blocks, SEG]) for a in (cos, sin))
                    for e in range(2):
                        dve.wait_ge(hrs_ready, c0 + e + 1)
                        x = src(e, 0)
                        dve.scalar_tensor_tensor(x, x, gain, rsh[:, e, :], ALU.mult, ALU.mult).then_inc(hn_ready, 1)
                    dve.drain()
                    for e in range(2):
                        dve.wait_ge(rot_done, c0 + e + 1)
                        dve.tensor_tensor(wide(rtmp[:, e, 0, t]), wide(src(e, t.start)), c, ALU.mult)
                        dve.tensor_tensor(wide(rtmp[:, e, 1, t]), wide(bank[6 + e][:, t]), s_, ALU.mult)
                    dve.drain()
                    for e in range(2):
                        dve.tensor_tensor(src(e, t.start), rtmp[:, e, 0, t], rtmp[:, e, 1, t], ALU.add
                                          ).then_inc(rope_done, 1)

                rotary(0, col("qk_g", 0), lambda e, at: kv[:, 2 + e, at:N], 1)
                for i in range(2):
                    rotary(i * 2 + 2, col("qk_g", 2), lambda e, at: q[:, (2 * i + e) * N + at:(2 * i + e + 1) * N], 2)
                dve.drain()

                def next_q(it, a):
                    dve.tensor_copy(qcur[:, a, :], q[:, bass.ds(it * SEG + 4 * a * SEG, SEG)]).then_inc(q_ready, 1)

                def maximum(t, s):
                    m = asm_[:, s % 4, :]
                    dve.wait_ge(sc_done, t + 1)
                    dve.tensor_reduce(m[:, 0:1], bank[s % 4][:, :], mybir.AxisListType.X, ALU.max)
                    dve.drain()
                    dve.tensor_scalar(m[:, 1:2], m[:, 0:1], -0.125, None, ALU.mult).then_inc(mx_ready, 1)

                def probabilities(t, s):
                    m = asm_[:, s % 4, :]
                    dve.wait_ge(ex_ready, t + 1)
                    dve.reciprocal(m[:, 3:4], m[:, 2:3])
                    dve.drain()
                    dve.tensor_scalar(prob[:, s % 4, :], prob[:, s % 4, :], m[:, 3:4], None, ALU.mult
                                      ).then_inc(pr_ready, 1)

                def output(it, a):
                    dve.wait_ge(pv_done, it * 8 + 4 * a + 4)
                    k = bass.ds(it + 4 * a, 1)
                    dve.tensor_copy(tmp[:, a, SEG:N], bank[6 + a][:, 0:SEG])
                    dve.tensor_copy(xh[:, k, SEG:N], bank[6 + a][:, 0:SEG].unsqueeze(1))
                    dve.drain()
                    dve.tensor_tensor(xl[:, k, SEG:N], tmp[:, a:a + 1, SEG:N], xh[:, k, SEG:N].bitcast(F32),
                                      ALU.subtract).then_inc(x_ready, 1)

                def steps(it, last):
                    for s in range(8):
                        if s in (3, 7) and not last:
                            next_q(it + 1, s // 4)
                        if not (last and s >= 6):
                            maximum(it * 8 + s + 2, s + 2)
                        if not (last and s == 7):
                            probabilities(it * 8 + s + 1, s + 1)
                        if s == 5:
                            output(it, 0)
                    output(it, 1)

                next_q(0, 0)
                next_q(0, 1)
                maximum(0, 0)
                maximum(1, 1)
                probabilities(0, 0)
                with dve.Fori(0, 3) as it:
                    steps(it, False)
                steps(3, True)

            dve.memset(cond[:, :, :], 0.0).then_inc(cleared, 1)
            dve.memset(meanm[:, 0, :], 1.0 / D)
            dve.memset(meanm[:, 1, :], 2.0 / D)
            dve.drain()
            dve.wait_ge(par_landed, 32)
            with dve.Fori(0, EARLY) as c:
                ada_to_sbuf(c)
                ada_to_mod(c, c, 0)
            finish_mod(0, (1,))
            dve.memset(credit[:, 2:3], 0.0).then_inc(cpair_free[0], 2)
            dve.wait_ge(h_landed, 16)
            for k in range(KT):
                first_operand(k)
            for L in range(layers):
                if L in CONV_LAYERS:
                    conv_mixer(L)
                    sweeps = [mix_base(L) + 19, mix_base(L) + 23]
                elif L == SSM_LAYER:
                    ssm_mixer()
                    sweeps = [mix_base(L) + 56, mix_base(L) + 64]
                else:
                    attn_mixer()
                    sweeps = [mix_base(L) + 15, mix_base(L) + 19]
                post_norm(L, MIX, sweeps)
                ffn(L)
                n0 = ffn_base(L) + 4 * FG
                post_norm(L, FFN, [n0 + FG - 1, n0 + 2 * FG - 1])


def tiles(w):
    w = np.asarray(w)
    if w.shape[1] % P:
        w = np.concatenate([w, np.zeros((w.shape[0], P - w.shape[1] % P), w.dtype)], axis=1)
    return w.reshape(w.shape[0] // P, P, w.shape[1] // P, P).transpose(0, 2, 1, 3)


def head_order():
    heads = [8 * (j // 4) + j % 4 + 4 * e for j in range(8) for e in range(2)]
    return np.concatenate([np.arange(HD) + HD * x for x in heads])


def weight_units(i, layers=DEPTH):
    units = []

    def four(t, cols, ks):
        for k in ks:
            units.append([t[c][0][2 * k + kk, m] for kk in range(2) for c, m in enumerate(cols)])

    def groups(a, b, offset, n):
        for g in range(n):
            pick = [(a, 2 * g), (b, offset + 2 * g), (a, 2 * g + 1), (b, offset + 2 * g + 1)]
            for ku in range(4):
                units.append([t[2 * ku + kk, m] for kk in range(2) for t, m in pick])

    def sweeps(t, kn):
        for s in range(2):
            for ku in range(kn):
                units.append([t[2 * ku + kk, 4 * s + m] for kk in range(2) for m in range(4)])

    for L in range(layers):
        if L in CONV_LAYERS:
            j = CONV_LAYERS.index(L)
            t = tiles(i["conv_pw1_w"][j])
            groups(t, t, KT, 4)
            sweeps(tiles(i["conv_pw2_w"][j]), 4)
        if L == SSM_LAYER:
            t = tiles(i["ssm_in_w"][0])
            order = [48]
            for g in range(-1, GROUPS):
                    order += [33 + g, 41 + g, 18 + 2 * g, 19 + 2 * g] if g + 1 < GROUPS else []
                    order += [2 * g, 2 * g + 1] if g >= 0 else []
            units += [[t[k, m] for k in range(KT)] for m in order]
            sweeps(tiles(i["ssm_out_w"][0]), 8)
        if L == ATTN_LAYER:
            w = np.asarray(i["attn_qkv_w"][0])
            kv = HD * 4
            w = np.concatenate([w[:, D + kv:], w[:, D:D + kv], w[:, :D][:, head_order()]], axis=1)
            t = tiles(w)
            for g in range(3):
                for ku in range(4):
                    units.append([t[2 * ku + kk, 4 * g + m] for kk in range(2) for m in range(4)])
            sweeps(tiles(np.asarray(i["attn_out_w"][0])[head_order()]), 4)
        w1, w3 = tiles(i["ffn_w1"][L]), tiles(i["ffn_w3"][L])
        groups(w1, w3, 0, FG)
        sweeps(tiles(i["ffn_w2"][L]), FG)
    out = np.empty((len(units), P, 8, P), np.float32)
    for n, u in enumerate(units):
        for e, t in enumerate(u):
            out[n, :, e, :] = t
    return out.reshape(len(units), P, UNIT)


def small_parameters(i):
    out = np.zeros((P, NPAR), np.float32)

    def put(name, a):
        at, width = PAR[name]
        a = np.asarray(a)
        out[:a.shape[0], at:at + width] = a

    def columns(v):
        return np.asarray(v).reshape(-1, P).T

    for L in range(DEPTH):
        for w in ("mix", "ffn"):
            for s in "gb":
                put(f"ln_{w}_{s}{L}", columns(i[f"ln_{w}_{s}"][L]))
    for j in range(2):
        put(f"pw1_b{j}", columns(i["conv_pw1_b"][j]))
        dw = np.concatenate([np.asarray(i["conv_dw_w"][j]), np.asarray(i["conv_dw_b"][j])[None]])
        put(f"dw{j}", dw.reshape(TAPS + 1, KT, P).transpose(2, 1, 0).reshape(P, -1))
        put(f"cn_g{j}", columns(i["conv_norm_g"][j]))
        put(f"cn_b{j}", columns(i["conv_norm_b"][j]))
        put(f"pw2_b{j}", columns(i["conv_pw2_b"][j]))
    put("ada_b", np.repeat(np.asarray(i["ada_b"]).reshape(DEPTH * 48, P).T, 2, axis=1))
    conv = np.concatenate([np.asarray(i["ssm_conv_w"][0]), np.asarray(i["ssm_conv_b"])])
    put("sconv", conv.reshape(CW + 1, 32, P).transpose(2, 1, 0).reshape(P, -1))
    put("snorm", columns(i["ssm_norm_g"][0]))
    put("sskip", columns(np.repeat(np.asarray(i["ssm_d"][0]), HD)))
    put("dt_b", np.asarray(i["ssm_dt_bias"][0])[:, None])
    put("a_log", np.asarray(i["ssm_a_log"][0])[:, None])
    qk = [np.tile(np.asarray(i[f"attn_{n}_norm"][0]), 2)[:, None] for n in "kq"]
    put("qk_g", np.concatenate([qk[0]] * 2 + [qk[1]] * 8, axis=1))
    put("eps_ln", np.full((P, 1), LN_EPS, np.float32))
    put("eps_rms", np.full((P, 1), RMS_EPS, np.float32))
    put("one", np.ones((P, 1), np.float32))
    return out


def constants():
    c = np.zeros((P, NCST + NATT), np.float32)
    r = np.arange(P)
    c[:, 0:128] = np.eye(P)
    c[:, CST["mask_f"]:][:, :P] = r[None, :] >= r[:, None]
    c[:, CST["mask_b"]:][:, :P] = r[None, :] <= r[:, None]
    rot = np.zeros((P, P), np.float32)
    rot[r[1::2], r[0::2]] = -1.0
    rot[r[0::2], r[1::2]] = 1.0
    c[:, ATT["rot"]:][:, :P] = rot
    c[:, ATT["headmean"]:][:, :P] = (r[None, :] // HD == r[:, None] // HD) / np.float32(HD)
    inv = np.float32(10000.0) ** (-np.arange(0, 32, 2, dtype=np.float32) / np.float32(32))
    t = np.arange(SEG)
    ang = np.concatenate([(t // 64).astype(np.float32)[:, None] * inv, (t % 64).astype(np.float32)[:, None] * inv], 1)
    c[:, ATT["cos"]:][:, :SEG] = np.cos(ang).T[(r % HD) // 2]
    c[:, ATT["sin"]:][:, :SEG] = np.sin(ang).T[(r % HD) // 2]
    c[:, CST["sel"]:][:, :2] = r[:, None] % 32 == np.arange(2)[None, :]
    return c


def laid_out(i, layers=DEPTH):
    x = np.concatenate([np.asarray(i["ctx"])[0], np.asarray(i["x"])[0]])
    cond = np.stack([np.asarray(i["c_ctx"]), np.asarray(i["c"])[0]])
    adaw = np.asarray(i["ada_w"])[:layers].reshape(layers, KT, P, CHUNKS, N).transpose(0, 3, 2, 1, 4)
    return {
        "xT": np.ascontiguousarray(x.T.reshape(KT, P, N).transpose(1, 0, 2)),
        "condT": np.ascontiguousarray(cond.T.reshape(KT, P, 2).transpose(1, 0, 2)),
        "par": small_parameters(i),
        "cst": constants(),
        "adaw": np.ascontiguousarray(adaw.reshape(layers * CHUNKS, P, KT, N)),
        "wstream": weight_units(i, layers),
    }


def kernel(**inputs):
    import concourse.bacc as bacc
    from concourse.bass_utils import run_bass_kernel_spmd

    arrays = laid_out(inputs)
    nc = bacc.Bacc("TRN2", target_bir_lowering=False, num_devices=1)
    args = [nc.dram_tensor(k, a.shape, F32, kind="ExternalInput").ap() for k, a in arrays.items()]
    out = nc.dram_tensor("out", (P, KT, SEG), F32, kind="ExternalOutput").ap()
    program(nc, *args, out)
    got = run_bass_kernel_spmd(nc, [arrays], core_ids=[0]).results[0]["out"]
    return np.ascontiguousarray(got.transpose(2, 1, 0).reshape(1, SEG, D))
```
